# Optimizing a Trainium2 kernel written in Bass

```python
import jax, jax.numpy as jnp
from jax import lax
import numpy as np
import math
import jax
import jax.numpy as jnp

D_MODEL = 1024
BATCH = 1
SEQ = 512
DEPTH = 1

N_MIXERS = 2
N_META = 16
FOX_HEADS = 16
FOX_HEAD_DIM = D_MODEL // FOX_HEADS
FOX_Q_BLOCK = 128
HGRN_EXPAND = 128
HGRN_HEADS = D_MODEL // HGRN_EXPAND
HGRN_DK = HGRN_EXPAND
HGRN_DV = D_MODEL // HGRN_HEADS
HGRN_CHUNK = 64
FFN_HIDDEN = -(-8 * D_MODEL // (3 * 256)) * 256
N_FOX = (DEPTH + N_MIXERS - 1) // N_MIXERS
N_HGRN = DEPTH // N_MIXERS
EPS = 1e-6


def rms_norm(x, gain):
    xf = x.astype(jnp.float32)
    y = xf * lax.rsqrt(jnp.mean(xf * xf, axis=-1, keepdims=True) + EPS)
    return (y * gain.astype(jnp.float32)).astype(x.dtype)

def _fox_attend(q_blk, c_q, pos_q, k, v, c_k, pos_k):
    s = jnp.einsum('bhqd,bhkd->bhqk', q_blk, k).astype(jnp.float32) * (FOX_HEAD_DIM ** -0.5)
    s = s + (c_q[..., :, None] - c_k[..., None, :])
    s = jnp.where(pos_k[None, :] <= pos_q[:, None], s, -jnp.inf)
    p = jax.nn.softmax(s, axis=-1)
    return jnp.einsum('bhqk,bhkd->bhqd', p, v.astype(jnp.float32))

def fox_mixer(h, w_in, b_f, q_gain, k_gain, w_out):
    B, L, D = h.shape
    n_blk = (L - N_META) // FOX_Q_BLOCK
    proj = h @ w_in
    q, k, v, gate, f_logit = jnp.split(proj, [D, 2 * D, 3 * D, 4 * D], axis=-1)
    q = rms_norm(q.reshape(B, L, FOX_HEADS, FOX_HEAD_DIM), q_gain)
    k = rms_norm(k.reshape(B, L, FOX_HEADS, FOX_HEAD_DIM), k_gain)
    v = v.reshape(B, L, FOX_HEADS, FOX_HEAD_DIM)
    log_f = jax.nn.log_sigmoid(f_logit.astype(jnp.float32) + b_f.astype(jnp.float32))
    c = jnp.cumsum(log_f, axis=1).transpose(0, 2, 1)
    q, k, v = (t.transpose(0, 2, 1, 3) for t in (q, k, v))
    pos = jnp.arange(L)
    o_meta = _fox_attend(q[:, :, :N_META], c[:, :, :N_META], pos[:N_META],
                         k[:, :, :N_META], v[:, :, :N_META], c[:, :, :N_META], pos[:N_META])
    qb = q[:, :, N_META:].reshape(B, FOX_HEADS, n_blk, FOX_Q_BLOCK, FOX_HEAD_DIM).transpose(2, 0, 1, 3, 4)
    cb = c[:, :, N_META:].reshape(B, FOX_HEADS, n_blk, FOX_Q_BLOCK).transpose(2, 0, 1, 3)
    pb = pos[N_META:].reshape(n_blk, FOX_Q_BLOCK)
    o_real = lax.map(lambda a: _fox_attend(a[0], a[1], a[2], k, v, c, pos), (qb, cb, pb))
    o_real = o_real.transpose(1, 2, 0, 3, 4).reshape(B, FOX_HEADS, L - N_META, FOX_HEAD_DIM)
    o = jnp.concatenate([o_meta, o_real], axis=2).transpose(0, 2, 1, 3).reshape(B, L, D)
    o = o * jax.nn.sigmoid(gate.astype(jnp.float32))
    return (o.astype(h.dtype) @ w_out).astype(h.dtype)

def _hgrn_chunk(S, inp):
    q, k, v, g = inp
    C = q.shape[2]
    b = jnp.cumsum(g, axis=2)
    causal = jnp.tril(jnp.ones((C, C), dtype=bool))
    diff = b[:, :, :, None, :] - b[:, :, None, :, :]
    decay = jnp.exp(jnp.where(causal[..., None], diff, -jnp.inf))
    attn = jnp.einsum('bhtd,bhsd,bhtsd->bhts', q, k, decay)
    o = jnp.einsum('bhts,bhsv->bhtv', attn, v) + jnp.einsum('bhtd,bhdv->bhtv', q * jnp.exp(b), S)
    b_last = b[:, :, -1:, :]
    S_new = jnp.exp(b_last[:, :, 0, :])[..., None] * S + jnp.einsum(
        'bhsd,bhsv->bhdv', k * jnp.exp(b_last - b), v)
    return S_new, o

def hgrn2_mixer(h, w_in, lb, g_gain, w_out):
    B, L, D = h.shape
    n_chunk = (L - N_META) // HGRN_CHUNK
    proj = h @ w_in
    q, f_logit, i, g_out = jnp.split(proj, 4, axis=-1)
    z = f_logit.astype(jnp.float32)
    lbf = lb.astype(jnp.float32)
    log_f = jnp.logaddexp(jnp.log(lbf), jnp.log1p(-lbf) + jax.nn.log_sigmoid(z))
    k = (1.0 - lbf) * jax.nn.sigmoid(-z)
    q = jax.nn.silu(q.astype(jnp.float32))
    v = i.astype(jnp.float32)
    heads = lambda t, d: t.reshape(B, L, HGRN_HEADS, d).transpose(0, 2, 1, 3)
    q, k, log_f, v = heads(q, HGRN_DK), heads(k, HGRN_DK), heads(log_f, HGRN_DK), heads(v, HGRN_DV)
    S0 = jnp.zeros((B, HGRN_HEADS, HGRN_DK, HGRN_DV), jnp.float32)
    S_meta, o_meta = _hgrn_chunk(S0, (q[:, :, :N_META], k[:, :, :N_META], v[:, :, :N_META], log_f[:, :, :N_META]))
    chunks = lambda t: t[:, :, N_META:].reshape(B, HGRN_HEADS, n_chunk, HGRN_CHUNK, t.shape[-1]).transpose(2, 0, 1, 3, 4)
    _, o_real = lax.scan(_hgrn_chunk, S_meta, (chunks(q), chunks(k), chunks(v), chunks(log_f)))
    o_real = o_real.transpose(1, 2, 0, 3, 4).reshape(B, HGRN_HEADS, L - N_META, HGRN_DV)
    o = jnp.concatenate([o_meta, o_real], axis=2).transpose(0, 2, 1, 3)
    o = rms_norm(o, g_gain) * jax.nn.silu(g_out.astype(jnp.float32).reshape(B, L, HGRN_HEADS, HGRN_DV))
    return (o.reshape(B, L, D).astype(h.dtype) @ w_out).astype(h.dtype)

def swiglu(h, w_in, w_out):
    gate, up = jnp.split(h @ w_in, 2, axis=-1)
    return ((jax.nn.silu(gate) * up) @ w_out).astype(h.dtype)

def first_inputs(seed: int = 0) -> dict:
    key = jax.random.key(seed)
    ks = jax.random.split(key, 18)
    D = D_MODEL
    nrm = lambda k, shape, fan: jax.random.normal(k, shape, jnp.float32) * fan ** -0.5
    gain = lambda k, shape: 1.0 + 0.02 * jax.random.normal(k, shape, jnp.float32)
    return {
        "x": jax.random.normal(ks[0], (BATCH, SEQ, D), jnp.float32),
        "meta_tokens": jax.random.normal(ks[1], (N_META, D), jnp.float32),
        "attn_norm": gain(ks[2], (DEPTH, D)),
        "ffn_norm": gain(ks[3], (DEPTH, D)),
        "final_norm": gain(ks[4], (D,)),
        "fox_w_in": nrm(ks[5], (N_FOX, D, 4 * D + FOX_HEADS), D),
        "fox_b_f": jax.random.uniform(ks[6], (N_FOX, FOX_HEADS), jnp.float32, 1.0, 4.0),
        "fox_q_norm": gain(ks[7], (N_FOX, FOX_HEAD_DIM)),
        "fox_k_norm": gain(ks[8], (N_FOX, FOX_HEAD_DIM)),
        "fox_w_out": nrm(ks[9], (N_FOX, D, D), D),
        "hgrn_w_in": nrm(ks[10], (N_HGRN, D, 4 * D), D),
        "hgrn_lower_bounds": 0.1 * jax.random.normal(ks[11], (DEPTH, D), jnp.float32),
        "hgrn_g_norm": gain(ks[12], (N_HGRN, HGRN_DV)),
        "hgrn_w_out": nrm(ks[13], (N_HGRN, D, D), D),
        "ffn_w_in": nrm(ks[14], (DEPTH, D, 2 * FFN_HIDDEN), D),
        "ffn_w_out": nrm(ks[15], (DEPTH, FFN_HIDDEN, D), FFN_HIDDEN),
    }

def first_block(x, meta_tokens, attn_norm, ffn_norm, final_norm, fox_w_in, fox_b_f, fox_q_norm,
              fox_k_norm, fox_w_out, hgrn_w_in, hgrn_lower_bounds, hgrn_g_norm, hgrn_w_out,
              ffn_w_in, ffn_w_out):
    B = x.shape[0]
    meta = jnp.broadcast_to(meta_tokens[None].astype(x.dtype), (B, N_META, D_MODEL))
    h = jnp.concatenate([meta, x], axis=1)
    lb_soft = jax.nn.softmax(hgrn_lower_bounds.astype(jnp.float32), axis=0)
    lower_bounds = jnp.cumsum(lb_soft, axis=0) - lb_soft[0]
    for i in range(DEPTH):
        hn = rms_norm(h, attn_norm[i])
        j = i // N_MIXERS
        if i % N_MIXERS == 0:
            h = h + fox_mixer(hn, fox_w_in[j], fox_b_f[j], fox_q_norm[j], fox_k_norm[j], fox_w_out[j])
        else:
            h = h + hgrn2_mixer(hn, hgrn_w_in[j], lower_bounds[i], hgrn_g_norm[j], hgrn_w_out[j])
        h = h + swiglu(rms_norm(h, ffn_norm[i]), ffn_w_in[i], ffn_w_out[i])
    h = rms_norm(h, final_norm)
    return h[:, N_META:]


CHUNK = 64
D_CONV = D_MODEL
CONV_K = 31
SSM_EXPAND = 2
D_INNER = SSM_EXPAND * D_MODEL
SSM_HEADDIM = 64
SSM_HEADS = D_INNER // SSM_HEADDIM
SSM_GROUPS = 4
SSM_HPG = SSM_HEADS // SSM_GROUPS
SSM_STATE = 128
SSM_CONV_K = 4
N_BRANCHES = 2
IN_GLU = 2 * D_CONV
IN_Z = D_INNER
IN_XBC = D_INNER + 2 * SSM_GROUPS * SSM_STATE
IN_DT = SSM_HEADS
IN_GATE = N_BRANCHES * D_MODEL
D_IN_PROJ = IN_GLU + IN_Z + IN_XBC + IN_DT + IN_GATE
MOE_GROUPS = 8
MOE_EXPERTS_PER_GROUP = 8
N_EXPERTS = MOE_GROUPS * MOE_EXPERTS_PER_GROUP
MOE_TOP_K = 2
D_FF_EXPERT = D_MODEL // 2
MOE_BLOCK = 128


def _rmsnorm(x, g):
    xf = x.astype(jnp.float32)
    y = xf * lax.rsqrt(jnp.mean(xf * xf, axis=-1, keepdims=True) + EPS)
    return (y * g.astype(jnp.float32)).astype(x.dtype)

def _layernorm(x, g, b):
    xf = x.astype(jnp.float32)
    mu = jnp.mean(xf, axis=-1, keepdims=True)
    var = jnp.mean(jnp.square(xf - mu), axis=-1, keepdims=True)
    y = (xf - mu) * lax.rsqrt(var + EPS)
    return (y * g.astype(jnp.float32) + b.astype(jnp.float32)).astype(x.dtype)

def _causal_dwconv(x, w, b):
    k = w.shape[0]
    xp = jnp.pad(x, ((0, 0), (k - 1, 0), (0, 0)))
    y = lax.conv_general_dilated(xp, w[:, None, :].astype(x.dtype), (1,), 'VALID',
                                 dimension_numbers=('NWC', 'WIO', 'NWC'),
                                 feature_group_count=x.shape[-1])
    return y + b.astype(x.dtype)

def _ssd(xh, dt, a, bm, cm):
    bsz, seq = xh.shape[0], xh.shape[1]
    nc = seq // CHUNK
    x = (xh * dt[..., None]).reshape(bsz, nc, CHUNK, SSM_GROUPS, SSM_HPG, SSM_HEADDIM)
    ad = (dt * a).reshape(bsz, nc, CHUNK, SSM_GROUPS, SSM_HPG)
    bc = bm.reshape(bsz, nc, CHUNK, SSM_GROUPS, SSM_STATE)
    cc = cm.reshape(bsz, nc, CHUNK, SSM_GROUPS, SSM_STATE)
    a_cs = jnp.cumsum(ad, axis=2)
    causal = jnp.tril(jnp.ones((CHUNK, CHUNK), dtype=bool))[:, :, None, None]
    seg = a_cs[:, :, :, None] - a_cs[:, :, None, :]
    lmat = jnp.exp(jnp.where(causal, seg, -jnp.inf))
    cb = jnp.einsum('bclgn,bcsgn->bclsg', cc, bc)
    y_diag = jnp.einsum('bclsgr,bcsgrp->bclgrp', cb[..., None] * lmat, x)
    decay = jnp.exp(a_cs[:, :, -1:] - a_cs)
    states = jnp.einsum('bclgn,bclgrp->bcgrpn', bc, x * decay[..., None])
    chunk_decay = jnp.exp(a_cs[:, :, -1])

    def step(carry, inp):
        st, dec = inp
        return carry * dec[..., None, None] + st, carry

    init = jnp.zeros((bsz, SSM_GROUPS, SSM_HPG, SSM_HEADDIM, SSM_STATE), jnp.float32)
    _, prev = lax.scan(step, init, (jnp.moveaxis(states, 1, 0), jnp.moveaxis(chunk_decay, 1, 0)))
    prev = jnp.moveaxis(prev, 0, 1)
    y_off = jnp.einsum('bclgn,bcgrpn->bclgrp', cc, prev) * jnp.exp(a_cs)[..., None]
    return (y_diag + y_off).reshape(bsz, seq, SSM_HEADS, SSM_HEADDIM)

def _mixer(n, w_in, cv_dw_w, cv_dw_b, cv_ln_g, cv_ln_b, w_cv_out, ssm_conv_w, ssm_conv_b,
           dt_bias, a_log, d_skip, ssm_norm_g, w_ssm_out, w_mix_out):
    bsz, seq, _ = n.shape
    f32 = jnp.float32
    cuts = [IN_GLU, IN_GLU + IN_Z, IN_GLU + IN_Z + IN_XBC, IN_GLU + IN_Z + IN_XBC + IN_DT]
    glu_in, z, xbc, dt_raw, gate_in = jnp.split(n @ w_in, cuts, axis=-1)
    u_a, u_b = jnp.split(glu_in, 2, axis=-1)
    u = u_a * jax.nn.sigmoid(u_b)
    u = jax.nn.silu(_layernorm(_causal_dwconv(u, cv_dw_w, cv_dw_b), cv_ln_g, cv_ln_b))
    y_cv = u @ w_cv_out
    xbc = jax.nn.silu(_causal_dwconv(xbc, ssm_conv_w, ssm_conv_b))
    xs, bm, cm = jnp.split(xbc, [D_INNER, D_INNER + SSM_GROUPS * SSM_STATE], axis=-1)
    dt = jax.nn.softplus(dt_raw.astype(f32) + dt_bias.astype(f32))
    a = -jnp.exp(a_log.astype(f32))
    xh = xs.reshape(bsz, seq, SSM_HEADS, SSM_HEADDIM).astype(f32)
    y = _ssd(xh, dt, a,
             bm.reshape(bsz, seq, SSM_GROUPS, SSM_STATE).astype(f32),
             cm.reshape(bsz, seq, SSM_GROUPS, SSM_STATE).astype(f32))
    y = y + d_skip.astype(f32)[:, None] * xh
    y = y.reshape(bsz, seq, D_INNER).astype(n.dtype) * jax.nn.silu(z)
    gs = D_INNER // SSM_GROUPS
    y = _rmsnorm(y.reshape(bsz, seq, SSM_GROUPS, gs), ssm_norm_g.reshape(SSM_GROUPS, gs))
    y_ssm = y.reshape(bsz, seq, D_INNER) @ w_ssm_out
    g_cv, g_ssm = jnp.split(jax.nn.sigmoid(gate_in), 2, axis=-1)
    return (g_cv * y_cv + g_ssm * y_ssm) @ w_mix_out

def _hier_moe(xt, w_grp, b_grp, w_er, b_er, w1, w3, w2):
    t, d = xt.shape
    f32 = jnp.float32
    gp = jax.nn.softmax((xt @ w_grp + b_grp).astype(f32), axis=-1)
    g_p, g_idx = lax.top_k(gp, 1)
    el = (xt @ w_er + b_er).astype(f32).reshape(t, MOE_GROUPS, MOE_EXPERTS_PER_GROUP)
    idx = jnp.broadcast_to(g_idx[:, :, None], (t, 1, MOE_EXPERTS_PER_GROUP))
    el_sel = jnp.take_along_axis(el, idx, axis=1)[:, 0]
    ep = jax.nn.softmax(el_sel, axis=-1)
    e_p, e_loc = lax.top_k(ep, MOE_TOP_K)
    e_p = e_p / jnp.sum(e_p, axis=-1, keepdims=True)
    weights = g_p * e_p
    e_glob = g_idx * MOE_EXPERTS_PER_GROUP + e_loc
    n_asg = t * MOE_TOP_K
    e_flat = e_glob.reshape(-1)
    tok_flat = jnp.repeat(jnp.arange(t, dtype=jnp.int32), MOE_TOP_K)
    w_flat = weights.reshape(-1)
    order = jnp.argsort(e_flat)
    e_sorted = e_flat[order]
    counts = jnp.bincount(e_flat, length=N_EXPERTS)
    starts = jnp.cumsum(counts) - counts
    pcounts = (counts + MOE_BLOCK - 1) // MOE_BLOCK * MOE_BLOCK
    pends = jnp.cumsum(pcounts)
    pstarts = pends - pcounts
    dest = pstarts[e_sorted] + (jnp.arange(n_asg) - starts[e_sorted])
    n_blocks = -(-n_asg // MOE_BLOCK) + N_EXPERTS
    n_rows = n_blocks * MOE_BLOCK
    buf_tok = jnp.zeros((n_rows,), jnp.int32).at[dest].set(tok_flat[order])
    buf_w = jnp.zeros((n_rows,), xt.dtype).at[dest].set(w_flat[order].astype(xt.dtype))
    blk_e = jnp.minimum(jnp.searchsorted(pends, jnp.arange(n_blocks) * MOE_BLOCK, side='right'),
                        N_EXPERTS - 1)
    xb = xt[buf_tok].reshape(n_blocks, MOE_BLOCK, d)

    def expert_block(args):
        xblk, e = args
        hdn = jax.nn.silu(xblk @ w1[e]) * (xblk @ w3[e])
        return hdn @ w2[e]

    yb = lax.map(expert_block, (xb, blk_e)).reshape(n_rows, d)
    return jnp.zeros_like(xt).at[buf_tok].add(yb * buf_w[:, None])

def second_inputs(seed: int = 0) -> dict:
    key = jax.random.key(seed)
    ks = jax.random.split(key, 30)
    f = jnp.float32
    L = DEPTH

    def nrm(k, shape, scale):
        return jax.random.normal(k, shape, f) * scale

    dt0 = jnp.exp(jax.random.uniform(ks[14], (L, SSM_HEADS), f, math.log(1e-3), math.log(1e-1)))
    return {
        'x': nrm(ks[0], (BATCH, SEQ, D_MODEL), 1.0),
        'c': nrm(ks[1], (BATCH, D_MODEL), 1.0),
        'w_ada': nrm(ks[2], (L, D_MODEL, 6 * D_MODEL), 0.5 * D_MODEL ** -0.5),
        'b_ada': nrm(ks[3], (L, 6 * D_MODEL), 0.02),
        'norm1_g': 1.0 + nrm(ks[4], (L, D_MODEL), 0.02),
        'w_in': nrm(ks[5], (L, D_MODEL, D_IN_PROJ), D_MODEL ** -0.5),
        'cv_dw_w': nrm(ks[6], (L, CONV_K, D_CONV), CONV_K ** -0.5),
        'cv_dw_b': nrm(ks[7], (L, D_CONV), 0.02),
        'cv_ln_g': 1.0 + nrm(ks[8], (L, D_CONV), 0.02),
        'cv_ln_b': nrm(ks[9], (L, D_CONV), 0.02),
        'w_cv_out': nrm(ks[10], (L, D_CONV, D_MODEL), D_CONV ** -0.5),
        'ssm_conv_w': nrm(ks[11], (L, SSM_CONV_K, IN_XBC), SSM_CONV_K ** -0.5),
        'ssm_conv_b': nrm(ks[12], (L, IN_XBC), 0.02),
        'dt_bias': dt0 + jnp.log(-jnp.expm1(-dt0)),
        'a_log': jnp.log(jax.random.uniform(ks[15], (L, SSM_HEADS), f, 1.0, 16.0)),
        'd_skip': 1.0 + nrm(ks[16], (L, SSM_HEADS), 0.1),
        'ssm_norm_g': 1.0 + nrm(ks[17], (L, D_INNER), 0.02),
        'w_ssm_out': nrm(ks[18], (L, D_INNER, D_MODEL), D_INNER ** -0.5),
        'w_mix_out': nrm(ks[19], (L, D_MODEL, D_MODEL), D_MODEL ** -0.5),
        'norm2_g': 1.0 + nrm(ks[20], (L, D_MODEL), 0.02),
        'w_grp': nrm(ks[21], (L, D_MODEL, MOE_GROUPS), D_MODEL ** -0.5),
        'b_grp': nrm(ks[22], (L, MOE_GROUPS), 0.01),
        'w_er': nrm(ks[23], (L, D_MODEL, N_EXPERTS), D_MODEL ** -0.5),
        'b_er': nrm(ks[24], (L, N_EXPERTS), 0.01),
        'w1': nrm(ks[25], (L, N_EXPERTS, D_MODEL, D_FF_EXPERT), D_MODEL ** -0.5),
        'w3': nrm(ks[26], (L, N_EXPERTS, D_MODEL, D_FF_EXPERT), D_MODEL ** -0.5),
        'w2': nrm(ks[27], (L, N_EXPERTS, D_FF_EXPERT, D_MODEL), D_FF_EXPERT ** -0.5),
        'final_g': 1.0 + nrm(ks[28], (D_MODEL,), 0.02),
    }

def second_block(x, c, w_ada, b_ada, norm1_g, w_in, cv_dw_w, cv_dw_b, cv_ln_g, cv_ln_b, w_cv_out,
              ssm_conv_w, ssm_conv_b, dt_bias, a_log, d_skip, ssm_norm_g, w_ssm_out, w_mix_out,
              norm2_g, w_grp, b_grp, w_er, b_er, w1, w3, w2, final_g):
    bsz, seq, d = x.shape
    h = x
    for i in range(DEPTH):
        mod = jax.nn.silu(c) @ w_ada[i] + b_ada[i]
        sh1, sc1, g1, sh2, sc2, g2 = jnp.split(mod[:, None, :], 6, axis=-1)
        n1 = _rmsnorm(h, norm1_g[i]) * (1.0 + sc1) + sh1
        h = h + g1 * _mixer(n1, w_in[i], cv_dw_w[i], cv_dw_b[i], cv_ln_g[i], cv_ln_b[i], w_cv_out[i],
                            ssm_conv_w[i], ssm_conv_b[i], dt_bias[i], a_log[i], d_skip[i],
                            ssm_norm_g[i], w_ssm_out[i], w_mix_out[i])
        n2 = _rmsnorm(h, norm2_g[i]) * (1.0 + sc2) + sh2
        moe = _hier_moe(n2.reshape(bsz * seq, d), w_grp[i], b_grp[i], w_er[i], b_er[i],
                        w1[i], w3[i], w2[i])
        h = h + g2 * moe.reshape(bsz, seq, d)
    return _rmsnorm(h, final_g)


def setup_inputs(seed=0):
    out = dict(first_inputs(seed))
    for name, value in second_inputs(seed + 1).items():
        if name != "x":
            out[name + "_2"] = value
    return out


def reference(
    x, meta_tokens, attn_norm, ffn_norm, final_norm, fox_w_in, fox_b_f, fox_q_norm, fox_k_norm,
    fox_w_out, hgrn_w_in, hgrn_lower_bounds, hgrn_g_norm, hgrn_w_out, ffn_w_in, ffn_w_out, c_2,
    w_ada_2, b_ada_2, norm1_g_2, w_in_2, cv_dw_w_2, cv_dw_b_2, cv_ln_g_2, cv_ln_b_2, w_cv_out_2,
    ssm_conv_w_2, ssm_conv_b_2, dt_bias_2, a_log_2, d_skip_2, ssm_norm_g_2, w_ssm_out_2,
    w_mix_out_2, norm2_g_2, w_grp_2, b_grp_2, w_er_2, b_er_2, w1_2, w3_2, w2_2, final_g_2,
):
    x = first_block(
        x, meta_tokens, attn_norm, ffn_norm, final_norm, fox_w_in, fox_b_f, fox_q_norm,
        fox_k_norm, fox_w_out, hgrn_w_in, hgrn_lower_bounds, hgrn_g_norm, hgrn_w_out, ffn_w_in,
        ffn_w_out,
    )
    return second_block(
        x, c_2, w_ada_2, b_ada_2, norm1_g_2, w_in_2, cv_dw_w_2, cv_dw_b_2, cv_ln_g_2, cv_ln_b_2,
        w_cv_out_2, ssm_conv_w_2, ssm_conv_b_2, dt_bias_2, a_log_2, d_skip_2, ssm_norm_g_2,
        w_ssm_out_2, w_mix_out_2, norm2_g_2, w_grp_2, b_grp_2, w_er_2, b_er_2, w1_2, w3_2, w2_2,
        final_g_2,
    )


_drawn_inputs = setup_inputs


def setup_inputs(seed=0):
    import zlib

    import numpy as np

    out = dict(_drawn_inputs(seed))
    spreads = {}
    factors = {'attn_norm': 6.557,
     'ffn_norm': 3.544,
     'fox_q_norm': 8.0,
     'fox_k_norm': 8.0,
     'b_ada_2': 2.958,
     'norm1_g_2': 7.913,
     'cv_dw_b_2': 8.0,
     'cv_ln_g_2': 8.0,
     'cv_ln_b_2': 8.0,
     'ssm_conv_b_2': 8.0,
     'd_skip_2': 168.803,
     'ssm_norm_g_2': 8.0,
     'norm2_g_2': 6.317,
     'b_grp_2': 8.0,
     'b_er_2': 8.0,
     'final_g_2': 23.86}
    for name, (base, spread) in spreads.items():
        noise = np.random.default_rng([zlib.crc32(name.encode()), seed]).standard_normal(out[name].shape)
        drawn = base * np.exp(spread * noise) if base else spread * noise
        out[name] = jnp.asarray(drawn.astype(out[name].dtype))
    for name, factor in factors.items():
        out[name] = (out[name] * factor).astype(out[name].dtype)
    return out
```

```python
from collections import deque
from contextlib import ExitStack

import numpy as np
import concourse.bass as bass
from concourse import mybir

F32 = mybir.dt.float32
U32 = mybir.dt.uint32
I32 = mybir.dt.int32
ALU = mybir.AluOpType
ACT = mybir.ActivationFunctionType
AX = mybir.AxisListType.X

T = 512
NM = 16
L = T + NM
D = 1024
FH = 2816
EPS = 1e-6
NE = 64
BLK = 64
MAIN = NE * BLK
OVER = 16
ROWS = MAIN + OVER * BLK
WC = 4096

CONST_COLS = [("ident", 128), ("ones", 128), ("bones", 128), ("ustrict", 128), ("cmask", 128), ("smask", 128),
              ("iota8", 8), ("iota64", 64), ("tok", 4), ("eps", 1), ("sel4", 1)]
PARAM_COLS = [("attn_norm", 8), ("ffn_norm", 8), ("final_norm", 8), ("qg", 1), ("kg", 1), ("bf", 1), ("norm1", 8),
              ("cvw", 248), ("cvb", 8), ("lng", 8), ("lnb", 8), ("scw", 96), ("scb", 24), ("dtb", 1), ("alog", 1),
              ("dsk", 16), ("sng", 16), ("norm2", 8), ("c", 8), ("bada", 48), ("rb", 72), ("wf", 128), ("wdt", 256)]


def offsets(cols):
    out, at = {}, 0
    for name, n in cols:
        out[name] = (at, n)
        at += n
    return out, at


CO, CN = offsets(CONST_COLS)
PO, PN = offsets(PARAM_COLS)


class Queue:

    def __init__(self, engine, sem):
        self.engine, self.sem, self.count, self.seen = engine, sem, 0, {}

    def wait(self, *toks):
        for tok in toks:
            if tok is None:
                continue
            if isinstance(tok, list):
                self.wait(*tok)
                continue
            sem, value = tok
            if self.seen.get(id(sem), 0) < value:
                self.seen[id(sem)] = value
                if self.engine is not None:
                    self.engine.wait_ge(sem, value)

    def __call__(self, fn, *toks, inc=True):
        self.wait(*toks)
        self.count += inc
        if self.engine is not None:
            ins = fn(self.engine)
            if inc:
                ins.then_inc(self.sem, 1)
        return (self.sem, self.count)

    def raw(self, fn):
        if self.engine is not None:
            fn(self.engine)

    def dma(self, counter, fn, *toks):
        self.wait(*toks)
        counter[1] += 16
        if self.engine is not None:
            fn(self.engine).then_inc(counter[0], 16)
        return (counter[0], counter[1])


def build_program(nc, a, stop=None):
    with ExitStack() as ctx:
        made = {}

        def tensor(name, shape, dt=F32):
            if name not in made:
                made[name] = ctx.enter_context(nc.sbuf_tensor(name, shape, dt))
            return made[name]

        def semaphore(name):
            if name not in made:
                made[name] = ctx.enter_context(nc.semaphore(name))
            return made[name]

        PS = ctx.enter_context(nc.psum_tensor("ps", [128, 8, 512], F32))
        program(a, tensor, semaphore, PS, {}, stop)
        block = ctx.enter_context(nc.Block())

        @block.sync
        def _(e):
            program(a, tensor, semaphore, PS, {"sp": e}, stop)

        @block.tensor
        def _(e):
            program(a, tensor, semaphore, PS, {"pe": e}, stop)

        @block.scalar
        def _(e):
            program(a, tensor, semaphore, PS, {"act": e}, stop)

        @block.vector
        def _(e):
            program(a, tensor, semaphore, PS, {"dve": e}, stop)

        @block.gpsimd
        def _(e):
            program(a, tensor, semaphore, PS, {"pool": e}, stop)


def program(a, sb, sem_of, PS, engines, stop):
    pe, act, dve, pool, sp = (Queue(engines.get(n), sem_of(f"s_{n}")) for n in ("pe", "act", "dve", "pool", "sp"))
    counters = {}

    def dsem(name):
        if name not in counters:
            counters[name] = [sem_of("d_" + name), 0]
        return counters[name]

    A = sb("arena", [128, 32768])
    RG = sb("ring", [128, 4 * WC])
    CS = sb("consts_sb", [128, CN])
    PR = sb("params_sb", [128, PN])
    SCR = sb("scr", [128, 1640])
    PSF = PS[:, :, :].rearrange("p a b -> p (a b)")

    def C(name, r0=0, r1=128):
        at, n = CO[name]
        return CS[r0:r1, at:at + n]

    def P(name, r0=0, r1=128):
        at, n = PO[name]
        return PR[r0:r1, at:at + n]

    def pc(name, k, r0=0, r1=128):
        at, n = PO[name]
        return PR[r0:r1, at + k:at + k + 1]

    def view(off, *dims):
        n = int(np.prod(dims))
        v = A[:, off:off + n]
        if len(dims) == 2:
            v = v.rearrange("p (a b) -> p a b", a=dims[0])
        if len(dims) == 3:
            v = v.rearrange("p (a b c) -> p a b c", a=dims[0], b=dims[1])
        return v

    ident, ones, bones = C("ident"), C("ones"), C("bones")

    class Slot:
        def __init__(self, ap, name):
            self.ap, self.free, self.counter = ap, [], dsem(name)

    ring = deque(Slot(RG[:, i * WC:(i + 1) * WC], f"w{i}") for i in range(4))

    def fetch(*parts):
        slot = ring.popleft()
        ring.append(slot)
        tok = None
        for off, shape, src in parts:
            n = int(np.prod(shape))
            dst = slot.ap[:, off:off + n].rearrange("p (a b) -> p a b", a=shape[0])
            tok = sp.dma(slot.counter, lambda e, dst=dst, src=src: e.dma_start(dst, src), slot.free)
        slot.free = []
        return slot, tok

    def wrows(w, r0, nk, c0, nc_):
        return w[r0:r0 + nk * 128, c0:c0 + nc_].rearrange("(k p) n -> p k n", p=128)

    def fetch_w(w, c0, ncol=512, r0=0, nk=8):
        slot, tok = fetch((0, (nk, ncol), wrows(w, r0, nk, c0, ncol)))
        return slot, tok, slot.ap[:, :nk * ncol].rearrange("p (k n) -> p k n", k=nk)

    bank_free = [[] for _ in range(8)]
    turn = [0]

    def bank(n=1, among=None):
        if among is None:
            b = turn[0] % 8
            turn[0] += 1
        else:
            b = among[turn[0] % len(among)]
            turn[0] += 1
        return b

    def mms(out, pairs, *toks, start=True, stop=True, inc=True):
        tok = None
        for i, (lt, r) in enumerate(pairs):
            last = i == len(pairs) - 1
            tok = pe(lambda e, lt=lt, r=r, s=(start and i == 0), t=(stop and last): e.matmul(out, lt, r, start=s, stop=t),
                     *(toks if i == 0 else ()), inc=inc and last)
        return tok

    t_const = act.dma(dsem("const"), lambda e: e.dma_start(CS[:, :], a["consts"]))
    t_param = act.dma(dsem("param"), lambda e: e.dma_start(PR[:, :], a["params"]))

    hT = view(0, 8, L)
    hn = view(4224, 8, L)
    kT = view(8448, 8, L)
    v = view(12672, 5, D)
    qT = view(17792, 8, T)
    gT = view(21888, 8, T)
    oT = view(25984, 8, T)
    t_x = act.dma(dsem("x"), lambda e: e.dma_start(hT, a["xT"]))

    ZERO = view(25984, 1, D)[:, 0, :]
    t_zero = pool(lambda e: e.memset(ZERO, 0.0))
    for i in range(OVER * BLK // 128):
        t_zy = pool.dma(dsem("zy"), lambda e, i=i: e.dma_start(a["y_d"][MAIN + 128 * i:MAIN + 128 * i + 128, :], ZERO), t_zero)
    t_zl = pool.dma(dsem("zl"), lambda e: e.dma_start(a["list_d"].rearrange("(p n) o -> p (n o)", p=128), ZERO[:, 0:ROWS // 128].bitcast(U32)), t_zero)

    TMP = [SCR[:, 0:528], SCR[:, 528:1056]]
    RST = SCR[:, 1056:1584]
    tmp_free = [[], []]
    tmp_turn = [0]

    def take_tmp():
        i = tmp_turn[0] % 2
        tmp_turn[0] += 1
        return i, TMP[i], tmp_free[i]

    rst_free = []

    def colsum(src, nk, segs, mat, tok_of, square=True):
        banks = [bank() for _ in segs]
        tok = None
        for k in range(nk):
            if square:
                i, tmp, free = take_tmp()
                n = segs[-1][0] + segs[-1][1]
                s = src(k)
                t_sq = act(lambda e, tmp=tmp, s=s, n=n: e.activation(tmp[:, :n], s, ACT.Square), tok_of(k), free)
                m, ready = tmp, t_sq
            else:
                m, ready = src(k), tok_of(k)
            for b, (s0, n) in zip(banks, segs):
                tok = pe(lambda e, b=b, m=m, s0=s0, n=n, k=k: e.matmul(PS[:, b, :n], mat, m[:, s0:s0 + n], start=(k == 0), stop=(k == nk - 1)),
                         ready, bank_free[b] if k == 0 else None, t_const, inc=True)
            if square:
                tmp_free[i] = [tok]
        return banks, tok

    def rstd(banks, segs, scale, tok, out=None):
        out = RST if out is None else out
        t = None
        for b, (s0, n) in zip(banks, segs):
            t = act(lambda e, b=b, s0=s0, n=n: e.activation(out[:, s0:s0 + n], PS[:, b, :n], ACT.Sqrt, scale=scale, bias=C("eps")),
                    tok, rst_free)
            bank_free[b] = [t]
        n = segs[-1][0] + segs[-1][1]
        return dve(lambda e: e.reciprocal(out[:, :n], out[:, :n]), t)

    def rms_to(dst, src, nk, segs, scale, gain, tok_of, extra=None):
        banks, tok = colsum(src, nk, segs, ones, tok_of)
        t = rstd(banks, segs, scale, tok)
        n = segs[-1][0] + segs[-1][1]
        out = []
        for k in range(nk):
            out.append(dve(lambda e, k=k: e.scalar_tensor_tensor(dst(k), src(k), gain(k), RST[:, :n], ALU.mult, ALU.mult),
                           t, t_param, extra, tok_of(k)))
        rst_free[:] = [out[-1]]
        return out

    SC = SCR[:, 1584:1592]
    MOD = SCR[:, 1592:1640]
    t_sc = act(lambda e: e.activation(SC, P("c"), ACT.Silu), t_param)
    ada = {"n": 0, "tok": None}
    ADAP = view(30080, 1, 512)[:, 0, :]
    ada_free = []

    def ada_step():
        n = ada["n"]
        if n == 12:
            return
        ada["n"] += 1
        slot, tw, w = fetch_w(a["w_ada"], n * 512)
        b = bank()
        tok = None
        for k in range(8):
            g = k % 4
            tok = pe(lambda e, k=k, g=g, w=w, b=b: e.matmul(PS[32 * g:32 * g + 32, b, :], SC[:, k:k + 1].broadcast_to([128, 32]), w[:, k, :],
                                                       start=(k < 4), stop=(k >= 4)),
                     tw, t_sc, bank_free[b] if k == 0 else None, inc=(k == 7))
        slot.free = [tok]
        t = act(lambda e, b=b: e.activation(ADAP, PS[:, b, :], ACT.Copy), tok, ada_free)
        bank_free[b] = [t]
        b2 = bank()
        for j in range(4):
            tok = pe(lambda e, j=j, b2=b2: e.matmul(PS[:, b2, j:j + 1], ADAP[:, j * 128:(j + 1) * 128], C("sel4"), start=True, stop=True),
                     t, bank_free[b2] if j == 0 else None, t_const, inc=(j == 3))
        ada_free[:] = [tok]
        o = PO["bada"][0] + 4 * n
        t = dve(lambda e, b2=b2, n=n, o=o: e.tensor_tensor(MOD[:, 4 * n:4 * n + 4], PS[:, b2, 0:4], PR[:, o:o + 4], ALU.add), tok, t_param)
        bank_free[b2] = [t]
        ada["tok"] = t

    SEGL = [(0, 512), (512, 16)]
    SEGT = [(0, 512)]
    t_hn = rms_to(lambda k: hn[:, k, :], lambda k: hT[:, k, :], 8, SEGL, 1.0 / D, lambda k: pc("attn_norm", k), lambda k: t_x)

    def proj_T(w, lhs_cols, acts, segs, t_w, t_acts, nk=8):
        out = []
        for s0, n in segs:
            b = bank()
            tok = mms(PS[:, b, :n], [(lhs_cols(k), acts(k, s0, n)) for k in range(nk)], t_w, t_acts, bank_free[b])
            out.append((b, tok))
        return out

    hn_seg = lambda k, s0, n: hn[:, k, s0:s0 + n]
    t_kraw = [None] * 8
    for c in range(2):
        slot, tw, w = fetch_w(a["fox_w_in"], 1024 + 512 * c)
        for j in range(4):
            nt = 4 * c + j
            res = proj_T(None, lambda k, j=j, w=w: w[:, k, j * 128:(j + 1) * 128], hn_seg, SEGL, tw, t_hn[7])
            for (b, tok), (s0, n) in zip(res, SEGL):
                t = act(lambda e, b=b, nt=nt, s0=s0, n=n: e.activation(kT[:, nt, s0:s0 + n], PS[:, b, :n], ACT.Copy), tok)
                bank_free[b] = [t]
            t_kraw[nt] = t
        slot.free = [res[-1][1]]
        ada_step()
    t_v = None
    for c in range(2):
        slot, tw, w = fetch_w(a["fox_w_in"], 2048 + 512 * c)
        for tt in range(5):
            r0, n = (0, NM) if tt == 0 else (NM + 128 * (tt - 1), 128)
            b = bank()
            tok = mms(PS[0:n, b, :], [(hn[:, k, r0:r0 + n], w[:, k, :]) for k in range(8)], tw, t_hn[7], bank_free[b])
            t_v = dve(lambda e, b=b, tt=tt, n=n, c=c: e.tensor_copy(v[0:n, tt, c * 512:(c + 1) * 512], PS[0:n, b, :]), tok)
            bank_free[b] = [t_v]
        slot.free = [tok]
        ada_step()
    wf = P("wf").rearrange("p (k n) -> p k n", k=8)
    FL = view(30592, 4, L)[0:16]
    t = None
    for s0, n in SEGL:
        b = bank()
        tok = mms(PS[0:16, b, :n], [(wf[:, k, :], hn[:, k, s0:s0 + n]) for k in range(8)], t_param, t_hn[7], bank_free[b])
        t = act(lambda e, b=b, s0=s0, n=n: e.activation(FL[:, 0, s0:s0 + n], PS[0:16, b, :n], ACT.Identity, bias=P("bf", 0, 16)), tok)
        bank_free[b] = [t]

    def log1p_exp(z, u, s, q, tok, rows):
        t = dve(lambda e: e.tensor_scalar(u, z, -1.0, None, ALU.mult), tok)
        t = dve(lambda e: e.tensor_tensor(u, u, z, ALU.min), t)
        t = act(lambda e: e.activation(u, u, ACT.Exp), t)
        t = dve(lambda e: e.tensor_scalar(s, u, 2.0, None, ALU.add), t)
        t = dve(lambda e: e.reciprocal(s, s), t)
        t = dve(lambda e: e.tensor_tensor(u, u, s, ALU.mult), t)
        t = dve(lambda e: e.tensor_tensor(s, u, u, ALU.mult), t)
        t = dve(lambda e: e.tensor_scalar(q, s, 1.0 / 17, None, ALU.mult), t)
        for c in (15, 13, 11, 9, 7, 5, 3):
            t = dve(lambda e, c=c: e.scalar_tensor_tensor(q, q, 1.0 / c, s, ALU.add, ALU.mult), t)
        t = dve(lambda e: e.scalar_tensor_tensor(q, q, 1.0, u, ALU.add, ALU.mult), t)
        return dve(lambda e: e.tensor_scalar(q, q, 2.0, None, ALU.mult), t)

    t = log1p_exp(FL[:, 0, :], FL[:, 1, :], FL[:, 2, :], FL[:, 3, :], t, 16)
    t = dve(lambda e: e.scalar_tensor_tensor(FL[:, 1, :], FL[:, 0, :], 0.0, FL[:, 3, :], ALU.min, ALU.subtract), t)
    cT = FL[:, 0, :]
    t_c = dve(lambda e: e.tensor_tensor_scan(cT, C("ones", 0, 16)[:, 0:1].broadcast_to([16, L]), FL[:, 1, :], 0.0, ALU.mult, ALU.add), t)
    CQ = view(32704, 4, 16)
    b = bank()
    for tt in range(4):
        tok = pe(lambda e, tt=tt, b=b: e.transpose(PS[:, b, tt * 16:tt * 16 + 16], cT[:, NM + tt * 128:NM + tt * 128 + 128], C("ident", 0, 16)[:, 0:16]),
                 t_c, bank_free[b], t_const, inc=(tt == 3))
    t_cq = dve(lambda e, b=b: e.tensor_copy(CQ, PS[:, b, 0:64].rearrange("p (a b) -> p a b", a=4)), tok)
    bank_free[b] = [t_cq]
    t_qraw = [None] * 8
    for c in range(2):
        slot, tw, w = fetch_w(a["fox_w_in"], 512 * c)
        for j in range(4):
            nt = 4 * c + j
            (b, tok), = proj_T(None, lambda k, j=j, w=w: w[:, k, j * 128:(j + 1) * 128], hn_seg, [(NM, 512)], tw, t_hn[7])
            t = act(lambda e, b=b, nt=nt: e.activation(qT[:, nt, :], PS[:, b, :], ACT.Copy), tok)
            bank_free[b] = [t]
            t_qraw[nt] = t
        slot.free = [tok]
        ada_step()

    def head_norm(x, nt, n, segs, gain, tok):
        banks, tk = colsum(lambda k: x[:, nt, :], 1, segs, bones, lambda k: tok)
        t = rstd(banks, segs, 1.0 / 64, tk)
        t = dve(lambda e: e.scalar_tensor_tensor(x[:, nt, :], x[:, nt, :], gain, RST[:, :n], ALU.mult, ALU.mult), t, t_param)
        rst_free[:] = [t]
        return t

    t_k = [head_norm(kT, i, L, SEGL, pc("kg", 0), t_kraw[i]) for i in range(8)]
    t_qg = dve(lambda e: e.tensor_scalar(pc("qg", 0), pc("qg", 0), 0.125, None, ALU.mult), t_param)
    t_q = [head_norm(qT, i, T, SEGT, pc("qg", 0), [t_qraw[i], t_qg]) for i in range(8)]
    if stop == "qkv":
        return done(pe, act, dve, pool, sp, counters)

    t_g = [None] * 8
    for c in range(2):
        slot, tw, w = fetch_w(a["fox_w_in"], 3072 + 512 * c)
        for j in range(4):
            nt = 4 * c + j
            (b, tok), = proj_T(None, lambda k, j=j, w=w: w[:, k, j * 128:(j + 1) * 128], hn_seg, [(NM, 512)], tw, t_hn[7])
            t = act(lambda e, b=b, nt=nt: e.activation(gT[:, nt, :], PS[:, b, :], ACT.Sigmoid), tok)
            bank_free[b] = [t]
            t_g[nt] = t
        slot.free = [tok]
        ada_step()

    W0 = 4224
    NCK = [A[:, W0 + i * L:W0 + (i + 1) * L] for i in range(2)]
    PB = [A[:, W0 + (2 + i) * L:W0 + (3 + i) * L] for i in range(3)]
    PT = [A[:, W0 + 5 * L + 640 * i:W0 + 5 * L + 640 * (i + 1)] for i in range(2)]
    ST0 = W0 + 5 * L + 1280
    NMX = A[:, ST0:ST0 + 64]
    SUM = A[:, ST0 + 64:ST0 + 128]
    hn_done = (pe.sem, pe.count)
    nck_free = [[hn_done], [hn_done]]
    pb_free = [[hn_done]] * 3
    pt_free = [[hn_done], [hn_done]]
    st = {}
    NCKTOK = [None, None]
    aux = [0]

    def aux_bank():
        b = 4 + aux[0] % 2
        aux[0] += 1
        return b

    def at_s(n):
        h, qt = divmod(n, 4)
        i, off = h // 2, 64 * (h % 2)
        if qt == 0:
            ba = aux_bank()
            sl = C("ident", 0, 16)[:, h:h + 1].broadcast_to([16, 128])
            tok = pe(lambda e: e.matmul(PS[:, ba, :], sl, cT[:, 0:512], start=True, stop=True), bank_free[ba], t_c, t_const)
            u = h % 2
            t1 = act(lambda e: e.activation(NCK[u][:, 0:512], PS[:, ba, :], ACT.Copy, scale=-1.0), tok, nck_free[u])
            bank_free[ba] = [t1]
            ba = aux_bank()
            tok = pe(lambda e, ba=ba: e.matmul(PS[:, ba, 0:16], sl, cT[:, 512:528], start=True, stop=True), bank_free[ba])
            t1 = act(lambda e, ba=ba: e.activation(NCK[u][:, 512:528], PS[:, ba, 0:16], ACT.Copy, scale=-1.0), tok)
            bank_free[ba] = [t1]
            NCKTOK[u] = t1
        pr = (n % 2) * 2
        ln = NM + 128 * (qt + 1)
        q = qT[off:off + 64, i, qt * 128:(qt + 1) * 128]
        m = min(ln, 512)
        tok = pe(lambda e: e.matmul(PS[:, pr, 0:m], q, kT[off:off + 64, i, 0:m], start=True, stop=True),
                 bank_free[pr], bank_free[pr + 1], t_q[i], t_k[i])
        if ln > 512:
            tok = pe(lambda e: e.matmul(PS[:, pr + 1, 0:ln - 512], q, kT[off:off + 64, i, 512:ln], start=True, stop=True))
        pb = PB[n % 3]
        S = PSF[:, pr * 512:pr * 512 + ln]
        u = h % 2
        t = dve(lambda e: e.scalar_tensor_tensor(pb[:, :ln], S, CQ[:, qt, h:h + 1], NCK[u][:, :ln], ALU.add, ALU.add),
                tok, NCKTOK[u], t_cq, pb_free[n % 3])
        bank_free[pr] = [t]
        bank_free[pr + 1] = [t]
        if qt == 3:
            nck_free[u] = [t]
        t = dve(lambda e: e.tensor_tensor(pb[:, ln - 128:ln], pb[:, ln - 128:ln], C("cmask"), ALU.add), t)
        t = dve(lambda e: e.tensor_reduce(NMX[:, n:n + 1], pb[:, :ln], AX, ALU.max, negate=True), t)
        t = act(lambda e: e.activation(pb[:, :ln], pb[:, :ln], ACT.Exp, bias=NMX[:, n:n + 1], accum_out=SUM[:, n:n + 1]), t)
        t = dve(lambda e: e.reciprocal(SUM[:, n:n + 1], SUM[:, n:n + 1]), t)
        st[n] = pool(lambda e: e.tensor_scalar(pb[:, :ln], pb[:, :ln], SUM[:, n:n + 1], 1.0, ALU.mult, ALU.mult), t)

    def at_t(n):
        h, qt = divmod(n, 4)
        ln = NM + 128 * (qt + 1)
        pb, pt = PB[n % 3], PT[n % 2]
        ba = aux_bank()
        mb = 2 * (n % 2) + 1
        for j in range(qt + 1):
            tok = pe(lambda e, j=j: e.transpose(PS[:, ba, j * 128:(j + 1) * 128], pb[:, NM + 128 * j:NM + 128 * (j + 1)], ident),
                     st[n], bank_free[ba], inc=False)
        tok = pe(lambda e: e.transpose(PS[0:NM, mb, 128:256], pb[:, 0:NM], ident), bank_free[mb])
        pb_free[n % 3] = [tok]
        t1 = act(lambda e: e.activation(pt[:, 0:128 * (qt + 1)], PS[:, ba, 0:128 * (qt + 1)], ACT.Copy), tok, pt_free[n % 2])
        t2 = dve(lambda e: e.tensor_copy(pt[0:NM, 512:640], PS[0:NM, mb, 128:256]), tok, pt_free[n % 2])
        bank_free[ba] = [t1]
        bank_free[mb] = bank_free[mb] + [t2]
        st[n] = [t1, t2]

    def at_pv(n):
        h, qt = divmod(n, 4)
        i, off = h // 2, 64 * (h % 2)
        pt = PT[n % 2]
        bo = 6 + i % 2
        out = PS[off:off + 64, bo, qt * 128:(qt + 1) * 128]
        pairs = [(v[0:NM, 0, 64 * h:64 * h + 64], pt[0:NM, 512:640])]
        pairs += [(v[:, 1 + j, 64 * h:64 * h + 64], pt[:, j * 128:(j + 1) * 128]) for j in range(qt + 1)]
        tok = mms(out, pairs, st[n], t_v, bank_free[bo] if h % 2 == 0 and qt == 0 else None)
        pt_free[n % 2] = [tok]
        if h % 2 == 1 and qt == 3:
            t = dve(lambda e: e.tensor_tensor(oT[:, i, :], PS[:, bo, :], gT[:, i, :], ALU.mult), tok, t_g[i], t_zy, t_zl)
            bank_free[bo] = [t]
            t_o[i] = t

    t_o = [None] * 8
    for n in range(64 + 2):
        if n < 64:
            at_s(n)
        if n >= 1 and n - 1 < 64:
            at_t(n - 1)
        if n >= 2:
            at_pv(n - 2)
    turn[0] = 0
    if stop == "attn":
        return done(pe, act, dve, pool, sp, counters)

    t_h = [None] * 8
    for c in range(2):
        slot, tw, w = fetch_w(a["fox_w_out"], 512 * c)
        for j in range(4):
            nt = 4 * c + j
            b = bank()
            tok = mms(PS[:, b, :], [(w[:, k, j * 128:(j + 1) * 128], oT[:, k, :]) for k in range(8)], tw, t_o, bank_free[b])
            t_h[nt] = dve(lambda e, b=b, nt=nt: e.tensor_tensor(hT[:, nt, NM:L], hT[:, nt, NM:L], PS[:, b, :], ALU.add), tok)
            bank_free[b] = [t_h[nt]]
        slot.free = [tok]
        ada_step()
    h1 = lambda k: hT[:, k, NM:L]
    attn_done = (pe.sem, pe.count)
    h2n = view(4224, 8, T)
    t_n = rms_to(lambda k: h2n[:, k, :], h1, 8, SEGT, 1.0 / D, lambda k: pc("ffn_norm", k), lambda k: t_h[k], extra=attn_done)
    hid = view(8448, 22, T)
    t_hid = [None] * 22
    for c in range(11):
        slot, tw = fetch((0, (8, 256), wrows(a["ffn_w_in"], 0, 8, 256 * c, 256)),
                         (2048, (8, 256), wrows(a["ffn_w_in"], 0, 8, FH + 256 * c, 256)))
        w = slot.ap.rearrange("p (g k n) -> p g k n", g=2, k=8)
        for j in range(2):
            nt = 2 * c + j
            bs = []
            for g in range(2):
                b = bank()
                tok = mms(PS[:, b, :], [(w[:, g, k, j * 128:(j + 1) * 128], h2n[:, k, :]) for k in range(8)], tw, t_n[7], bank_free[b])
                bs.append((b, tok))
            t = act(lambda e, b=bs[0][0], nt=nt: e.activation(hid[:, nt, :], PS[:, b, :], ACT.Silu), bs[0][1], attn_done)
            bank_free[bs[0][0]] = [t]
            t_hid[nt] = dve(lambda e, b=bs[1][0], nt=nt: e.tensor_tensor(hid[:, nt, :], hid[:, nt, :], PS[:, b, :], ALU.mult), t, bs[1][1])
            bank_free[bs[1][0]] = [t_hid[nt]]
        slot.free = [tok]
        if c < 4:
            ada_step()
    for c in range(2):
        bs = [bank() for _ in range(4)]
        k0 = 0
        for nk in (8, 8, 6):
            slot, tw, w = fetch_w(a["ffn_w_out"], 512 * c, r0=128 * k0, nk=nk)
            for j in range(4):
                tok = mms(PS[:, bs[j], :], [(w[:, k, j * 128:(j + 1) * 128], hid[:, k0 + k, :]) for k in range(nk)],
                          tw, [t_hid[k0 + k] for k in range(nk)], bank_free[bs[j]] if k0 == 0 else None, start=(k0 == 0), stop=(k0 + nk == 22))
                if k0 + nk == 22:
                    nt = 4 * c + j
                    t_h[nt] = dve(lambda e, b=bs[j], nt=nt: e.tensor_tensor(hT[:, nt, NM:L], hT[:, nt, NM:L], PS[:, b, :], ALU.add), tok)
                    bank_free[bs[j]] = [t_h[nt]]
            slot.free = [tok]
            k0 += nk
    x2 = view(28672, 8, T)
    t_x2 = rms_to(lambda k: x2[:, k, :], h1, 8, SEGT, 1.0 / D, lambda k: pc("final_norm", k), lambda k: t_h[k])
    if stop == "fb":
        return done(pe, act, dve, pool, sp, counters)
    while ada["n"] < 12:
        ada_step()
    t_spill = act.dma(dsem("spill"), lambda e: e.dma_start(a["x2_d"], x2), t_x2[7])

    def modcol(j, k):
        return MOD[:, 8 * j + k:8 * j + k + 1]

    def ada_norm(dst, src, tok_of, gname, jsh, jsc, gm, extra):
        t = dve(lambda e: e.tensor_scalar(gm, MOD[:, 8 * jsc:8 * jsc + 8], 1.0, None, ALU.add), ada["tok"], extra)
        t_gm = dve(lambda e: e.tensor_tensor(gm, gm, P(gname), ALU.mult), t, t_param)
        banks, tok = colsum(src, 8, SEGT, ones, tok_of)
        t = rstd(banks, SEGT, 1.0 / D, tok)
        out = []
        ts = [dve(lambda e, k=k: e.scalar_tensor_tensor(dst(k), src(k), gm[:, k:k + 1], RST[:, :T], ALU.mult, ALU.mult), t, t_gm, extra)
              for k in range(8)]
        rst_free[:] = [ts[-1]]
        for k in range(8):
            out.append(dve(lambda e, k=k: e.tensor_scalar(dst(k), dst(k), modcol(jsh, k), None, ALU.add), ts[k]))
        return out

    n1 = view(0, 8, T)
    hT_done = t_x2[7]
    t_n1 = ada_norm(lambda k: n1[:, k, :], lambda k: x2[:, k, :], lambda k: t_x2[k], "norm1", 0, 1, SC, hT_done)
    if stop == "n1":
        return done(pe, act, dve, pool, sp, counters)

    UW = T + 30
    u = view(4096, 8, UW)
    cv = view(4096 + 8 * UW, 8, T)
    CG = A[:, 12528:12528 + 512]
    ymix = view(13312, 8, T)
    ffn_done = t_x2[7]
    t_z = dve(lambda e: e.memset(u[:, :, 0:30], 0.0), ffn_done)
    t_cv = [None] * 8
    CA = [A[:, 17408 + 512 * i:17408 + 512 * (i + 1)] for i in range(2)]
    wi = a["w_in"]
    for c in range(4):
        slot, tw = fetch((0, (8, 256), wrows(wi, 0, 8, 256 * c, 256)), (2048, (8, 256), wrows(wi, 0, 8, 1024 + 256 * c, 256)))
        w = slot.ap.rearrange("p (g k n) -> p g k n", g=2, k=8)
        for j in range(2):
            nt = 2 * c + j
            bs = []
            for g in (1, 0):
                b = bank()
                tok = mms(PS[:, b, :], [(w[:, g, k, j * 128:(j + 1) * 128], n1[:, k, :]) for k in range(8)], tw, t_n1[7], bank_free[b])
                bs.append((b, tok))
            dst = u[:, nt, 30:UW]
            t = act(lambda e, b=bs[0][0], dst=dst: e.activation(dst, PS[:, b, :], ACT.Sigmoid), bs[0][1], ffn_done)
            bank_free[bs[0][0]] = [t]
            t = dve(lambda e, b=bs[1][0], dst=dst: e.tensor_tensor(dst, dst, PS[:, b, :], ALU.mult), t, bs[1][1], t_z)
            bank_free[bs[1][0]] = [t]
            w0 = PO["cvw"][0] + 31 * nt
            t = dve(lambda e, nt=nt, w0=w0: e.tensor_scalar(cv[:, nt, :], u[:, nt, 0:T], PR[:, w0:w0 + 1], pc("cvb", nt), ALU.mult, ALU.add), t)
            for i in range(1, 31):
                t = dve(lambda e, nt=nt, i=i, w0=w0: e.scalar_tensor_tensor(cv[:, nt, :], u[:, nt, i:i + T], PR[:, w0 + i:w0 + i + 1], cv[:, nt, :], ALU.mult, ALU.add), t)
            t_cv[nt] = t
        slot.free = [tok]

    def xbc_tile(nt, lhs, tw, dst, raw, raw_free, extra=None):
        b = bank()
        tok = mms(PS[:, b, :], [(lhs(k), n1[:, k, :]) for k in range(8)], tw, t_n1[7], bank_free[b])
        t = act(lambda e: e.activation(raw[:, 3:3 + T], PS[:, b, :], ACT.Copy), tok, raw_free)
        bank_free[b] = [t]
        s0 = PO["scw"][0] + 4 * nt
        t = dve(lambda e: e.tensor_scalar(dst, raw[:, 0:T], PR[:, s0:s0 + 1], pc("scb", nt), ALU.mult, ALU.add), t, t_rz, extra)
        for i in range(1, 4):
            t = dve(lambda e, i=i: e.scalar_tensor_tensor(dst, raw[:, i:i + T], PR[:, s0 + i:s0 + i + 1], dst, ALU.mult, ALU.add), t)
        t2 = act(lambda e: e.activation(dst, dst, ACT.Silu), t)
        return tok, t2, t

    Bf = view(18432, 4, T)
    Cf = view(20480, 4, T)
    Bt = view(22528, 4, 512)
    RAW = [A[:, 24576 + 516 * i:24576 + 516 * i + 515] for i in range(2)]
    t_rz = [dve(lambda e, i=i: e.memset(RAW[i][:, 0:3], 0.0), ffn_done) for i in range(2)]
    raw_free = [[], []]
    t_B, t_C = [None] * 4, [None] * 4
    for c, (dst, tt_) in enumerate(((Bf, t_B), (Cf, t_C))):
        slot, tw, w = fetch_w(wi, 4096 + 2048 + 512 * c)
        for j in range(4):
            i = j % 2
            tok, t2, t = xbc_tile(16 + 4 * c + j, lambda k, j=j, w=w: w[:, k, j * 128:(j + 1) * 128], tw, dst[:, j, :], RAW[i], raw_free[i], ffn_done)
            raw_free[i] = [t]
            tt_[j] = t2
        slot.free = [tok]
    for tt in range(4):
        b = bank()
        for g in range(4):
            tok = pe(lambda e, tt=tt, g=g, b=b: e.transpose(PS[:, b, g * 128:(g + 1) * 128], Bf[:, g, tt * 128:(tt + 1) * 128], ident),
                     bank_free[b], t_B[g], inc=(g == 3))
        t_Bt = act(lambda e, tt=tt, b=b: e.activation(Bt[:, tt, :], PS[:, b, :], ACT.Copy), tok)
        bank_free[b] = [t_Bt]
    wdt = P("wdt").rearrange("p (k n) -> p k n", k=8)
    DT = view(25632, 4, T)[0:32]
    b = bank()
    tok = mms(PS[0:32, b, :], [(wdt[:, k, :], n1[:, k, :]) for k in range(8)], t_n1[7], bank_free[b])
    t = act(lambda e, b=b: e.activation(DT[:, 0, :], PS[0:32, b, :], ACT.Identity, bias=P("dtb", 0, 32)), tok, ffn_done)
    bank_free[b] = [t]
    t = log1p_exp(DT[:, 0, :], DT[:, 1, :], DT[:, 2, :], DT[:, 3, :], t, 32)
    t_dt = dve(lambda e: e.scalar_tensor_tensor(DT[:, 0, :], DT[:, 0, :], 0.0, DT[:, 3, :], ALU.max, ALU.add), t)
    alg = P("alog", 0, 32)
    t = act(lambda e: e.activation(alg, alg, ACT.Exp), t_param)
    t = dve(lambda e: e.tensor_scalar(DT[:, 1, :], DT[:, 0, :], alg, -1.0, ALU.mult, ALU.mult), t, t_dt)
    for c in range(4):
        t_acs = dve(lambda e, c=c: e.tensor_tensor_scan(DT[:, 2, c * 128:(c + 1) * 128], C("ones", 0, 32),
                                                DT[:, 1, c * 128:(c + 1) * 128], 0.0, ALU.mult, ALU.add), t)
    dtT, acsT = DT[:, 0, :], DT[:, 2, :]
    TK = view(27680, 5, 128)
    b = bank()
    for w_, srcT in enumerate((dtT, acsT)):
        for c in range(4):
            tok = pe(lambda e, w_=w_, c=c, srcT=srcT, b=b: e.transpose(PS[:, b, w_ * 128 + c * 32:w_ * 128 + c * 32 + 32], srcT[:, c * 128:(c + 1) * 128],
                                                             C("ident", 0, 32)[:, 0:32]), bank_free[b], t_acs, inc=(w_ == 1 and c == 3))
    t_tk = dve(lambda e, b=b: e.tensor_copy(TK[:, 0:2, :], PS[:, b, 0:256].rearrange("p (a b) -> p a b", a=2)), tok, ffn_done)
    bank_free[b] = [t_tk]
    b = bank()
    tok = pe(lambda e, b=b: e.matmul(PS[:, b, 0:128], ident[:, 127:128].broadcast_to([128, 128]), TK[:, 1, :], start=True, stop=True), bank_free[b], t_tk)
    t = dve(lambda e, b=b: e.tensor_copy(TK[:, 2, :], PS[:, b, 0:128]), tok)
    bank_free[b] = [t]
    t = dve(lambda e: e.tensor_tensor(TK[:, 3, :], TK[:, 2, :], TK[:, 1, :], ALU.subtract), t)
    t = act(lambda e: e.activation(TK[:, 3, :], TK[:, 3, :], ACT.Exp), t)
    t_tk2 = act(lambda e: e.activation(TK[:, 4, :], TK[:, 2, :], ACT.Exp), t)

    banks, tok = colsum(lambda k: cv[:, k, :], 8, SEGT, ones, lambda k: t_cv[k], square=False)
    t = act(lambda e, b=banks[0]: e.activation(RST[:, :T], PS[:, b, :], ACT.Copy, scale=1.0 / D), tok, rst_free)
    bank_free[banks[0]] = [t]
    tc = [dve(lambda e, k=k: e.tensor_tensor(cv[:, k, :], cv[:, k, :], RST[:, :T], ALU.subtract), t) for k in range(8)]
    rst_free[:] = [tc[-1]]
    banks, tok = colsum(lambda k: cv[:, k, :], 8, SEGT, ones, lambda k: tc[k])
    t = rstd(banks, SEGT, 1.0 / D, tok)
    tl = []
    for k in range(8):
        t1 = dve(lambda e, k=k: e.tensor_tensor(cv[:, k, :], cv[:, k, :], RST[:, :T], ALU.mult), t, tc[k])
        tl.append(act(lambda e, k=k: e.activation(cv[:, k, :], cv[:, k, :], ACT.Silu, scale=pc("lng", k), bias=pc("lnb", k)), t1))
    rst_free[:] = [t1]
    SG = [A[:, 17408 + 512 * i:17408 + 512 * (i + 1)] for i in range(2)]
    sg_free = [[ffn_done], [ffn_done]]
    t_y = [None] * 8
    for c in range(2):
        slot1, tw1, w1_ = fetch_w(wi, 7200 + 512 * c)
        slot2, tw2, w2_ = fetch_w(a["w_cv_out"], 512 * c)
        for j in range(4):
            nt = 4 * c + j
            i = nt % 2
            b1, b2 = bank(), bank()
            tok1 = mms(PS[:, b1, :], [(w1_[:, k, j * 128:(j + 1) * 128], n1[:, k, :]) for k in range(8)], tw1, bank_free[b1])
            t = act(lambda e, b1=b1, i=i: e.activation(SG[i], PS[:, b1, :], ACT.Sigmoid), tok1, sg_free[i])
            bank_free[b1] = [t]
            tok2 = mms(PS[:, b2, :], [(w2_[:, k, j * 128:(j + 1) * 128], cv[:, k, :]) for k in range(8)], tw2, tl, bank_free[b2])
            t_y[nt] = dve(lambda e, b2=b2, nt=nt, i=i: e.tensor_tensor(ymix[:, nt, :], SG[i], PS[:, b2, :], ALU.mult), t, tok2)
            bank_free[b2] = [t_y[nt]]
            sg_free[i] = [t_y[nt]]
        slot1.free = [tok1]
        slot2.free = [tok2]
    if stop == "ycv":
        return done(pe, act, dve, pool, sp, counters)

    cv_done = [(pe.sem, pe.count), (dve.sem, dve.count), t_spill]
    t_yspill = act.dma(dsem("yspill"), lambda e: e.dma_start(a["ymix_d"], ymix), t_y[7])
    free2 = cv_done + [t_yspill]
    xsf = view(4096, 4, T)
    xdt = view(6144, 4, 512)
    yT = [view(8192, 8, T), view(28672, 8, T)]
    yt = lambda k: yT[k // 8][:, k % 8, :]
    STS = [A[:, 13312 + 512 * i:13312 + 512 * (i + 1)] for i in range(3)]
    XD = [A[:, 14848 + 512 * i:14848 + 512 * (i + 1)] for i in range(2)]
    EB = [A[:, 15872 + 512 * i:15872 + 512 * (i + 1)] for i in range(2)]
    ZB = A[:, 16896:17408]
    MB = [view(12288, 2, 512), view(17408, 2, 512)]
    CBM = sb("cbm", [128, 512])
    mb_free, eb_free, xd_free = [free2, free2], [free2, free2], [free2, free2]
    zb_free, cbm_free, xs_free, xdt_free = free2, [], free2, free2
    t_dsk = t_param
    h64 = lambda x: x.rearrange("p (h d) -> p h d", d=64)
    for g in range(4):
        slot1, tw1, w1_ = fetch_w(wi, 4096 + 512 * g)
        t_xs = []
        for j in range(4):
            i = j % 2
            tok, t2, t = xbc_tile(4 * g + j, lambda k, j=j, w=w1_: w[:, k, j * 128:(j + 1) * 128], tw1, xsf[:, j, :], RAW[i], raw_free[i], xs_free)
            raw_free[i] = [t]
            t_xs.append(t2)
        slot1.free = [tok]
        b = bank()
        for c in range(4):
            tok = pe(lambda e, c=c, b=b, g=g: e.matmul(PS[:, b, c * 128:(c + 1) * 128], Bf[:, g, c * 128:(c + 1) * 128], Cf[:, g, c * 128:(c + 1) * 128],
                                                  start=True, stop=True), bank_free[b], t_B[g], t_C[g], inc=(c == 3))
        sm = C("smask").rearrange("p (a b) -> p a b", a=1).broadcast_to([128, 4, 128])
        t_cb = dve(lambda e, b=b, sm=sm: e.tensor_tensor(CBM[:, :].rearrange("p (a b) -> p a b", a=4), PS[:, b, :].rearrange("p (a b) -> p a b", a=4), sm, ALU.mult),
                   tok, cbm_free)
        bank_free[b] = [t_cb]
        t_xdt = []
        for c in range(4):
            b = bank()
            for j in range(4):
                tok = pe(lambda e, c=c, j=j, b=b: e.transpose(PS[:, b, j * 128:(j + 1) * 128], xsf[:, j, c * 128:(c + 1) * 128], ident),
                         bank_free[b], t_xs[j], inc=(j == 3))
            sc = TK[:, 0, c * 32 + 8 * g:c * 32 + 8 * g + 8].rearrange("p (h d) -> p h d", d=1).broadcast_to([128, 8, 64])
            t = dve(lambda e, c=c, b=b, sc=sc: e.tensor_tensor(h64(xdt[:, c, :]), h64(PS[:, b, :]), sc, ALU.mult), tok, xdt_free, t_tk)
            bank_free[b] = [t]
            t_xdt.append(t)
        t_st = [None] * 3
        for c in range(3):
            i = c % 2
            dc = TK[:, 3, c * 32 + 8 * g:c * 32 + 8 * g + 8].rearrange("p (h d) -> p h d", d=1).broadcast_to([128, 8, 64])
            t = dve(lambda e, c=c, i=i, dc=dc: e.tensor_tensor(h64(XD[i]), h64(xdt[:, c, :]), dc, ALU.mult), t_xdt[c], xd_free[i], t_tk2)
            b = bank()
            tok = pe(lambda e, c=c, b=b, g=g, i=i: e.matmul(PS[:, b, :], Bt[:, c, g * 128:(g + 1) * 128], XD[i], start=True, stop=True), t, t_Bt, bank_free[b])
            xd_free[i] = [tok]
            if c == 0:
                t = dve(lambda e, b=b: e.tensor_copy(STS[0], PS[:, b, :]), tok, zb_free)
            else:
                cd = TK[:, 4, c * 32 + 8 * g:c * 32 + 8 * g + 8].rearrange("p (h d) -> p h d", d=1).broadcast_to([128, 8, 64])
                t = dve(lambda e, c=c, cd=cd: e.tensor_tensor(h64(STS[c]), h64(STS[c - 1]), cd, ALU.mult), t_st[c - 1], zb_free)
                t = dve(lambda e, c=c, b=b: e.tensor_tensor(STS[c], STS[c], PS[:, b, :], ALU.add), t, tok)
            bank_free[b] = [t]
            t_st[c] = t
        slot2, tw2, w2_ = fetch_w(wi, 2048 + 512 * g)
        t_yg = []
        for i in range(4):
            nt = 4 * g + i
            m, eb = MB[i % 2], EB[i % 2]
            td = []
            for hh in range(2):
                h = 8 * g + 2 * i + hh
                b = bank()
                tok = pe(lambda e, b=b, h=h: e.matmul(PS[:, b, :], C("ident", 0, 32)[:, h:h + 1].broadcast_to([32, 128]), acsT, start=True, stop=True),
                         t_acs, bank_free[b])
                for c in range(4):
                    t = dve(lambda e, b=b, h=h, hh=hh, c=c, m=m: e.tensor_scalar(m[:, hh, c * 128:(c + 1) * 128], PS[:, b, c * 128:(c + 1) * 128],
                                                                 TK[:, 1, c * 32 + h:c * 32 + h + 1], 0.0, ALU.subtract, ALU.min), tok, mb_free[i % 2], t_tk)
                bank_free[b] = [t]
            t = act(lambda e, m=m: e.activation(m, m, ACT.Exp), t)
            cb = CBM[:, :].rearrange("p (a b) -> p a b", a=1).broadcast_to([128, 2, 512])
            t_m = dve(lambda e, m=m, cb=cb: e.tensor_tensor(m, m, cb, ALU.mult), t, t_cb)
            b = bank()
            h0 = 8 * g + 2 * i
            for hh in range(2):
                tok = pe(lambda e, b=b, h0=h0, hh=hh: e.matmul(PS[64 * hh:64 * hh + 64, b, :], C("ident", 0, 32)[:, h0 + hh:h0 + hh + 1].broadcast_to([32, 64]), acsT,
                                                            start=True, stop=True), t_acs, bank_free[b])
            t_eb = act(lambda e, b=b, eb=eb: e.activation(eb, PS[:, b, :], ACT.Exp), tok, eb_free[i % 2])
            bank_free[b] = [t_eb]
            bz = bank()
            tokz = mms(PS[:, bz, :], [(w2_[:, k, i * 128:(i + 1) * 128], n1[:, k, :]) for k in range(8)], tw2, bank_free[bz])
            t_z = act(lambda e, bz=bz: e.activation(ZB, PS[:, bz, :], ACT.Silu), tokz, zb_free)
            bank_free[bz] = [t_z]
            bo = bank()
            for c in range(1, 4):
                tok = pe(lambda e, c=c, bo=bo, g=g, i=i: e.matmul(PS[:, bo, c * 128:(c + 1) * 128], STS[c - 1][:, i * 128:(i + 1) * 128], Cf[:, g, c * 128:(c + 1) * 128],
                                                             start=True, stop=True), t_st[c - 1], bank_free[bo], inc=(c == 3))
            t = dve(lambda e, bo=bo, eb=eb: e.tensor_tensor(eb[:, 128:512], eb[:, 128:512], PS[:, bo, 128:512], ALU.mult), t_eb, tok)
            bank_free[bo] = [t]
            bd = bank()
            for c in range(4):
                for hh in range(2):
                    tok = pe(lambda e, c=c, hh=hh, bd=bd, i=i, m=m: e.matmul(PS[64 * hh:64 * hh + 64, bd, c * 128:(c + 1) * 128], xdt[:, c, (2 * i + hh) * 64:(2 * i + hh) * 64 + 64],
                                                                m[:, hh, c * 128:(c + 1) * 128], start=True, stop=True),
                             t_m, t_xdt[c], bank_free[bd] if c == 0 and hh == 0 else None, inc=(c == 3 and hh == 1))
            mb_free[i % 2] = [tok]
            t2 = dve(lambda e, nt=nt, i=i, bd=bd: e.scalar_tensor_tensor(yt(nt), xsf[:, i, :], pc("dsk", nt), PS[:, bd, :], ALU.mult, ALU.add), tok, free2)
            bank_free[bd] = [t2]
            t2 = dve(lambda e, nt=nt, eb=eb: e.tensor_tensor(yt(nt)[:, 128:512], yt(nt)[:, 128:512], eb[:, 128:512], ALU.add), t, t2)
            eb_free[i % 2] = [t2]
            t2 = dve(lambda e, nt=nt: e.tensor_tensor(yt(nt), yt(nt), ZB, ALU.mult), t2, t_z)
            zb_free = [t2]
            t_yg.append(t2)
        slot2.free = [tokz]
        cbm_free, xs_free, xdt_free = [t_m], [t2], [tok]
        banks, tok = colsum(lambda k, g=g: yt(4 * g + k), 4, SEGT, ones, lambda k, t_yg=t_yg: t_yg[k])
        t = rstd(banks, SEGT, 1.0 / 512, tok)
        for k in range(4):
            nt = 4 * g + k
            t_yl = dve(lambda e, nt=nt: e.scalar_tensor_tensor(yt(nt), yt(nt), pc("sng", nt), RST[:, :T], ALU.mult, ALU.mult), t, t_param)
        rst_free[:] = [t_yl]
    ssd_done = [t_yl, (pe.sem, pe.count)]
    if stop == "ssd":
        return done(pe, act, dve, pool, sp, counters)

    ymix2 = view(4096, 8, T)
    x2b = view(18432, 8, T)
    t_ym = act.dma(dsem("back"), lambda e: e.dma_start(ymix2, a["ymix_d"]), ssd_done)
    t_x2b = act.dma(dsem("back2"), lambda e: e.dma_start(x2b, a["x2_d"]), ssd_done)
    SG = [A[:, 12288 + 512 * i:12288 + 512 * (i + 1)] for i in range(2)]
    sg_free = [ssd_done, ssd_done]
    t_ym_ = [None] * 8
    for c in range(2):
        slot1, tw1, w1_ = fetch_w(wi, 8224 + 512 * c)
        slot2, tw2, w2_ = fetch_w(a["w_ssm_out"], 512 * c)
        slot3, tw3, w3_ = fetch_w(a["w_ssm_out"], 512 * c, r0=1024)
        for j in range(4):
            nt = 4 * c + j
            i = nt % 2
            b1, b2 = bank(), bank()
            tok1 = mms(PS[:, b1, :], [(w1_[:, k, j * 128:(j + 1) * 128], n1[:, k, :]) for k in range(8)], tw1, bank_free[b1])
            t = act(lambda e, b1=b1, i=i: e.activation(SG[i], PS[:, b1, :], ACT.Sigmoid), tok1, sg_free[i])
            bank_free[b1] = [t]
            pairs = [(w2_[:, k, j * 128:(j + 1) * 128], yt(k)) for k in range(8)] + [(w3_[:, k, j * 128:(j + 1) * 128], yt(8 + k)) for k in range(8)]
            tok2 = mms(PS[:, b2, :], pairs, tw2, tw3, t_yl, bank_free[b2])
            t = dve(lambda e, b2=b2, i=i: e.tensor_tensor(SG[i], SG[i], PS[:, b2, :], ALU.mult), t, tok2)
            bank_free[b2] = [t]
            t = dve(lambda e, nt=nt, i=i: e.tensor_tensor(ymix2[:, nt, :], ymix2[:, nt, :], SG[i], ALU.add), t, t_ym)
            sg_free[i] = [t]
            t_ym_[nt] = t
        slot1.free, slot2.free, slot3.free = [tok1], [tok2], [tok2]
    t_h2 = [None] * 8
    for c in range(2):
        slot, tw, w = fetch_w(a["w_mix_out"], 512 * c)
        for j in range(4):
            nt = 4 * c + j
            b = bank()
            tok = mms(PS[:, b, :], [(w[:, k, j * 128:(j + 1) * 128], ymix2[:, k, :]) for k in range(8)], tw, t_ym_, bank_free[b])
            t_h2[nt] = dve(lambda e, b=b, nt=nt: e.scalar_tensor_tensor(x2b[:, nt, :], PS[:, b, :], modcol(2, nt), x2b[:, nt, :], ALU.mult, ALU.add), tok, t_x2b)
            bank_free[b] = [t_h2[nt]]
        slot.free = [tok]
    n2 = view(0, 8, T)
    mix_done = [(pe.sem, pe.count)]
    t_n2 = ada_norm(lambda k: n2[:, k, :], lambda k: x2b[:, k, :], lambda k: t_h2[k], "norm2", 3, 4, SC, mix_done)
    if stop == "n2":
        return done(pe, act, dve, pool, sp, counters)

    RW = view(8192, 8, 72)
    t_rw = act.dma(dsem("rw"), lambda e: e.dma_start(RW, a["rw"]), mix_done)
    LG = view(8768, 4, 72)
    R = 9088
    r3 = lambda o, n: view(R + o, 4, n)
    gmax, gidx, emax, eidx = r3(0, 8), r3(32, 8), r3(64, 8), r3(96, 8)
    eg = r3(128, 8)
    s1, s2, gp, wa, wb, tmp1, tmp2 = (r3(160 + 4 * i, 1) for i in range(7))
    el8 = r3(200, 8)
    msel = view(R + 240, 4, 64)
    OH = [view(R + 496 + 256 * i, 4, 64) for i in range(2)]
    OHS = view(R + 1008, 4, 64)
    POS = view(R + 1264, 4, 64)
    IDX = CBM[:, 64:80].bitcast(U32)
    KEEP = CBM[:, 0:64]
    SLOTU = CBM[:, 80:88].bitcast(U32)
    LIST = CBM[:, 88:120].bitcast(U32)
    TOKU = CBM[:, 120:124].bitcast(U32)
    for tt in range(4):
        b = bank()
        tok = mms(PS[:, b, 0:72], [(n2[:, k, tt * 128:(tt + 1) * 128], RW[:, k, :]) for k in range(8)], t_rw, t_n2, bank_free[b])
        t_lg = dve(lambda e, b=b, tt=tt: e.tensor_tensor(LG[:, tt, :], PS[:, b, 0:72], P("rb"), ALU.add), tok, t_param)
        bank_free[b] = [t_lg]
    h2t = view(4096, 4, D)
    n2t = [A[:, 28672 + 1024 * i:28672 + 1024 * (i + 1)] for i in range(2)]
    n2t_free = [mix_done, mix_done]
    for tt in range(4):
        for half in range(2):
            for src, dst_of in ((n2, None), (x2b, h2t)):
                b = bank()
                for j in range(4):
                    tok = pe(lambda e, tt=tt, half=half, j=j, src=src, b=b: e.transpose(PS[:, b, j * 128:(j + 1) * 128], src[:, 4 * half + j, tt * 128:(tt + 1) * 128], ident),
                             bank_free[b], t_n2, t_h2, inc=(j == 3))
                dst = (n2t[tt % 2] if dst_of is None else h2t[:, tt, :])[:, 512 * half:512 * half + 512]
                t = act(lambda e, dst=dst, b=b: e.activation(dst, PS[:, b, :], ACT.Copy), tok, n2t_free[tt % 2] if dst_of is None else mix_done)
                bank_free[b] = [t]
                if dst_of is None:
                    t_nt = t
                else:
                    t_h2t = t
        t_n2d = act.dma(dsem(f"n2d{tt % 2}"), lambda e, tt=tt: e.dma_start(a["n2_d"][tt * 128:(tt + 1) * 128, :], n2t[tt % 2]), t_nt)
        n2t_free[tt % 2] = [t_n2d]
    t_n2ds = [(dsem("n2d0")[0], dsem("n2d0")[1]), (dsem("n2d1")[0], dsem("n2d1")[1])]
    dense_done = [(pe.sem, pe.count)]
    extra_slots = [Slot(A[:, 11264 + WC * i:11264 + WC * (i + 1)], f"x{i}") for i in range(5)]

    bc = lambda x, n: x.broadcast_to([128, 4, n])
    t = t_lg
    for tt in range(4):
        tm = dve(lambda e, tt=tt: e.max(gmax[:, tt, :], LG[:, tt, 0:8]), t)
    for tt in range(4):
        t = dve(lambda e, tt=tt: e.max_index(IDX[:, 0:8], gmax[:, tt, :], LG[:, tt, 0:8]), tm, t)
        t = dve(lambda e, tt=tt: e.tensor_copy(gidx[:, tt, :], IDX[:, 0:8]), t)
    t1 = dve(lambda e: e.tensor_tensor(eg, LG[:, :, 0:8], bc(gmax[:, :, 0:1], 8), ALU.subtract), tm)
    t1 = act(lambda e: e.activation(eg, eg, ACT.Exp), t1)
    t1 = dve(lambda e: e.tensor_reduce(s1, eg, AX, ALU.add), t1)
    t_gp = dve(lambda e: e.reciprocal(gp, s1), t1)
    t2 = dve(lambda e: e.tensor_tensor(el8, C("iota8").rearrange("p (a b) -> p a b", a=1).broadcast_to([128, 4, 8]), bc(gidx[:, :, 0:1], 8), ALU.is_equal), t)
    t2 = [dve(lambda e, tt=tt: e.tensor_tensor(msel[:, tt, :].rearrange("p (a b) -> p a b", b=8), LG[:, tt, 8:72].rearrange("p (a b) -> p a b", b=8),
                                        el8[:, tt, :].rearrange("p (a b) -> p a b", b=1).broadcast_to([128, 8, 8]), ALU.mult), t2) for tt in range(4)][-1]
    t2 = [dve(lambda e, tt=tt: e.tensor_reduce(el8[:, tt, :], msel[:, tt, :].rearrange("p (a b) -> p b a", b=8), AX, ALU.add), t2) for tt in range(4)][-1]
    for tt in range(4):
        tm = dve(lambda e, tt=tt: e.max(emax[:, tt, :], el8[:, tt, :]), t2)
    for tt in range(4):
        t = dve(lambda e, tt=tt: e.max_index(IDX[:, 8:16], emax[:, tt, :], el8[:, tt, :]), tm, t)
        t = dve(lambda e, tt=tt: e.tensor_copy(eidx[:, tt, :], IDX[:, 8:16]), t)
    t3 = dve(lambda e: e.tensor_tensor(eg, emax, bc(emax[:, :, 0:1], 8), ALU.subtract), t_gp, tm)
    t3 = act(lambda e: e.activation(eg, eg, ACT.Exp), t3)
    t3 = dve(lambda e: e.tensor_reduce(s1, eg, AX, ALU.add), t3)
    t3 = dve(lambda e: e.reciprocal(s1, s1), t3)
    t3 = dve(lambda e: e.tensor_tensor(eg, eg, bc(s1, 8), ALU.mult), t3)
    t3 = dve(lambda e: e.tensor_tensor(s2, eg[:, :, 0:1], eg[:, :, 1:2], ALU.add), t3)
    t3 = dve(lambda e: e.reciprocal(s2, s2), t3)
    t3 = dve(lambda e: e.tensor_tensor(s2, s2, gp, ALU.mult), t3)
    WK = [KEEP[:, 4 * i:4 * i + 4].rearrange("p (a b) -> p a b", b=1) for i in range(2)]
    for i in range(2):
        t_wk = dve(lambda e, i=i: e.tensor_tensor(WK[i], eg[:, :, i:i + 1], s2, ALU.mult), t3)
    t4 = dve(lambda e: e.tensor_scalar(gidx[:, :, 0:1], gidx[:, :, 0:1], 8.0, None, ALU.mult), t, t2)
    t4 = dve(lambda e: e.tensor_tensor(eidx[:, :, 0:2], eidx[:, :, 0:2], bc(gidx[:, :, 0:1], 2), ALU.add), t4)
    i64 = C("iota64").rearrange("p (a b) -> p a b", a=1).broadcast_to([128, 4, 64])
    for i in range(2):
        t5 = dve(lambda e, i=i: e.tensor_tensor(OH[i], i64, bc(eidx[:, :, i:i + 1], 64), ALU.is_equal), t4)
    t5 = dve(lambda e: e.tensor_tensor(OHS, OH[0], OH[1], ALU.add), t5)
    b = bank()
    for tt in range(4):
        for s in range(tt + 1):
            tok = pe(lambda e, tt=tt, s=s, b=b: e.matmul(PS[:, b, tt * 64:tt * 64 + 64], C("ustrict") if s == tt else ones, OHS[:, s, :], start=(s == 0), stop=(s == tt)),
                     t5, bank_free[b])
    for s in range(4):
        tok = pe(lambda e, s=s, b=b: e.matmul(PS[:, b, 256:320], ones, OHS[:, s, :], start=(s == 0), stop=(s == 3)))
    tok_pos = tok
    t6 = dve(lambda e, b=b: e.tensor_copy(POS, PS[:, b, 0:256].rearrange("p (a b) -> p a b", a=4)), tok)
    CNTF = CBM[:, 188:254]
    t_cnt = dve(lambda e, b=b: e.tensor_copy(CNTF[:, 0:64], PS[:, b, 256:320]), tok)
    bank_free[b] = [t6, t_cnt]
    NB, INC, VV = (A[:, 10608 + 64 * i:10672 + 64 * i] for i in range(3))
    CNT = CNTF[:, 0:64]
    t9 = dve(lambda e: e.tensor_scalar(NB, CNT, float(BLK), None, ALU.is_gt), t_cnt, mix_done)
    for k in range(2, T // BLK):
        t9 = dve(lambda e, k=k: e.scalar_tensor_tensor(NB, CNT, float(BLK * k), NB, ALU.is_gt, ALU.add), t9)
    t9 = dve(lambda e: e.tensor_tensor_scan(INC, ones[:, 0:64], NB, 0.0, ALU.mult, ALU.add), t9)
    t10 = dve(lambda e: e.tensor_tensor(VV, INC, NB, ALU.subtract), t9)
    t10 = dve(lambda e: e.tensor_tensor(VV, VV, C("iota64"), ALU.subtract), t10)
    t_v = dve(lambda e: e.tensor_scalar(VV, VV, float(BLK), float(MAIN - BLK), ALU.mult, ALU.add), t10)
    t11 = dve(lambda e: e.tensor_scalar(NB, INC, C("tok")[:, 0:1], None, ALU.is_le), t10)
    t11 = dve(lambda e: e.tensor_reduce(KEEP[:, 24:25], NB, AX, ALU.add), t11, t_wk)
    b = bank()
    tok = pe(lambda e, b=b: e.matmul(PS[0:1, b, 0:OVER], KEEP[:, 24:25], ident[:, 0:OVER], start=True, stop=True), t11, bank_free[b])
    OVI = CBM[0:1, 124:141].bitcast(I32)
    t11 = dve(lambda e, b=b: e.tensor_copy(OVI[:, 0:OVER], PS[0:1, b, 0:OVER]), tok)
    bank_free[b] = [t11]
    t_ovi = dve(lambda e: e.tensor_copy(OVI[:, OVER:OVER + 1], INC[0:1, 63:64]), t11)
    vb = VV.rearrange("p (a b) -> p a b", a=1).broadcast_to([128, 4, 64])
    for i in range(2):
        t6 = dve(lambda e, i=i: e.tensor_tensor(OHS, OH[i], POS, ALU.mult), t6, tok_pos)
        t6 = dve(lambda e: e.tensor_reduce(tmp1, OHS, AX, ALU.add), t6)
        t6 = dve(lambda e, i=i: e.tensor_tensor(msel, OH[i], vb, ALU.mult), t6, t_v)
        t6 = dve(lambda e: e.tensor_reduce(tmp2, msel, AX, ALU.add), t6)
        t6 = dve(lambda e: e.scalar_tensor_tensor(tmp2, tmp1, float(BLK), tmp2, ALU.is_ge, ALU.mult), t6)
        t6 = dve(lambda e: e.tensor_tensor(tmp2, tmp2, tmp1, ALU.add), t6)
        t6 = dve(lambda e, i=i: e.scalar_tensor_tensor(tmp2, eidx[:, :, i:i + 1], float(BLK), tmp2, ALU.mult, ALU.add), t6)
        t_slot = dve(lambda e, i=i: e.tensor_copy(SLOTU[:, 4 * i:4 * i + 4].rearrange("p (a b) -> p a b", b=1), tmp2), t6)
        t6 = t_slot
    t7 = dve(lambda e: e.tensor_copy(TOKU[:, :], C("tok")), t_const)
    for i in range(2):
        for tt in range(4):
            t_sc = pool.dma(dsem("scat"), lambda e, i=i, tt=tt: e.indirect_dma_start(a["list_d"], bass.IndirectOffsetOnAxis(ap=SLOTU[:, 4 * i + tt:4 * i + tt + 1], axis=0),
                                                                           TOKU[:, tt:tt + 1], None), t_zl, t_slot, t7)
    ld = a["list_d"][0:MAIN, :].rearrange("(q s j) o -> s j (q o)", s=2, j=BLK)
    for s in range(2):
        t_list = pool.dma(dsem("list"), lambda e, s=s: e.dma_start(LIST[64 * s:64 * s + 64, :], ld[s], allow_slow_non_contiguous=True), t_sc)
    if stop == "route":
        return done(pe, act, dve, pool, sp, counters)

    route_done = [t_list, t_slot, t_ovi, t_wk] + dense_done + t_n2ds
    for i in range(4):
        extra_slots[i].free = dense_done + ([t_h2t] if i == 0 else [])
    extra_slots[4].free = t_n2ds + dense_done
    for s in extra_slots[::-1]:
        ring.appendleft(s)
    XG = [A[:, 1024 * i:1024 * (i + 1)] for i in range(2)]
    XT = [view(2048 + 1024 * i, 8, 128) for i in range(2)]
    H13 = [A[:, 8192 + 512 * i:8192 + 512 * (i + 1)] for i in range(2)]
    YO = [A[:, 9216 + 512 * i:9216 + 512 * (i + 1)] for i in range(2)]
    HT = [view(10240 + 256 * i, 4, 64) for i in range(2)]
    SL = [view(10752 + 256 * i, 4, 64) for i in range(2)]
    xg_free, xt_free, h13_free, yo_free, ht_free = ([route_done, route_done] for _ in range(5))
    t_xt = {}

    def m_gather(q):
        i = q % 2
        t = pool.dma(dsem(f"xg{i}"), lambda e: e.indirect_dma_start(XG[i], None, a["n2_d"], bass.IndirectOffsetOnAxis(ap=LIST[:, q:q + 1], axis=0)),
                     xg_free[i], t_n2ds)
        for half in range(2):
            b = bank()
            for j in range(4):
                k = 4 * half + j
                tok = pe(lambda e, b=b, j=j, k=k: e.transpose(PS[:, b, j * 128:(j + 1) * 128], XG[i][:, k * 128:(k + 1) * 128], ident), t, bank_free[b], inc=(j == 3))
            fn = lambda e, b=b, half=half: e.tensor_copy(XT[i][:, 4 * half:4 * half + 4, :], PS[:, b, :].rearrange("p (a b) -> p a b", a=4))
            t_ = dve(fn, tok, xt_free[i])
            bank_free[b] = [t_]
        xg_free[i] = [tok]
        t_xt[q] = t_

    hst, tst = {}, {}
    w2s = {}

    def m_h(ex):
        q, s = divmod(ex, 2)
        i = q % 2
        sl1, tw1, w1_ = fetch_w(a["w1"][ex], 0)
        sl3, tw3, w3_ = fetch_w(a["w3"][ex], 0)
        sl2, tw2 = fetch((0, (4, D), a["w2"][ex].rearrange("(k p) n -> p k n", p=128)))
        w2s[ex] = (sl2, tw2, sl2.ap.rearrange("p (k n) -> p k n", k=4))
        b = bank()
        for k in range(8):
            for hh, w, tw in ((0, w1_, tw1), (1, w3_, tw3)):
                tok = pe(lambda e, k=k, hh=hh, w=w, b=b: e.matmul(PS[64 * hh:64 * hh + 64, b, :], XT[i][:, k, 64 * s:64 * s + 64], w[:, k, :], start=(k == 0), stop=(k == 7)),
                         tw, t_xt[q], bank_free[b] if k == 0 and hh == 0 else None, inc=(k == 7 and hh == 1))
        sl1.free, sl3.free = [tok], [tok]
        if s == 1:
            xt_free[i] = [tok]
        p = ex % 2
        t = act(lambda e: e.activation(H13[p], PS[:, b, :], ACT.Copy), tok, h13_free[p])
        bank_free[b] = [t]
        hst[ex] = t

    def m_t(ex):
        p = ex % 2
        b = bank()
        for j in range(4):
            tok = pe(lambda e, j=j: e.transpose(PS[:, b, j * 128:(j + 1) * 128], H13[p][:, j * 128:(j + 1) * 128], ident), hst[ex], bank_free[b], inc=(j == 3))
        h13_free[p] = [tok]
        pv = PS[:, b, :].rearrange("p (a b) -> p a b", a=4)
        t = act(lambda e: e.activation(SL[p], pv[:, :, 0:64], ACT.Silu), tok, ht_free[p])
        t = dve(lambda e: e.tensor_tensor(HT[p], SL[p], pv[:, :, 64:128], ALU.mult), t, tok)
        bank_free[b] = [t]
        tst[ex] = t

    def m_y(ex):
        p = ex % 2
        sl2, tw2, w2_ = w2s[ex]
        b = bank()
        for k in range(4):
            for hh in range(2):
                tok = pe(lambda e, k=k, hh=hh: e.matmul(PS[64 * hh:64 * hh + 64, b, :], HT[p][:, k, :], w2_[:, k, 512 * hh:512 * hh + 512], start=(k == 0), stop=(k == 3)),
                         tw2, tst[ex], bank_free[b] if k == 0 and hh == 0 else None, inc=(k == 3 and hh == 1))
        sl2.free = [tok]
        ht_free[p] = [tok]
        t = dve(lambda e: e.tensor_copy(YO[p], PS[:, b, :]), tok, yo_free[p])
        bank_free[b] = [t]
        for hh in range(2):
            t_ = act.dma(dsem(f"yo{p}"), lambda e, hh=hh: e.dma_start(a["y_d"][BLK * ex:BLK * ex + BLK, 512 * hh:512 * hh + 512], YO[p][64 * hh:64 * hh + 64, :]), t)
        yo_free[p] = [t_]

    nx = 4 if stop == "moe4" else NE
    for n in range(nx + 2):
        if n < nx:
            if n == 0:
                m_gather(0)
            if n % 2 == 0 and n + 2 < nx:
                m_gather(n // 2 + 1)
            m_h(n)
        if 1 <= n <= nx:
            m_t(n - 1)
        if n >= 2:
            m_y(n - 2)
    if stop == "moe4":
        return done(pe, act, dve, pool, sp, counters)

    o_ = {n: sem_of("o_" + n) for n in ("load", "gather", "xt", "xtc", "h", "hc", "ht", "silu", "mul", "y", "yc", "store", "end", "pad")}
    moe_done = [(pe.sem, pe.count), (dve.sem, dve.count), (act.sem, act.count)] + [tuple(dsem(f"yo{p}")) for p in range(2)]
    OW = [A[:, 11264 + WC * i:11264 + WC * (i + 1)] for i in range(3)]
    o1, o3 = (w.rearrange("p (k n) -> p k n", k=8) for w in OW[0:2])
    o2 = OW[2].rearrange("p (k n) -> p k n", k=4)
    LX = CBM[0:BLK, 142:143].bitcast(U32)
    OXG, OXT, OH13, OSL, OHT, OYO = XG[0][0:BLK, :], view(2048, 8, BLK), H13[0], SL[0], HT[0], YO[0]

    def blocks(e, body):
        e.wait_ge(t_ovi[0], t_ovi[1])
        n = e.value_load(OVI[0:1, OVER:OVER + 1], min_val=0, max_val=OVER - 1)
        i = e.alloc_register()
        e.reg_mov(i, 0)
        with e.While(lambda: e.snap(i, min_val=0, max_val=OVER - 1) < n):
            at = e.snap(i, min_val=0, max_val=OVER - 2)
            body(at, at + 1)
            e.reg_add(i, i, 1)
        e.drain().then_inc(o_["end"], 1)

    def await_block(e, sem, value):
        e.wait_ge(sem, value)
        e.sem_inc(o_["pad"], 1)

    def o_sp(e):
        def body(at, done):
            await_block(e, o_["store"], done * 32)
            ex = e.value_load(OVI[0:1, bass.ds(at, 1)], min_val=0, max_val=NE - 1)
            for dst, w, k in ((o1, a["w1"], 8), (o3, a["w3"], 8), (o2, a["w2"], 4)):
                src = w.rearrange("x (k p) n -> x p k n", p=128)[bass.ds(ex, 1)].rearrange("x p k n -> (x p) k n")
                e.dma_start(dst, src).then_inc(o_["load"], 16)
            e.dma_start(LX, a["list_d"][MAIN:ROWS, :].rearrange("(x j) o -> x j o", j=BLK)[bass.ds(at, 1)].rearrange("x j o -> (x j) o")).then_inc(o_["load"], 16)
        for sem, v in moe_done:
            e.wait_ge(sem, v)
        e.sem_inc(o_["store"], 32)
        blocks(e, body)

    def o_pool(e):
        def body(at, done):
            await_block(e, o_["load"], done * 64)
            e.indirect_dma_start(OXG, None, a["n2_d"], bass.IndirectOffsetOnAxis(ap=LX, axis=0)).then_inc(o_["gather"], 16)
        blocks(e, body)

    def o_pe(e):
        def body(at, done):
            await_block(e, o_["gather"], done * 16)
            for k in range(8):
                m = e.transpose(PS[:, 0, k * BLK:(k + 1) * BLK], OXG[:, k * 128:(k + 1) * 128], C("ident", 0, BLK)[:, 0:BLK])
            m.then_inc(o_["xt"], 1)
            await_block(e, o_["xtc"], done)
            await_block(e, o_["load"], done * 64)
            for k in range(8):
                for hh, w in ((0, o1), (1, o3)):
                    m = e.matmul(PS[64 * hh:64 * hh + 64, 1, :], OXT[:, k, :], w[:, k, :], start=(k == 0), stop=(k == 7))
            m.then_inc(o_["h"], 1)
            await_block(e, o_["hc"], done)
            for j in range(4):
                m = e.transpose(PS[:, 2, j * 128:(j + 1) * 128], OH13[:, j * 128:(j + 1) * 128], ident)
            m.then_inc(o_["ht"], 1)
            await_block(e, o_["mul"], done)
            for k in range(4):
                for hh in range(2):
                    m = e.matmul(PS[64 * hh:64 * hh + 64, 3, :], OHT[:, k, :], o2[:, k, 512 * hh:512 * hh + 512], start=(k == 0), stop=(k == 3))
            m.then_inc(o_["y"], 1)
        blocks(e, body)

    def o_act(e):
        def body(at, done):
            await_block(e, o_["h"], done)
            e.activation(OH13, PS[:, 1, :], ACT.Copy).then_inc(o_["hc"], 1)
            await_block(e, o_["ht"], done)
            e.activation(OSL, PS[:, 2, :].rearrange("p (a b) -> p a b", a=4)[:, :, 0:64], ACT.Silu).then_inc(o_["silu"], 1)
            await_block(e, o_["yc"], done)
            rows = a["y_d"][MAIN:ROWS, :].rearrange("(x j) n -> x j n", j=BLK)[bass.ds(at, 1)].rearrange("x j n -> (x j) n")
            for hh in range(2):
                e.dma_start(rows[:, 512 * hh:512 * hh + 512], OYO[64 * hh:64 * hh + 64, :]).then_inc(o_["store"], 16)
        blocks(e, body)

    def o_dve(e):
        def body(at, done):
            await_block(e, o_["xt"], done)
            e.tensor_copy(OXT, PS[:, 0, :].rearrange("p (a b) -> p a b", a=8)).then_inc(o_["xtc"], 1)
            await_block(e, o_["silu"], done)
            e.tensor_tensor(OHT, OSL, PS[:, 2, :].rearrange("p (a b) -> p a b", a=4)[:, :, 64:128], ALU.mult).then_inc(o_["mul"], 1)
            await_block(e, o_["y"], done)
            e.tensor_copy(OYO, PS[:, 3, :]).then_inc(o_["yc"], 1)
        blocks(e, body)

    for q, fn in ((sp, o_sp), (pool, o_pool), (pe, o_pe), (act, o_act), (dve, o_dve)):
        q.raw(fn)
    over_done = [(o_["end"], 5)]
    def last_store(e):
        n = e.value_load(OVI[0:1, OVER:OVER + 1], min_val=0, max_val=OVER - 1)
        e.wait_ge(o_["store"], (n + 1) * 32)
        e.sem_inc(o_["end"], 1)
    sp.raw(last_store)
    over_done = [(o_["end"], 6)]

    G2 = A[:, 0:1024]
    FG = A[:, 1024:2048]
    GC = KEEP[:, 8:16]
    t = dve(lambda e: e.tensor_copy(GC, MOD[:, 40:48]), ada["tok"])
    t = act.dma(dsem("g2"), lambda e: e.dma_start(a["g2_d"].rearrange("o (k p) -> p (o k)", p=128), GC, allow_slow_non_contiguous=True), t)
    t_g2 = act.dma(dsem("g2b"), lambda e: e.dma_start(G2, a["g2_d"].broadcast_to([128, D])), t, over_done)
    t_fg = act.dma(dsem("fg"), lambda e: e.dma_start(FG, a["final_g"].broadcast_to([128, D])), over_done)
    Y = [[A[:, 11264 + 2048 * tt + 1024 * i:11264 + 2048 * tt + 1024 * (i + 1)] for i in range(2)] for tt in range(4)]
    OUT = [A[:, 20480 + 1024 * tt:20480 + 1024 * (tt + 1)] for tt in range(4)]
    SS = KEEP[:, 16:20]
    for tt in range(4):
        for i in range(2):
            ty = pool.dma(dsem(f"fy{tt}"), lambda e, tt=tt, i=i: e.indirect_dma_start(Y[tt][i], None, a["y_d"], bass.IndirectOffsetOnAxis(ap=SLOTU[:, 4 * i + tt:4 * i + tt + 1], axis=0)),
                          over_done)
        y0, y1, o = Y[tt][0], Y[tt][1], OUT[tt]
        hrow = h2t[:, tt, :]
        t = act(lambda e, y0=y0, tt=tt: e.activation(y0, y0, ACT.Copy, scale=KEEP[:, tt:tt + 1]), ty, t_wk)
        t = dve(lambda e, y0=y0, y1=y1, tt=tt: e.scalar_tensor_tensor(y0, y1, KEEP[:, 4 + tt:5 + tt], y0, ALU.mult, ALU.add), t, ty)
        t = dve(lambda e, y0=y0: e.tensor_tensor(y0, y0, G2, ALU.mult), t, t_g2)
        t = dve(lambda e, y0=y0, hrow=hrow: e.tensor_tensor(y0, y0, hrow, ALU.add), t, t_h2t)
        ts = act(lambda e, y0=y0, y1=y1, tt=tt: e.activation(y1, y0, ACT.Square, accum_out=SS[:, tt:tt + 1]), t)
        ts = act(lambda e, tt=tt: e.activation(SS[:, tt:tt + 1], SS[:, tt:tt + 1], ACT.Sqrt, scale=1.0 / D, bias=C("eps")), ts)
        ts = dve(lambda e, tt=tt: e.reciprocal(SS[:, tt:tt + 1], SS[:, tt:tt + 1]), ts)
        t = dve(lambda e, y0=y0, o=o, tt=tt: e.scalar_tensor_tensor(o, y0, SS[:, tt:tt + 1], FG, ALU.mult, ALU.mult), ts, t, t_fg)
        sp.dma(dsem("out"), lambda e, tt=tt, o=o: e.dma_start(a["out"][tt * 128:(tt + 1) * 128, :], o), t)
    return done(pe, act, dve, pool, sp, counters)


def done(pe, act, dve, pool, sp, counters):
    sp.wait(*[(c[0], c[1]) for c in counters.values()])
    sp.wait((pe.sem, pe.count), (act.sem, act.count), (dve.sem, dve.count), (pool.sem, pool.count))


def shape_constants():
    i = np.arange(128)
    c = np.zeros((128, CN), np.float32)

    def put(name, x):
        at, n = CO[name]
        c[:, at:at + n] = x

    put("ident", np.eye(128))
    put("ones", 1.0)
    put("bones", (i[:, None] // 64 == i[None] // 64))
    put("ustrict", i[:, None] < i[None])
    put("cmask", np.where(i[None] <= i[:, None], 0.0, -1e30))
    put("smask", i[None] >= i[:, None])
    put("iota8", np.arange(8)[None])
    put("iota64", np.arange(64)[None])
    put("tok", i[:, None] + 128 * np.arange(4)[None])
    put("eps", EPS)
    put("sel4", (i[:, None] % 32 == 0))
    return c


def lay_params(x):
    p = np.zeros((128, PN), np.float32)

    def put(name, v, rows=128):
        at, n = PO[name]
        p[:rows, at:at + n] = v

    col = lambda v: np.asarray(v).reshape(-1, 128).T
    put("attn_norm", col(x["attn_norm"]))
    put("ffn_norm", col(x["ffn_norm"]))
    put("final_norm", col(x["final_norm"]))
    put("qg", np.tile(x["fox_q_norm"][0], 2)[:, None])
    put("kg", np.tile(x["fox_k_norm"][0], 2)[:, None])
    put("bf", x["fox_b_f"][0][:, None], 16)
    put("norm1", col(x["norm1_g_2"]))
    put("cvw", x["cv_dw_w_2"][0].T.reshape(8, 128, 31).transpose(1, 0, 2).reshape(128, 248))
    put("cvb", col(x["cv_dw_b_2"]))
    put("lng", col(x["cv_ln_g_2"]))
    put("lnb", col(x["cv_ln_b_2"]))
    put("scw", x["ssm_conv_w_2"][0].T.reshape(24, 128, 4).transpose(1, 0, 2).reshape(128, 96))
    put("scb", col(x["ssm_conv_b_2"]))
    put("dtb", x["dt_bias_2"][0][:, None], 32)
    put("alog", x["a_log_2"][0][:, None], 32)
    put("dsk", np.repeat(x["d_skip_2"][0].reshape(16, 2).T, 64, axis=0))
    put("sng", col(x["ssm_norm_g_2"]))
    put("norm2", col(x["norm2_g_2"]))
    put("c", col(x["c_2"]))
    put("bada", col(x["b_ada_2"]))
    put("rb", np.broadcast_to(np.concatenate([x["b_grp_2"][0], x["b_er_2"][0]])[None], (128, 72)))
    put("wf", x["fox_w_in"][0][:, 4096:4112].reshape(8, 128, 16).transpose(1, 0, 2).reshape(128, 128))
    put("wdt", x["w_in_2"][0][:, 7168:7200].reshape(8, 128, 32).transpose(1, 0, 2).reshape(128, 256))
    return p


def arrays(x):
    xt = np.concatenate([x["meta_tokens"], x["x"][0]], axis=0)
    return {
        "consts": shape_constants(),
        "params": lay_params(x),
        "xT": np.ascontiguousarray(xt.T.reshape(8, 128, L).transpose(1, 0, 2)),
        "rw": np.ascontiguousarray(np.concatenate([x["w_grp_2"][0], x["w_er_2"][0]], axis=1).reshape(8, 128, 72).transpose(1, 0, 2)),
        "fox_w_in": x["fox_w_in"][0], "fox_w_out": x["fox_w_out"][0], "ffn_w_in": x["ffn_w_in"][0], "ffn_w_out": x["ffn_w_out"][0],
        "w_ada": x["w_ada_2"][0], "w_in": x["w_in_2"][0], "w_cv_out": x["w_cv_out_2"][0], "w_ssm_out": x["w_ssm_out_2"][0],
        "w_mix_out": x["w_mix_out_2"][0], "w1": x["w1_2"][0], "w3": x["w3_2"][0], "w2": x["w2_2"][0],
        "final_g": x["final_g_2"].reshape(1, D),
    }


def declare(nc, arr):
    a = {k: nc.dram_tensor("in_" + k, v.shape, mybir.dt.from_np(v.dtype), kind="ExternalInput").ap() for k, v in arr.items()}
    a["out"] = nc.dram_tensor("out_0", (T, D), F32, kind="ExternalOutput").ap()
    for name, shape, dt in (("x2_d", (128, 8, T), F32), ("ymix_d", (128, 8, T), F32), ("n2_d", (T, D), F32), ("g2_d", (1, D), F32),
                            ("list_d", (ROWS, 1), U32), ("y_d", (ROWS, D), F32)):
        a[name] = nc.dram_tensor(name, shape, dt).ap()
    return a


def kernel(**inputs):
    from concourse import bacc
    from concourse.bass_utils import run_bass_kernel_spmd

    arr = {k: np.ascontiguousarray(v) for k, v in arrays({k: np.asarray(v) for k, v in inputs.items()}).items()}
    nc = bacc.Bacc("TRN2", target_bir_lowering=False, num_devices=1)
    a = declare(nc, arr)
    build_program(nc, a)
    r = run_bass_kernel_spmd(nc, [{"in_" + k: v for k, v in arr.items()}], core_ids=[0])
    return r.results[0]["out_0"].reshape(1, T, D)
```

```python
from collections import deque
from contextlib import ExitStack

import numpy as np
import concourse.bass as bass
from concourse import mybir

F32 = mybir.dt.float32
U32 = mybir.dt.uint32
I32 = mybir.dt.int32
F32R = mybir.dt.float32r
ALU = mybir.AluOpType
ACT = mybir.ActivationFunctionType
AX = mybir.AxisListType.X

T = 512
NM = 16
L = T + NM
D = 1024
FH = 2816
EPS = 1e-6
NE = 64
BLK = 64
MAIN = NE * BLK
OVER = 16
ROWS = MAIN + OVER * BLK
WC = 4096

CONST_COLS = [("ident", 128), ("ones", 128), ("bones", 128), ("ustrict", 128), ("cmask", 128), ("smask", 128),
              ("iota8", 8), ("iota64", 64), ("tok", 4), ("eps", 1), ("sel4", 1), ("sel16", 16)]
PARAM_COLS = [("attn_norm", 8), ("ffn_norm", 8), ("final_norm", 8), ("qg", 1), ("kg", 1), ("bf", 1), ("norm1", 8),
              ("cvw", 248), ("cvb", 8), ("lng", 8), ("lnb", 8), ("scw", 96), ("scb", 24), ("dtb", 1), ("alog", 1),
              ("dsk", 16), ("sng", 16), ("norm2", 8), ("c", 8), ("bada", 48), ("rb", 72), ("wf", 128), ("wdt", 256)]


PARTS_AT = [(4224, 4096), (25984, 4096), (17792, 4096), (8320, 4096), (12416, 6144), (18560, 6144), (0, 4096), (4096, 4096), (8192, 4096), (12528, 4096), (12288, 4096), (28672, 4096), (16384, 4096), (24576, 4096)]


def offsets(cols):
    out, at = {}, 0
    for name, n in cols:
        out[name] = (at, n)
        at += n
    return out, at


CO, CN = offsets(CONST_COLS)
PO, PN = offsets(PARAM_COLS)


class Queue:

    def __init__(self, engine, sem):
        self.engine, self.sem, self.count, self.seen = engine, sem, 0, {}

    def wait(self, *toks):
        for tok in toks:
            if tok is None:
                continue
            if isinstance(tok, list):
                self.wait(*tok)
                continue
            sem, value = tok
            if self.seen.get(id(sem), 0) < value:
                self.seen[id(sem)] = value
                if self.engine is not None:
                    self.engine.wait_ge(sem, value)

    def __call__(self, fn, *toks, inc=True):
        self.wait(*toks)
        self.count += inc
        if self.engine is not None:
            ins = fn(self.engine)
            if inc:
                ins.then_inc(self.sem, 1)
        return (self.sem, self.count)

    def raw(self, fn):
        if self.engine is not None:
            fn(self.engine)

    def dma(self, counter, fn, *toks):
        self.wait(*toks)
        counter[1] += 16
        if self.engine is not None:
            fn(self.engine).then_inc(counter[0], 16)
        return (counter[0], counter[1])


def build_program(nc, a, stop=None):
    with ExitStack() as ctx:
        made = {}

        def tensor(name, shape, dt=F32):
            if name not in made:
                made[name] = ctx.enter_context(nc.sbuf_tensor(name, shape, dt))
            return made[name]

        def semaphore(name):
            if name not in made:
                made[name] = ctx.enter_context(nc.semaphore(name))
            return made[name]

        for name, off, n in [(f"r{off}", off, n) for off, n in PARTS_AT] + [("ring_r", 32768 + 2 * WC, 2 * WC)]:
            with ExitStack() as under:
                if off:
                    under.enter_context(nc.sbuf_tensor("before_" + name, [128, off], F32))
                made[name] = under.enter_context(nc.sbuf_tensor(name, [128, n], F32R))
        PS = ctx.enter_context(nc.psum_tensor("ps", [128, 8, 512], F32))
        program(a, tensor, semaphore, PS, {}, stop)
        block = ctx.enter_context(nc.Block())

        @block.sync
        def _(e):
            program(a, tensor, semaphore, PS, {"sp": e}, stop)

        @block.tensor
        def _(e):
            program(a, tensor, semaphore, PS, {"pe": e}, stop)

        @block.scalar
        def _(e):
            program(a, tensor, semaphore, PS, {"act": e}, stop)

        @block.vector
        def _(e):
            program(a, tensor, semaphore, PS, {"dve": e}, stop)

        @block.gpsimd
        def _(e):
            program(a, tensor, semaphore, PS, {"pool": e}, stop)


def program(a, sb, sem_of, PS, engines, stop):
    pe, act, dve, pool, sp = (Queue(engines.get(n), sem_of(f"s_{n}")) for n in ("pe", "act", "dve", "pool", "sp"))
    counters = {}

    def dsem(name):
        if name not in counters:
            counters[name] = [sem_of("d_" + name), 0]
        return counters[name]

    A = sb("arena", [128, 32768])
    RG = sb("ring", [128, 4 * WC])
    CS = sb("consts_sb", [128, CN])
    PR = sb("params_sb", [128, PN])
    SCR = sb("scr", [128, 1640])
    CBM = sb("cbm", [128, 512])
    RR = sb("ring_r", None)
    PSF = PS[:, :, :].rearrange("p a b -> p (a b)")

    def C(name, r0=0, r1=128):
        at, n = CO[name]
        return CS[r0:r1, at:at + n]

    def P(name, r0=0, r1=128):
        at, n = PO[name]
        return PR[r0:r1, at:at + n]

    def pc(name, k, r0=0, r1=128):
        at, n = PO[name]
        return PR[r0:r1, at + k:at + k + 1]

    def parts_at(off, n):
        return sb(f"r{off}", None)[:, :].rearrange("p (a b) -> p a b", a=n)

    def view(off, *dims):
        n = int(np.prod(dims))
        v = A[:, off:off + n]
        if len(dims) == 2:
            v = v.rearrange("p (a b) -> p a b", a=dims[0])
        if len(dims) == 3:
            v = v.rearrange("p (a b c) -> p a b c", a=dims[0], b=dims[1])
        return v

    ident, ones, bones = C("ident"), C("ones"), C("bones")

    class Slot:
        def __init__(self, ap, name):
            self.ap, self.free, self.counter, self.busy = ap, [], dsem(name), False

    ring = deque(Slot(RG[:, i * WC:(i + 1) * WC], f"w{i}") for i in range(2))

    def fetch(*parts):
        slot = ring.popleft()
        assert not slot.busy
        ring.append(slot)
        tok = None
        for off, shape, src in parts:
            n = int(np.prod(shape))
            dst = slot.ap[:, off:off + n].rearrange("p (a b) -> p a b", a=shape[0])
            tok = sp.dma(slot.counter, lambda e, dst=dst, src=src: e.dma_start(dst, src), slot.free)
        slot.free = []
        return slot, tok

    def wrows(w, r0, nk, c0, nc_):
        return w[r0:r0 + nk * 128, c0:c0 + nc_].rearrange("(k p) n -> p k n", p=128)

    def fetch_w(w, c0, ncol=512, r0=0, nk=8):
        slot, tok = fetch((0, (nk, ncol), wrows(w, r0, nk, c0, ncol)))
        return slot, tok, slot.ap[:, :nk * ncol].rearrange("p (k n) -> p k n", k=nk)

    class Gran:
        def __init__(self, i):
            o = 2048 * i
            self.H, self.L, self.free = RR[:, o:o + 1024], RR[:, o + 1024:o + 2048], []

    grans, plan, ready = deque(Gran(i) for i in range(4)), deque(), deque()
    chunk = {"slot": None, "tok": None, "todo": deque()}

    def split(hi, lo, x, *toks):
        t = act(lambda e: e.activation(hi, x, ACT.Copy), *toks)
        return pool(lambda e: e.tensor_tensor(lo, x, hi.bitcast(F32), ALU.subtract), t, *toks)

    def feed():
        while len(ready) < 4 and (plan or chunk["todo"]):
            if not chunk["todo"]:
                parts, views = plan.popleft()
                chunk["slot"], chunk["tok"] = fetch(*parts) if parts else (None, t_param)
                if parts:
                    chunk["slot"].busy = True
                chunk["todo"] = deque(views)
            raw = chunk["todo"].popleft()
            slot = chunk["slot"]
            if slot is not None:
                raw = raw(slot.ap)
            g = grans.popleft()
            grans.append(g)
            _, nk, n = raw.shape
            H, L = (x[:, :nk * n].rearrange("p (k n) -> p k n", k=nk) for x in (g.H, g.L))
            t = split(H, L, raw, chunk["tok"], g.free)
            if slot is not None and not chunk["todo"]:
                slot.free.append(t)
                slot.busy = False
            ready.append((g, H, L, t, slot, chunk["tok"]))

    def gran():
        feed()
        return ready.popleft()

    def plan_w(w, c0, r0=0, nk=8):
        plan.append(([(0, (nk, 512), wrows(w, r0, nk, c0, 512))],
                     [lambda ap, j=j: ap[:, :nk * 512].rearrange("p (k n) -> p k n", k=nk)[:, :, j * 128:(j + 1) * 128] for j in range(4)]))

    def plan_two(w, c0, c1):
        plan.append(([(2048 * i, (8, 256), wrows(w, 0, 8, c, 256)) for i, c in enumerate((c0, c1))],
                     [lambda ap, j=j, i=i: ap.rearrange("p (g k n) -> p g k n", g=2, k=8)[:, i, :, j * 128:(j + 1) * 128] for j in range(2) for i in range(2)]))

    fw, wi = a["fox_w_in"], a["w_in"]
    for c in range(2):
        plan_w(fw, 1024 + 512 * c)
    for c in range(2):
        plan.append(([(0, (8, 512), wrows(fw, 0, 8, 2048 + 512 * c, 512))],
                     [lambda ap, j=j: ap.rearrange("p (k n) -> p k n", k=8)[:, 2 * j:2 * j + 2, :] for j in range(4)]))
    plan.append((None, [P("wf").rearrange("p (k n) -> p k n", k=8)]))
    for c in range(2):
        plan_w(fw, 512 * c)
    for c in range(2):
        plan_w(fw, 3072 + 512 * c)
    for c in range(2):
        plan_w(a["fox_w_out"], 512 * c)
    HALVES = [(0, 12), (12, 10)]
    for k0, n in HALVES:
        for nt in range(k0, k0 + n, 2):
            plan_two(a["ffn_w_in"], 128 * nt, FH + 128 * nt)
        for c in range(2):
            plan_w(a["ffn_w_out"], 512 * c, r0=128 * k0)
            plan_w(a["ffn_w_out"], 512 * c, r0=128 * (k0 + 8), nk=n - 8)
    for c in range(4):
        plan_two(wi, 1024 + 256 * c, 256 * c)
    for c in range(2):
        plan_w(wi, 6144 + 512 * c)
    plan.append((None, [P("wdt").rearrange("p (k n) -> p k n", k=8)]))
    for c in range(2):
        plan_w(wi, 7200 + 512 * c)
        plan_w(a["w_cv_out"], 512 * c)
    for g_ in range(4):
        plan_w(wi, 4096 + 512 * g_)
        plan_w(wi, 2048 + 512 * g_)
    for c in range(2):
        plan_w(wi, 8224 + 512 * c)
    for c in range(2):
        plan_w(a["w_ssm_out"], 512 * c)
        plan_w(a["w_ssm_out"], 512 * c, r0=1024)
    for c in range(2):
        plan_w(a["w_mix_out"], 512 * c)

    def mm3(out, g, X, toks, start=True, stop=True, k0=0):
        _, WH, WL, tw = g[:4]
        nk = WH.shape[1]
        tok = None
        for k in range(nk):
            XH, XL, tx = X(k0 + k)
            for i, (w, x) in enumerate(((WH, XH), (WH, XL), (WL, XH))):
                s, e_ = start and k == 0 and i == 0, stop and k == nk - 1 and i == 2
                tok = pe(lambda e, w=w, x=x, k=k, s=s, e_=e_: e.matmul(out, w[:, k, :], x, start=s, stop=e_), tw, tx, toks, inc=(k == nk - 1 and i == 2))
        g[0].free = [tok]
        return tok

    def tile(X, m=128, n=512):
        b = bank()
        return b, mm3(PS[0:m, b, :n], gran(), X, bank_free[b])

    bank_free = [[] for _ in range(8)]
    turn = [0]

    def bank(n=1, among=None):
        if among is None:
            b = turn[0] % 8
            turn[0] += 1
        else:
            b = among[turn[0] % len(among)]
            turn[0] += 1
        return b

    def mms(out, pairs, *toks, start=True, stop=True, inc=True):
        tok = None
        for i, (lt, r) in enumerate(pairs):
            last = i == len(pairs) - 1
            tok = pe(lambda e, lt=lt, r=r, s=(start and i == 0), t=(stop and last): e.matmul(out, lt, r, start=s, stop=t),
                     *(toks if i == 0 else ()), inc=inc and last)
        return tok

    t_const = act.dma(dsem("const"), lambda e: e.dma_start(CS[:, :], a["consts"]))
    t_param = act.dma(dsem("param"), lambda e: e.dma_start(PR[:, :], a["params"]))

    hT = view(0, 8, L)
    hnH, hnL = parts_at(4224, 8), parts_at(25984, 8)
    hnm = CBM[:, 0:256].rearrange("p (a b) -> p a b", a=8)
    kT = view(8448, 8, L)
    v = view(12672, 5, D)
    qT = view(17792, 8, T)
    gT = view(21888, 8, T)
    oH, oL = parts_at(25984, 8), parts_at(17792, 8)
    t_x = act.dma(dsem("x"), lambda e: e.dma_start(hT, a["xT"]))

    ZERO = view(21888, 1, D)[:, 0, :]
    t_zero = pool(lambda e: e.memset(ZERO, 0.0))
    for i in range(OVER * BLK // 128):
        t_zy = pool.dma(dsem("zy"), lambda e, i=i: e.dma_start(a["y_d"][MAIN + 128 * i:MAIN + 128 * i + 128, :], ZERO), t_zero)
    t_zl = pool.dma(dsem("zl"), lambda e: e.dma_start(a["list_d"].rearrange("(p n) o -> p (n o)", p=128), ZERO[:, 0:ROWS // 128].bitcast(U32)), t_zero)

    TMP = [SCR[:, 0:528], SCR[:, 528:1056]]
    RST = SCR[:, 1056:1584]
    tmp_free = [[], []]
    tmp_turn = [0]

    def take_tmp():
        i = tmp_turn[0] % 2
        tmp_turn[0] += 1
        return i, TMP[i], tmp_free[i]

    rst_free = []

    def colsum(src, nk, segs, mat, tok_of, square=True):
        banks = [bank() for _ in segs]
        tok = None
        for k in range(nk):
            if square:
                i, tmp, free = take_tmp()
                n = segs[-1][0] + segs[-1][1]
                s = src(k)
                t_sq = act(lambda e, tmp=tmp, s=s, n=n: e.activation(tmp[:, :n], s, ACT.Square), tok_of(k), free)
                m, ready = tmp, t_sq
            else:
                m, ready = src(k), tok_of(k)
            for b, (s0, n) in zip(banks, segs):
                tok = pe(lambda e, b=b, m=m, s0=s0, n=n, k=k: e.matmul(PS[:, b, :n], mat, m[:, s0:s0 + n], start=(k == 0), stop=(k == nk - 1)),
                         ready, bank_free[b] if k == 0 else None, t_const, inc=True)
            if square:
                tmp_free[i] = [tok]
        return banks, tok

    def rstd(banks, segs, scale, tok, out=None):
        out = RST if out is None else out
        t = None
        for b, (s0, n) in zip(banks, segs):
            t = act(lambda e, b=b, s0=s0, n=n: e.activation(out[:, s0:s0 + n], PS[:, b, :n], ACT.Sqrt, scale=scale, bias=C("eps")),
                    tok, rst_free)
            bank_free[b] = [t]
        n = segs[-1][0] + segs[-1][1]
        return dve(lambda e: e.reciprocal(out[:, :n], out[:, :n]), t)

    def rms_to(dst, src, nk, segs, scale, gain, tok_of, extra=None):
        banks, tok = colsum(src, nk, segs, ones, tok_of)
        t = rstd(banks, segs, scale, tok)
        n = segs[-1][0] + segs[-1][1]
        out = []
        for k in range(nk):
            out.append(dve(lambda e, k=k: e.scalar_tensor_tensor(dst(k), src(k), gain(k), RST[:, :n], ALU.mult, ALU.mult),
                           t, t_param, extra, tok_of(k)))
        rst_free[:] = [out[-1]]
        return out

    SC = SCR[:, 1584:1592]
    MOD = SCR[:, 1592:1640]
    t_sc = act(lambda e: e.activation(SC, P("c"), ACT.Silu), t_param)
    ada = {"n": 0, "tok": None}
    ADAP = view(30080, 1, 512)[:, 0, :]
    ada_free = []

    def ada_step():
        n = ada["n"]
        if n == 12:
            return
        ada["n"] += 1
        slot, tw, w = fetch_w(a["w_ada"], n * 512)
        b = bank()
        tok = None
        for k in range(8):
            g = k % 4
            tok = pe(lambda e, k=k, g=g, w=w, b=b: e.matmul(PS[32 * g:32 * g + 32, b, :], SC[:, k:k + 1].broadcast_to([128, 32]), w[:, k, :],
                                                       start=(k < 4), stop=(k >= 4)),
                     tw, t_sc, bank_free[b] if k == 0 else None, inc=(k == 7))
        slot.free = [tok]
        t = act(lambda e, b=b: e.activation(ADAP, PS[:, b, :], ACT.Copy), tok, ada_free)
        bank_free[b] = [t]
        b2 = bank()
        for j in range(4):
            tok = pe(lambda e, j=j, b2=b2: e.matmul(PS[:, b2, j:j + 1], ADAP[:, j * 128:(j + 1) * 128], C("sel4"), start=True, stop=True),
                     t, bank_free[b2] if j == 0 else None, t_const, inc=(j == 3))
        ada_free[:] = [tok]
        o = PO["bada"][0] + 4 * n
        t = dve(lambda e, b2=b2, n=n, o=o: e.tensor_tensor(MOD[:, 4 * n:4 * n + 4], PS[:, b2, 0:4], PR[:, o:o + 4], ALU.add), tok, t_param)
        bank_free[b2] = [t]
        ada["tok"] = t

    SEGL = [(0, 512), (512, 16)]
    SEGT = [(0, 512)]
    banks, tok = colsum(lambda k: hT[:, k, :], 8, SEGL, ones, lambda k: t_x)
    t = rstd(banks, SEGL, 1.0 / D, tok)
    t_hn = []
    for k in range(8):
        i, tmp, free = take_tmp()
        t1 = dve(lambda e, k=k, tmp=tmp: e.scalar_tensor_tensor(tmp, hT[:, k, :], pc("attn_norm", k), RST, ALU.mult, ALU.mult), t, t_param, free)
        t_hm = dve(lambda e, k=k, tmp=tmp: e.tensor_copy(hnm[:, k, :], tmp[:, 0:32]), t1)
        t_hn.append(split(hnH[:, k, :], hnL[:, k, :], tmp[:, NM:L], t1))
        tmp_free[i] = [t_hn[-1], t_hm]
    rst_free[:] = [t1]
    XN = lambda k: (hnH[:, k, :], hnL[:, k, :], t_hn[k])

    def meta_rows(g):
        slot, tw = g[4:6]
        w = slot.ap.rearrange("p (k n) -> p k n", k=8)
        b = bank()
        for k in range(8):
            r = 32 * (k % 4)
            tok = pe(lambda e, k=k, r=r: e.matmul(PS[r:r + 32, b, :], hnm[:, k, :], w[:, k, :], start=(k < 4), stop=(k >= 4)),
                     tw, t_hm, bank_free[b] if k == 0 else None, inc=(k == 7))
        slot.free.append(tok)
        t = act(lambda e: e.activation(ADAP, PS[:, b, :], ACT.Copy), tok, ada_free)
        bank_free[b] = [t]
        return t

    SEL16 = C("sel16")
    t_kraw = [None] * 8
    for c in range(2):
        feed()
        t_m = meta_rows(ready[0])
        for j in range(4):
            nt = 4 * c + j
            b, tok = tile(XN)
            t = act(lambda e, b=b, nt=nt: e.activation(kT[:, nt, NM:L], PS[:, b, :], ACT.Copy), tok)
            bank_free[b] = [t]
            t_kraw[nt] = t
        b = bank()
        for j in range(4):
            tok = pe(lambda e, b=b, j=j: e.matmul(PS[:, b, 16 * j:16 * j + 16], ADAP[:, j * 128:(j + 1) * 128], SEL16, start=True, stop=True),
                     t_m, bank_free[b], t_const, inc=(j == 3))
        ada_free[:] = [tok]
        t = dve(lambda e, b=b, c=c: e.tensor_copy(kT[:, 4 * c:4 * c + 4, 0:NM], PS[:, b, 0:64].rearrange("p (a b) -> p a b", a=4)), tok)
        bank_free[b] = [t]
        for j in range(4):
            t_kraw[4 * c + j] = [t_kraw[4 * c + j], t]
        ada_step()
    for c in range(2):
        feed()
        t_m = meta_rows(ready[0])
        bs = [bank() for _ in range(4)]
        for kk in range(4):
            g = gran()
            for tt in range(4):
                for k in range(2):
                    kx = 2 * kk + k
                    sl = slice(tt * 128, (tt + 1) * 128)
                    for i, (x, w) in enumerate(((hnH, g[1]), (hnL, g[1]), (hnH, g[2]))):
                        last = kx == 7 and i == 2
                        tok = pe(lambda e, x=x, w=w, k=k, kx=kx, sl=sl, i=i, last=last, b=bs[tt]: e.matmul(PS[:, b, :], x[:, kx, sl], w[:, k, :], start=(kx == 0 and i == 0), stop=last),
                                 g[3], t_hn[kx], bank_free[bs[tt]] if kx == 0 else None, inc=last or (tt == 3 and k == 1 and i == 2))
                if kk == 3:
                    t_v = act(lambda e, b=bs[tt], tt=tt, c=c: e.activation(v[:, 1 + tt, c * 512:(c + 1) * 512], PS[:, b, :], ACT.Copy), tok)
                    bank_free[bs[tt]] = [t_v]
            g[0].free = [tok]
        b = bank()
        tok = pe(lambda e, b=b: e.matmul(PS[0:16, b, :], SEL16, ADAP, start=True, stop=True), t_m, bank_free[b], t_const)
        ada_free[:] = [tok]
        t_vm = dve(lambda e, b=b, c=c: e.tensor_copy(v[0:NM, 0, c * 512:(c + 1) * 512], PS[0:16, b, :]), tok)
        bank_free[b] = [t_vm]
        ada_step()
    t_v = [t_v, t_vm]
    wf = P("wf").rearrange("p (k n) -> p k n", k=8)
    FL = view(30592, 4, L)[0:16]
    t = None
    b = bank()
    g = gran()
    tok = mm3(PS[0:16, b, :], g, XN, bank_free[b])
    t = act(lambda e, b=b: e.activation(FL[:, 0, NM:L], PS[0:16, b, :], ACT.Identity, bias=P("bf", 0, 16)), tok)
    bank_free[b] = [t]
    b = bank()
    tok = mms(PS[0:16, b, :NM], [(wf[:, k, :], hnm[:, k, 0:NM]) for k in range(8)], t_param, t_hm, bank_free[b])
    t = act(lambda e, b=b: e.activation(FL[:, 0, 0:NM], PS[0:16, b, :NM], ACT.Identity, bias=P("bf", 0, 16)), tok)
    bank_free[b] = [t]

    def log1p_exp(z, u, s, q, tok, rows):
        t = dve(lambda e: e.tensor_scalar(u, z, -1.0, None, ALU.mult), tok)
        t = dve(lambda e: e.tensor_tensor(u, u, z, ALU.min), t)
        t = act(lambda e: e.activation(u, u, ACT.Exp), t)
        t = dve(lambda e: e.tensor_scalar(s, u, 2.0, None, ALU.add), t)
        t = dve(lambda e: e.reciprocal(s, s), t)
        t = dve(lambda e: e.tensor_tensor(u, u, s, ALU.mult), t)
        t = dve(lambda e: e.tensor_tensor(s, u, u, ALU.mult), t)
        t = dve(lambda e: e.tensor_scalar(q, s, 1.0 / 17, None, ALU.mult), t)
        for c in (15, 13, 11, 9, 7, 5, 3):
            t = dve(lambda e, c=c: e.scalar_tensor_tensor(q, q, 1.0 / c, s, ALU.add, ALU.mult), t)
        t = dve(lambda e: e.scalar_tensor_tensor(q, q, 1.0, u, ALU.add, ALU.mult), t)
        return dve(lambda e: e.tensor_scalar(q, q, 2.0, None, ALU.mult), t)

    t = log1p_exp(FL[:, 0, :], FL[:, 1, :], FL[:, 2, :], FL[:, 3, :], t, 16)
    t = dve(lambda e: e.scalar_tensor_tensor(FL[:, 1, :], FL[:, 0, :], 0.0, FL[:, 3, :], ALU.min, ALU.subtract), t)
    cT = FL[:, 0, :]
    t_c = dve(lambda e: e.tensor_tensor_scan(cT, C("ones", 0, 16)[:, 0:1].broadcast_to([16, L]), FL[:, 1, :], 0.0, ALU.mult, ALU.add), t)
    CQ = view(32704, 4, 16)
    b = bank()
    for tt in range(4):
        tok = pe(lambda e, tt=tt, b=b: e.transpose(PS[:, b, tt * 16:tt * 16 + 16], cT[:, NM + tt * 128:NM + tt * 128 + 128], C("ident", 0, 16)[:, 0:16]),
                 t_c, bank_free[b], t_const, inc=(tt == 3))
    t_cq = dve(lambda e, b=b: e.tensor_copy(CQ, PS[:, b, 0:64].rearrange("p (a b) -> p a b", a=4)), tok)
    bank_free[b] = [t_cq]
    t_qraw = [None] * 8
    for c in range(2):
        for j in range(4):
            nt = 4 * c + j
            b, tok = tile(XN)
            t = act(lambda e, b=b, nt=nt: e.activation(qT[:, nt, :], PS[:, b, :], ACT.Copy), tok)
            bank_free[b] = [t]
            t_qraw[nt] = t
        ada_step()

    def head_norm(x, nt, n, segs, gain, tok):
        banks, tk = colsum(lambda k: x[:, nt, :], 1, segs, bones, lambda k: tok)
        t = rstd(banks, segs, 1.0 / 64, tk)
        t = dve(lambda e: e.scalar_tensor_tensor(x[:, nt, :], x[:, nt, :], gain, RST[:, :n], ALU.mult, ALU.mult), t, t_param)
        rst_free[:] = [t]
        return t

    t_k = [head_norm(kT, i, L, SEGL, pc("kg", 0), t_kraw[i]) for i in range(8)]
    t_qg = dve(lambda e: e.tensor_scalar(pc("qg", 0), pc("qg", 0), 0.125, None, ALU.mult), t_param)
    t_q = [head_norm(qT, i, T, SEGT, pc("qg", 0), [t_qraw[i], t_qg]) for i in range(8)]
    if stop == "qkv":
        return done(pe, act, dve, pool, sp, counters)

    t_g = [None] * 8
    for c in range(2):
        for j in range(4):
            nt = 4 * c + j
            b, tok = tile(XN)
            t = act(lambda e, b=b, nt=nt: e.activation(gT[:, nt, :], PS[:, b, :], ACT.Sigmoid), tok, t_zy, t_zl)
            bank_free[b] = [t]
            t_g[nt] = t
        ada_step()

    W0 = 4224
    NCK = [A[:, W0 + i * L:W0 + (i + 1) * L] for i in range(2)]
    PB = [A[:, W0 + (2 + i) * L:W0 + (3 + i) * L] for i in range(3)]
    PT = [A[:, W0 + 5 * L + 640 * i:W0 + 5 * L + 640 * (i + 1)] for i in range(2)]
    ST0 = W0 + 5 * L + 1280
    NMX = A[:, ST0:ST0 + 64]
    SUM = A[:, ST0 + 64:ST0 + 128]
    hn_done = (pe.sem, pe.count)
    nck_free = [[hn_done], [hn_done]]
    pb_free = [[hn_done]] * 3
    pt_free = [[hn_done], [hn_done]]
    st = {}
    NCKTOK = [None, None]
    aux = [0]

    def aux_bank():
        b = 4 + aux[0] % 2
        aux[0] += 1
        return b

    def at_s(n):
        h, qt = divmod(n, 4)
        i, off = h // 2, 64 * (h % 2)
        if qt == 0:
            ba = aux_bank()
            sl = C("ident", 0, 16)[:, h:h + 1].broadcast_to([16, 128])
            tok = pe(lambda e: e.matmul(PS[:, ba, :], sl, cT[:, 0:512], start=True, stop=True), bank_free[ba], t_c, t_const)
            u = h % 2
            t1 = act(lambda e: e.activation(NCK[u][:, 0:512], PS[:, ba, :], ACT.Copy, scale=-1.0), tok, nck_free[u])
            bank_free[ba] = [t1]
            ba = aux_bank()
            tok = pe(lambda e, ba=ba: e.matmul(PS[:, ba, 0:16], sl, cT[:, 512:528], start=True, stop=True), bank_free[ba])
            t1 = act(lambda e, ba=ba: e.activation(NCK[u][:, 512:528], PS[:, ba, 0:16], ACT.Copy, scale=-1.0), tok)
            bank_free[ba] = [t1]
            NCKTOK[u] = t1
        pr = (n % 2) * 2
        ln = NM + 128 * (qt + 1)
        q = qT[off:off + 64, i, qt * 128:(qt + 1) * 128]
        m = min(ln, 512)
        tok = pe(lambda e: e.matmul(PS[:, pr, 0:m], q, kT[off:off + 64, i, 0:m], start=True, stop=True),
                 bank_free[pr], bank_free[pr + 1], t_q[i], t_k[i])
        if ln > 512:
            tok = pe(lambda e: e.matmul(PS[:, pr + 1, 0:ln - 512], q, kT[off:off + 64, i, 512:ln], start=True, stop=True))
        pb = PB[n % 3]
        S = PSF[:, pr * 512:pr * 512 + ln]
        u = h % 2
        t = dve(lambda e: e.scalar_tensor_tensor(pb[:, :ln], S, CQ[:, qt, h:h + 1], NCK[u][:, :ln], ALU.add, ALU.add),
                tok, NCKTOK[u], t_cq, pb_free[n % 3])
        bank_free[pr] = [t]
        bank_free[pr + 1] = [t]
        if qt == 3:
            nck_free[u] = [t]
        t = dve(lambda e: e.tensor_tensor(pb[:, ln - 128:ln], pb[:, ln - 128:ln], C("cmask"), ALU.add), t)
        t = dve(lambda e: e.tensor_reduce(NMX[:, n:n + 1], pb[:, :ln], AX, ALU.max, negate=True), t)
        t = act(lambda e: e.activation(pb[:, :ln], pb[:, :ln], ACT.Exp, bias=NMX[:, n:n + 1], accum_out=SUM[:, n:n + 1]), t)
        t = dve(lambda e: e.reciprocal(SUM[:, n:n + 1], SUM[:, n:n + 1]), t)
        st[n] = pool(lambda e: e.tensor_scalar(pb[:, :ln], pb[:, :ln], SUM[:, n:n + 1], 1.0, ALU.mult, ALU.mult), t)

    def at_t(n):
        h, qt = divmod(n, 4)
        ln = NM + 128 * (qt + 1)
        pb, pt = PB[n % 3], PT[n % 2]
        ba = aux_bank()
        mb = 2 * (n % 2) + 1
        for j in range(qt + 1):
            tok = pe(lambda e, j=j: e.transpose(PS[:, ba, j * 128:(j + 1) * 128], pb[:, NM + 128 * j:NM + 128 * (j + 1)], ident),
                     st[n], bank_free[ba], inc=False)
        tok = pe(lambda e: e.transpose(PS[0:NM, mb, 128:256], pb[:, 0:NM], ident), bank_free[mb])
        pb_free[n % 3] = [tok]
        t1 = act(lambda e: e.activation(pt[:, 0:128 * (qt + 1)], PS[:, ba, 0:128 * (qt + 1)], ACT.Copy), tok, pt_free[n % 2])
        t2 = dve(lambda e: e.tensor_copy(pt[0:NM, 512:640], PS[0:NM, mb, 128:256]), tok, pt_free[n % 2])
        bank_free[ba] = [t1]
        bank_free[mb] = bank_free[mb] + [t2]
        st[n] = [t1, t2]

    def at_pv(n):
        h, qt = divmod(n, 4)
        i, off = h // 2, 64 * (h % 2)
        pt = PT[n % 2]
        bo = 6 + i % 2
        out = PS[off:off + 64, bo, qt * 128:(qt + 1) * 128]
        pairs = [(v[0:NM, 0, 64 * h:64 * h + 64], pt[0:NM, 512:640])]
        pairs += [(v[:, 1 + j, 64 * h:64 * h + 64], pt[:, j * 128:(j + 1) * 128]) for j in range(qt + 1)]
        tok = mms(out, pairs, st[n], t_v, bank_free[bo] if h % 2 == 0 and qt == 0 else None)
        pt_free[n % 2] = [tok]
        if h % 2 == 1 and qt == 3:
            t = dve(lambda e: e.tensor_tensor(gT[:, i, :], PS[:, bo, :], gT[:, i, :], ALU.mult), tok, t_g[i])
            bank_free[bo] = [t]
            t_o[i] = split(oH[:, i, :], oL[:, i, :], gT[:, i, :], t)

    t_o = [None] * 8
    for n in range(64 + 2):
        if n < 64:
            at_s(n)
        if n >= 1 and n - 1 < 64:
            at_t(n - 1)
        if n >= 2:
            at_pv(n - 2)
    turn[0] = 0
    if stop == "attn":
        return done(pe, act, dve, pool, sp, counters)

    t_h = [None] * 8
    XO = lambda k: (oH[:, k, :], oL[:, k, :], t_o[k])
    for c in range(2):
        for j in range(4):
            nt = 4 * c + j
            b, tok = tile(XO)
            t_h[nt] = dve(lambda e, b=b, nt=nt: e.tensor_tensor(hT[:, nt, NM:L], hT[:, nt, NM:L], PS[:, b, :], ALU.add), tok)
            bank_free[b] = [t_h[nt]]
        ada_step()
    h1 = lambda k: hT[:, k, NM:L]
    attn_done = (pe.sem, pe.count)

    def norm_parts(H, Lo, src, gain, tok_of, extra, shift=None, t_gain=None):
        banks, tok = colsum(src, 8, SEGT, ones, tok_of)
        t = rstd(banks, SEGT, 1.0 / D, tok)
        out = []
        for k in range(8):
            i, tmp, free = take_tmp()
            x = tmp[:, :T]
            t1 = dve(lambda e, k=k, x=x: e.scalar_tensor_tensor(x, src(k), gain(k), RST[:, :T], ALU.mult, ALU.mult), t, t_param, t_gain, tok_of(k), free)
            rst_free[:] = [t1]
            if shift is not None:
                t1 = dve(lambda e, k=k, x=x: e.tensor_scalar(x, x, shift(k), None, ALU.add), t1)
            out.append(split(H[:, k, :], Lo[:, k, :], x, t1, extra))
            tmp_free[i] = [out[-1]]
        return out

    fH, fL = parts_at(4224, 8), parts_at(8320, 8)
    t_n = norm_parts(fH, fL, h1, lambda k: pc("ffn_norm", k), lambda k: t_h[k], attn_done)
    XF = lambda k: (fH[:, k, :], fL[:, k, :], t_n[k])
    hidH, hidL = parts_at(12416, 12), parts_at(18560, 12)
    HTM = [A[:, 24704 + 512 * i:25216 + 512 * i] for i in range(4)]
    htm_free = [[attn_done] for _ in range(4)]
    hid_free = attn_done
    for k0, nk in HALVES:
        t_hid = [None] * 22
        for nt in range(k0, k0 + nk):
            b0, tok0 = tile(XF)
            x = HTM[nt % 4]
            t = act(lambda e, b=b0, x=x: e.activation(x, PS[:, b, :], ACT.Silu), tok0, htm_free[nt % 4])
            bank_free[b0] = [t]
            b1, tok1 = tile(XF)
            t = dve(lambda e, b=b1, x=x: e.tensor_tensor(x, x, PS[:, b, :], ALU.mult), t, tok1)
            bank_free[b1] = [t]
            t_hid[nt] = split(hidH[:, nt - k0, :], hidL[:, nt - k0, :], x, t, hid_free)
            htm_free[nt % 4] = [t_hid[nt]]
            if nt % 2 == 1 and nt < 8:
                ada_step()
        XH_ = lambda k: (hidH[:, k - k0, :], hidL[:, k - k0, :], t_hid[k])
        for c in range(2):
            bs = [bank() for _ in range(4)]
            for r, n in ((0, 8), (8, nk - 8)):
                for j in range(4):
                    tok = mm3(PS[:, bs[j], :], gran(), XH_, bank_free[bs[j]] if r == 0 else None, start=(r == 0), stop=(r == 8), k0=k0 + r)
                    if r == 8:
                        nt = 4 * c + j
                        t_h[nt] = dve(lambda e, b=bs[j], nt=nt: e.tensor_tensor(hT[:, nt, NM:L], hT[:, nt, NM:L], PS[:, b, :], ALU.add), tok)
                        bank_free[bs[j]] = [t_h[nt]]
        hid_free = (pe.sem, pe.count)
    x2 = view(28672, 8, T)
    t_x2 = rms_to(lambda k: x2[:, k, :], h1, 8, SEGT, 1.0 / D, lambda k: pc("final_norm", k), lambda k: t_h[k])
    if stop == "fb":
        return done(pe, act, dve, pool, sp, counters)
    assert ada["n"] == 12
    t_spill = act.dma(dsem("spill"), lambda e: e.dma_start(a["x2_d"], x2), t_x2[7])

    def modcol(j, k):
        return MOD[:, 8 * j + k:8 * j + k + 1]

    def ada_norm(dst, src, tok_of, gname, jsh, jsc, gm, extra):
        t = dve(lambda e: e.tensor_scalar(gm, MOD[:, 8 * jsc:8 * jsc + 8], 1.0, None, ALU.add), ada["tok"], extra)
        t_gm = dve(lambda e: e.tensor_tensor(gm, gm, P(gname), ALU.mult), t, t_param)
        banks, tok = colsum(src, 8, SEGT, ones, tok_of)
        t = rstd(banks, SEGT, 1.0 / D, tok)
        out = []
        ts = [dve(lambda e, k=k: e.scalar_tensor_tensor(dst(k), src(k), gm[:, k:k + 1], RST[:, :T], ALU.mult, ALU.mult), t, t_gm, extra)
              for k in range(8)]
        rst_free[:] = [ts[-1]]
        for k in range(8):
            out.append(dve(lambda e, k=k: e.tensor_scalar(dst(k), dst(k), modcol(jsh, k), None, ALU.add), ts[k]))
        return out

    n1H, n1L = parts_at(0, 8), parts_at(4096, 8)
    hT_done = [t_x2[7], (pe.sem, pe.count)]
    t = dve(lambda e: e.tensor_scalar(SC, MOD[:, 8:16], 1.0, None, ALU.add), ada["tok"])
    t_gm = dve(lambda e: e.tensor_tensor(SC, SC, P("norm1"), ALU.mult), t, t_param)
    t_n1 = norm_parts(n1H, n1L, lambda k: x2[:, k, :], lambda k: SC[:, k:k + 1], lambda k: t_x2[k], hT_done, shift=lambda k: modcol(0, k), t_gain=t_gm)
    X1 = lambda k: (n1H[:, k, :], n1L[:, k, :], t_n1[k])
    if stop == "n1":
        return done(pe, act, dve, pool, sp, counters)

    UW = T + 30
    u = view(8192, 8, UW)
    cv = view(12528, 8, T)
    cvH, cvL = parts_at(8192, 8), parts_at(12528, 8)
    ymix = view(28672, 8, T)
    ffn_done = hT_done
    t_z = dve(lambda e: e.memset(u[:, :, 0:30], 0.0), ffn_done)
    t_cv = [None] * 8
    for c in range(4):
        for j in range(2):
            nt = 2 * c + j
            bs = [tile(X1) for _ in range(2)]
            dst = u[:, nt, 30:UW]
            t = act(lambda e, b=bs[0][0], dst=dst: e.activation(dst, PS[:, b, :], ACT.Sigmoid), bs[0][1], ffn_done)
            bank_free[bs[0][0]] = [t]
            t = dve(lambda e, b=bs[1][0], dst=dst: e.tensor_tensor(dst, dst, PS[:, b, :], ALU.mult), t, bs[1][1], t_z)
            bank_free[bs[1][0]] = [t]
            w0 = PO["cvw"][0] + 31 * nt
            t = dve(lambda e, nt=nt, w0=w0: e.tensor_scalar(cv[:, nt, :], u[:, nt, 0:T], PR[:, w0:w0 + 1], pc("cvb", nt), ALU.mult, ALU.add), t)
            for i in range(1, 31):
                t = dve(lambda e, nt=nt, i=i, w0=w0: e.scalar_tensor_tensor(cv[:, nt, :], u[:, nt, i:i + T], PR[:, w0 + i:w0 + i + 1], cv[:, nt, :], ALU.mult, ALU.add), t)
            t_cv[nt] = t

    def xbc_tile(nt, dst, raw, raw_free, extra=None):
        b, tok = tile(X1)
        t = act(lambda e: e.activation(raw[:, 3:3 + T], PS[:, b, :], ACT.Copy), tok, raw_free)
        bank_free[b] = [t]
        s0 = PO["scw"][0] + 4 * nt
        t = dve(lambda e: e.tensor_scalar(dst, raw[:, 0:T], PR[:, s0:s0 + 1], pc("scb", nt), ALU.mult, ALU.add), t, t_rz, extra)
        for i in range(1, 4):
            t = dve(lambda e, i=i: e.scalar_tensor_tensor(dst, raw[:, i:i + T], PR[:, s0 + i:s0 + i + 1], dst, ALU.mult, ALU.add), t)
        t2 = act(lambda e: e.activation(dst, dst, ACT.Silu), t)
        return tok, t2, t

    Bf = view(18432, 4, T)
    Cf = view(20480, 4, T)
    Bt = view(22528, 4, 512)
    RAW = [A[:, 24576 + 516 * i:24576 + 516 * i + 515] for i in range(2)]
    t_rz = [dve(lambda e, i=i: e.memset(RAW[i][:, 0:3], 0.0), ffn_done) for i in range(2)]
    raw_free = [[], []]
    t_B, t_C = [None] * 4, [None] * 4
    for c, (dst, tt_) in enumerate(((Bf, t_B), (Cf, t_C))):
        for j in range(4):
            i = j % 2
            tok, t2, t = xbc_tile(16 + 4 * c + j, dst[:, j, :], RAW[i], raw_free[i], ffn_done)
            raw_free[i] = [t]
            tt_[j] = t2
    for tt in range(4):
        b = bank()
        for g in range(4):
            tok = pe(lambda e, tt=tt, g=g, b=b: e.transpose(PS[:, b, g * 128:(g + 1) * 128], Bf[:, g, tt * 128:(tt + 1) * 128], ident),
                     bank_free[b], t_B[g], inc=(g == 3))
        t_Bt = act(lambda e, tt=tt, b=b: e.activation(Bt[:, tt, :], PS[:, b, :], ACT.Copy), tok)
        bank_free[b] = [t_Bt]
    DT = view(25632, 4, T)[0:32]
    b, tok = tile(X1, m=32)
    t = act(lambda e, b=b: e.activation(DT[:, 0, :], PS[0:32, b, :], ACT.Identity, bias=P("dtb", 0, 32)), tok, ffn_done)
    bank_free[b] = [t]
    t = log1p_exp(DT[:, 0, :], DT[:, 1, :], DT[:, 2, :], DT[:, 3, :], t, 32)
    t_dt = dve(lambda e: e.scalar_tensor_tensor(DT[:, 0, :], DT[:, 0, :], 0.0, DT[:, 3, :], ALU.max, ALU.add), t)
    alg = P("alog", 0, 32)
    t = act(lambda e: e.activation(alg, alg, ACT.Exp), t_param)
    t = dve(lambda e: e.tensor_scalar(DT[:, 1, :], DT[:, 0, :], alg, -1.0, ALU.mult, ALU.mult), t, t_dt)
    for c in range(4):
        t_acs = dve(lambda e, c=c: e.tensor_tensor_scan(DT[:, 2, c * 128:(c + 1) * 128], C("ones", 0, 32),
                                                DT[:, 1, c * 128:(c + 1) * 128], 0.0, ALU.mult, ALU.add), t)
    dtT, acsT = DT[:, 0, :], DT[:, 2, :]
    TK = view(27680, 5, 128)
    b = bank()
    for w_, srcT in enumerate((dtT, acsT)):
        for c in range(4):
            tok = pe(lambda e, w_=w_, c=c, srcT=srcT, b=b: e.transpose(PS[:, b, w_ * 128 + c * 32:w_ * 128 + c * 32 + 32], srcT[:, c * 128:(c + 1) * 128],
                                                             C("ident", 0, 32)[:, 0:32]), bank_free[b], t_acs, inc=(w_ == 1 and c == 3))
    t_tk = dve(lambda e, b=b: e.tensor_copy(TK[:, 0:2, :], PS[:, b, 0:256].rearrange("p (a b) -> p a b", a=2)), tok, ffn_done)
    bank_free[b] = [t_tk]
    b = bank()
    tok = pe(lambda e, b=b: e.matmul(PS[:, b, 0:128], ident[:, 127:128].broadcast_to([128, 128]), TK[:, 1, :], start=True, stop=True), bank_free[b], t_tk)
    t = dve(lambda e, b=b: e.tensor_copy(TK[:, 2, :], PS[:, b, 0:128]), tok)
    bank_free[b] = [t]
    t = dve(lambda e: e.tensor_tensor(TK[:, 3, :], TK[:, 2, :], TK[:, 1, :], ALU.subtract), t)
    t = act(lambda e: e.activation(TK[:, 3, :], TK[:, 3, :], ACT.Exp), t)
    t_tk2 = act(lambda e: e.activation(TK[:, 4, :], TK[:, 2, :], ACT.Exp), t)

    banks, tok = colsum(lambda k: cv[:, k, :], 8, SEGT, ones, lambda k: t_cv[k], square=False)
    t = act(lambda e, b=banks[0]: e.activation(RST[:, :T], PS[:, b, :], ACT.Copy, scale=1.0 / D), tok, rst_free)
    bank_free[banks[0]] = [t]
    tc = [dve(lambda e, k=k: e.tensor_tensor(cv[:, k, :], cv[:, k, :], RST[:, :T], ALU.subtract), t) for k in range(8)]
    rst_free[:] = [tc[-1]]
    banks, tok = colsum(lambda k: cv[:, k, :], 8, SEGT, ones, lambda k: tc[k])
    t = rstd(banks, SEGT, 1.0 / D, tok)
    tl = []
    for k in range(8):
        t1 = dve(lambda e, k=k: e.tensor_tensor(cv[:, k, :], cv[:, k, :], RST[:, :T], ALU.mult), t, tc[k])
        t1 = act(lambda e, k=k: e.activation(cv[:, k, :], cv[:, k, :], ACT.Silu, scale=pc("lng", k), bias=pc("lnb", k)), t1)
        tl.append(split(cvH[:, k, :], cvL[:, k, :], cv[:, k, :], t1, t_cv[7]))
    rst_free[:] = [t1, (dve.sem, dve.count)]
    XC = lambda k: (cvH[:, k, :], cvL[:, k, :], tl[k])
    SG = [A[:, 17408 + 512 * i:17408 + 512 * (i + 1)] for i in range(2)] + [A[:, 24576 + 516 * i:25088 + 516 * i] for i in range(2)]
    sg_free = [[ffn_done], [ffn_done], [t_C[2]], [t_C[3]]]
    t_y = [None] * 8
    for c in range(2):
        t_sg = []
        for j in range(4):
            b1, tok1 = tile(X1)
            t = act(lambda e, b1=b1, j=j: e.activation(SG[j], PS[:, b1, :], ACT.Sigmoid), tok1, sg_free[j])
            bank_free[b1] = [t]
            t_sg.append(t)
        for j in range(4):
            nt = 4 * c + j
            b2, tok2 = tile(XC)
            t_y[nt] = dve(lambda e, b2=b2, nt=nt, j=j: e.tensor_tensor(ymix[:, nt, :], SG[j], PS[:, b2, :], ALU.mult), t_sg[j], tok2, t_spill)
            bank_free[b2] = [t_y[nt]]
            sg_free[j] = [t_y[nt]]
    if stop == "ycv":
        return done(pe, act, dve, pool, sp, counters)

    cv_done = [(pe.sem, pe.count), (dve.sem, dve.count), t_spill]
    t_yspill = act.dma(dsem("yspill"), lambda e: e.dma_start(a["ymix_d"], ymix), t_y[7])
    free2 = cv_done + [t_yspill]
    xsf = view(8192, 4, T)
    xdt = view(10240, 4, 512)
    yT = view(28672, 8, T)
    yt = lambda k: yT[:, k % 8, :]
    STS = [A[:, 13312 + 512 * i:13312 + 512 * (i + 1)] for i in range(3)]
    XD = [A[:, 14848 + 512 * i:14848 + 512 * (i + 1)] for i in range(2)]
    EB = [A[:, 15872 + 512 * i:15872 + 512 * (i + 1)] for i in range(2)]
    ZB = A[:, 16896:17408]
    MB = [view(12288, 2, 512), view(17408, 2, 512)]
    mb_free, eb_free, xd_free = [free2, free2], [free2, free2], [free2, free2]
    zb_free, cbm_free, xs_free, xdt_free = free2, [], free2, free2
    t_ysp = [None, None]
    h64 = lambda x: x.rearrange("p (h d) -> p h d", d=64)
    for g in range(4):
        if g == 0:
            t = [dve(lambda e, i=i: e.memset(RAW[i][:, 0:3], 0.0), cv_done) for i in range(2)]
            raw_free = [[t[0]], [t[1]]]
        t_xs = []
        for j in range(4):
            i = j % 2
            tok, t2, t = xbc_tile(4 * g + j, xsf[:, j, :], RAW[i], raw_free[i], xs_free)
            raw_free[i] = [t]
            t_xs.append(t2)
        b = bank()
        for c in range(4):
            tok = pe(lambda e, c=c, b=b, g=g: e.matmul(PS[:, b, c * 128:(c + 1) * 128], Bf[:, g, c * 128:(c + 1) * 128], Cf[:, g, c * 128:(c + 1) * 128],
                                                  start=True, stop=True), bank_free[b], t_B[g], t_C[g], inc=(c == 3))
        sm = C("smask").rearrange("p (a b) -> p a b", a=1).broadcast_to([128, 4, 128])
        t_cb = dve(lambda e, b=b, sm=sm: e.tensor_tensor(CBM[:, :].rearrange("p (a b) -> p a b", a=4), PS[:, b, :].rearrange("p (a b) -> p a b", a=4), sm, ALU.mult),
                   tok, cbm_free)
        bank_free[b] = [t_cb]
        t_xdt = []
        for c in range(4):
            b = bank()
            for j in range(4):
                tok = pe(lambda e, c=c, j=j, b=b: e.transpose(PS[:, b, j * 128:(j + 1) * 128], xsf[:, j, c * 128:(c + 1) * 128], ident),
                         bank_free[b], t_xs[j], inc=(j == 3))
            sc = TK[:, 0, c * 32 + 8 * g:c * 32 + 8 * g + 8].rearrange("p (h d) -> p h d", d=1).broadcast_to([128, 8, 64])
            t = dve(lambda e, c=c, b=b, sc=sc: e.tensor_tensor(h64(xdt[:, c, :]), h64(PS[:, b, :]), sc, ALU.mult), tok, xdt_free, t_tk)
            bank_free[b] = [t]
            t_xdt.append(t)
        t_st = [None] * 3
        for c in range(3):
            i = c % 2
            dc = TK[:, 3, c * 32 + 8 * g:c * 32 + 8 * g + 8].rearrange("p (h d) -> p h d", d=1).broadcast_to([128, 8, 64])
            t = dve(lambda e, c=c, i=i, dc=dc: e.tensor_tensor(h64(XD[i]), h64(xdt[:, c, :]), dc, ALU.mult), t_xdt[c], xd_free[i], t_tk2)
            b = bank()
            tok = pe(lambda e, c=c, b=b, g=g, i=i: e.matmul(PS[:, b, :], Bt[:, c, g * 128:(g + 1) * 128], XD[i], start=True, stop=True), t, t_Bt, bank_free[b])
            xd_free[i] = [tok]
            if c == 0:
                t = dve(lambda e, b=b: e.tensor_copy(STS[0], PS[:, b, :]), tok, zb_free)
            else:
                cd = TK[:, 4, c * 32 + 8 * g:c * 32 + 8 * g + 8].rearrange("p (h d) -> p h d", d=1).broadcast_to([128, 8, 64])
                t = dve(lambda e, c=c, cd=cd: e.tensor_tensor(h64(STS[c]), h64(STS[c - 1]), cd, ALU.mult), t_st[c - 1], zb_free)
                t = dve(lambda e, c=c, b=b: e.tensor_tensor(STS[c], STS[c], PS[:, b, :], ALU.add), t, tok)
            bank_free[b] = [t]
            t_st[c] = t
        t_yg = []
        for i in range(4):
            nt = 4 * g + i
            m, eb = MB[i % 2], EB[i % 2]
            td = []
            for hh in range(2):
                h = 8 * g + 2 * i + hh
                b = bank()
                tok = pe(lambda e, b=b, h=h: e.matmul(PS[:, b, :], C("ident", 0, 32)[:, h:h + 1].broadcast_to([32, 128]), acsT, start=True, stop=True),
                         t_acs, bank_free[b])
                for c in range(4):
                    t = dve(lambda e, b=b, h=h, hh=hh, c=c, m=m: e.tensor_scalar(m[:, hh, c * 128:(c + 1) * 128], PS[:, b, c * 128:(c + 1) * 128],
                                                                 TK[:, 1, c * 32 + h:c * 32 + h + 1], 0.0, ALU.subtract, ALU.min), tok, mb_free[i % 2], t_tk)
                bank_free[b] = [t]
            t = act(lambda e, m=m: e.activation(m, m, ACT.Exp), t)
            cb = CBM[:, :].rearrange("p (a b) -> p a b", a=1).broadcast_to([128, 2, 512])
            t_m = dve(lambda e, m=m, cb=cb: e.tensor_tensor(m, m, cb, ALU.mult), t, t_cb)
            b = bank()
            h0 = 8 * g + 2 * i
            for hh in range(2):
                tok = pe(lambda e, b=b, h0=h0, hh=hh: e.matmul(PS[64 * hh:64 * hh + 64, b, :], C("ident", 0, 32)[:, h0 + hh:h0 + hh + 1].broadcast_to([32, 64]), acsT,
                                                            start=True, stop=True), t_acs, bank_free[b])
            t_eb = act(lambda e, b=b, eb=eb: e.activation(eb, PS[:, b, :], ACT.Exp), tok, eb_free[i % 2])
            bank_free[b] = [t_eb]
            bz, tokz = tile(X1)
            t_z = act(lambda e, bz=bz: e.activation(ZB, PS[:, bz, :], ACT.Silu), tokz, zb_free)
            bank_free[bz] = [t_z]
            bo = bank()
            for c in range(1, 4):
                tok = pe(lambda e, c=c, bo=bo, g=g, i=i: e.matmul(PS[:, bo, c * 128:(c + 1) * 128], STS[c - 1][:, i * 128:(i + 1) * 128], Cf[:, g, c * 128:(c + 1) * 128],
                                                             start=True, stop=True), t_st[c - 1], bank_free[bo], inc=(c == 3))
            t = dve(lambda e, bo=bo, eb=eb: e.tensor_tensor(eb[:, 128:512], eb[:, 128:512], PS[:, bo, 128:512], ALU.mult), t_eb, tok)
            bank_free[bo] = [t]
            bd = bank()
            for c in range(4):
                for hh in range(2):
                    tok = pe(lambda e, c=c, hh=hh, bd=bd, i=i, m=m: e.matmul(PS[64 * hh:64 * hh + 64, bd, c * 128:(c + 1) * 128], xdt[:, c, (2 * i + hh) * 64:(2 * i + hh) * 64 + 64],
                                                                m[:, hh, c * 128:(c + 1) * 128], start=True, stop=True),
                             t_m, t_xdt[c], bank_free[bd] if c == 0 and hh == 0 else None, inc=(c == 3 and hh == 1))
            mb_free[i % 2] = [tok]
            t2 = dve(lambda e, nt=nt, i=i, bd=bd: e.scalar_tensor_tensor(yt(nt), xsf[:, i, :], pc("dsk", nt), PS[:, bd, :], ALU.mult, ALU.add), tok, free2, t_ysp[g % 2])
            bank_free[bd] = [t2]
            t2 = dve(lambda e, nt=nt, eb=eb: e.tensor_tensor(yt(nt)[:, 128:512], yt(nt)[:, 128:512], eb[:, 128:512], ALU.add), t, t2)
            eb_free[i % 2] = [t2]
            t2 = dve(lambda e, nt=nt: e.tensor_tensor(yt(nt), yt(nt), ZB, ALU.mult), t2, t_z)
            zb_free = [t2]
            t_yg.append(t2)
        cbm_free, xs_free, xdt_free = [t_m], [t2], [tok]
        banks, tok = colsum(lambda k, g=g: yt(4 * g + k), 4, SEGT, ones, lambda k, t_yg=t_yg: t_yg[k])
        t = rstd(banks, SEGT, 1.0 / 512, tok)
        for k in range(4):
            nt = 4 * g + k
            t_yl = dve(lambda e, nt=nt: e.scalar_tensor_tensor(yt(nt), yt(nt), pc("sng", nt), RST[:, :T], ALU.mult, ALU.mult), t, t_param)
        rst_free[:] = [t_yl]
        if g < 2:
            t_ysp[g] = act.dma(dsem(f"ysp{g}"), lambda e, g=g: e.dma_start(a["y01_d"][:, 4 * g:4 * g + 4, :], yT[:, 4 * g:4 * g + 4, :]), t_yl)
    ssd_done = [t_yl, (pe.sem, pe.count)]
    if stop == "ssd":
        return done(pe, act, dve, pool, sp, counters)

    ymix2 = view(24576, 8, T)
    x2b = view(0, 8, T)
    y01 = view(8192, 8, T)
    t_y01 = act.dma(dsem("back3"), lambda e: e.dma_start(y01, a["y01_d"]), ssd_done, t_ysp)
    t_ym = act.dma(dsem("back"), lambda e: e.dma_start(ymix2, a["ymix_d"]), ssd_done)
    SG = view(20480, 8, T)
    t_sg = []
    for nt in range(8):
        b1, tok1 = tile(X1)
        t = act(lambda e, b1=b1, nt=nt: e.activation(SG[:, nt, :], PS[:, b1, :], ACT.Sigmoid), tok1, ssd_done)
        bank_free[b1] = [t]
        t_sg.append(t)
    gate_done = (pe.sem, pe.count)
    t_x2b = act.dma(dsem("back2"), lambda e: e.dma_start(x2b, a["x2_d"]), gate_done)
    yH = [parts_at(12288, 8), parts_at(4096, 8)]
    yL = [parts_at(8192, 8), parts_at(28672, 8)]
    t_yp = [split(yH[0][:, k, :], yL[0][:, k, :], y01[:, k, :], t_y01, ssd_done) for k in range(8)]
    t_yp += [split(yH[1][:, k, :], yL[1][:, k, :], yT[:, k, :], gate_done, t_yl) for k in range(8)]
    XY = lambda k: (yH[k // 8][:, k % 8, :], yL[k // 8][:, k % 8, :], t_yp[k])
    mH, mL = parts_at(16384, 8), parts_at(24576, 8)
    t_m_ = [None] * 8
    for c in range(2):
        bs = [bank() for _ in range(4)]
        for r in (0, 8):
            for j in range(4):
                nt = 4 * c + j
                tok = mm3(PS[:, bs[j], :], gran(), XY, bank_free[bs[j]] if r == 0 else None, start=(r == 0), stop=(r == 8), k0=r)
                if r == 8:
                    t = dve(lambda e, b=bs[j], nt=nt: e.tensor_tensor(SG[:, nt, :], SG[:, nt, :], PS[:, b, :], ALU.mult), t_sg[nt], tok)
                    bank_free[bs[j]] = [t]
                    t = dve(lambda e, nt=nt: e.tensor_tensor(ymix2[:, nt, :], ymix2[:, nt, :], SG[:, nt, :], ALU.add), t, t_ym)
                    t_m_[nt] = split(mH[:, nt, :], mL[:, nt, :], ymix2[:, nt, :], t)
    XM = lambda k: (mH[:, k, :], mL[:, k, :], t_m_[k])
    t_h2 = [None] * 8
    for c in range(2):
        for j in range(4):
            nt = 4 * c + j
            b, tok = tile(XM)
            t_h2[nt] = dve(lambda e, b=b, nt=nt: e.scalar_tensor_tensor(x2b[:, nt, :], PS[:, b, :], modcol(2, nt), x2b[:, nt, :], ALU.mult, ALU.add), tok, t_x2b)
            bank_free[b] = [t_h2[nt]]
    n2 = view(18432, 8, T)
    mix_done = [(pe.sem, pe.count)]
    t_n2 = ada_norm(lambda k: n2[:, k, :], lambda k: x2b[:, k, :], lambda k: t_h2[k], "norm2", 3, 4, SC, mix_done)
    if stop == "n2":
        return done(pe, act, dve, pool, sp, counters)

    RW = view(8192, 8, 72)
    t_rw = act.dma(dsem("rw"), lambda e: e.dma_start(RW, a["rw"]), mix_done)
    LG = view(8768, 4, 72)
    R = 9088
    r3 = lambda o, n: view(R + o, 4, n)
    gmax, gidx, emax, eidx = r3(0, 8), r3(32, 8), r3(64, 8), r3(96, 8)
    eg = r3(128, 8)
    s1, s2, gp, wa, wb, tmp1, tmp2 = (r3(160 + 4 * i, 1) for i in range(7))
    el8 = r3(200, 8)
    msel = view(R + 240, 4, 64)
    OH = [view(R + 496 + 256 * i, 4, 64) for i in range(2)]
    OHS = view(R + 1008, 4, 64)
    POS = view(R + 1264, 4, 64)
    IDX = CBM[:, 64:80].bitcast(U32)
    KEEP = CBM[:, 0:64]
    SLOTU = CBM[:, 80:88].bitcast(U32)
    LIST = CBM[:, 88:120].bitcast(U32)
    TOKU = CBM[:, 120:124].bitcast(U32)
    for tt in range(4):
        b = bank()
        tok = mms(PS[:, b, 0:72], [(n2[:, k, tt * 128:(tt + 1) * 128], RW[:, k, :]) for k in range(8)], t_rw, t_n2, bank_free[b])
        t_lg = dve(lambda e, b=b, tt=tt: e.tensor_tensor(LG[:, tt, :], PS[:, b, 0:72], P("rb"), ALU.add), tok, t_param)
        bank_free[b] = [t_lg]
    h2t = view(4096, 4, D)
    n2t = [A[:, 28672 + 1024 * i:28672 + 1024 * (i + 1)] for i in range(2)]
    n2t_free = [mix_done, mix_done]
    for tt in range(4):
        for half in range(2):
            for src, dst_of in ((n2, None), (x2b, h2t)):
                b = bank()
                for j in range(4):
                    tok = pe(lambda e, tt=tt, half=half, j=j, src=src, b=b: e.transpose(PS[:, b, j * 128:(j + 1) * 128], src[:, 4 * half + j, tt * 128:(tt + 1) * 128], ident),
                             bank_free[b], t_n2, t_h2, inc=(j == 3))
                dst = (n2t[tt % 2] if dst_of is None else h2t[:, tt, :])[:, 512 * half:512 * half + 512]
                t = act(lambda e, dst=dst, b=b: e.activation(dst, PS[:, b, :], ACT.Copy), tok, n2t_free[tt % 2] if dst_of is None else mix_done)
                bank_free[b] = [t]
                if dst_of is None:
                    t_nt = t
                else:
                    t_h2t = t
        t_n2d = act.dma(dsem(f"n2d{tt % 2}"), lambda e, tt=tt: e.dma_start(a["n2_d"][tt * 128:(tt + 1) * 128, :], n2t[tt % 2]), t_nt)
        n2t_free[tt % 2] = [t_n2d]
    t_n2ds = [(dsem("n2d0")[0], dsem("n2d0")[1]), (dsem("n2d1")[0], dsem("n2d1")[1])]
    dense_done = [(pe.sem, pe.count)]
    extra_slots = [Slot(A[:, 11264 + WC * i:11264 + WC * (i + 1)], f"x{i}") for i in range(5)]

    bc = lambda x, n: x.broadcast_to([128, 4, n])
    t = t_lg
    for tt in range(4):
        tm = dve(lambda e, tt=tt: e.max(gmax[:, tt, :], LG[:, tt, 0:8]), t)
    for tt in range(4):
        t = dve(lambda e, tt=tt: e.max_index(IDX[:, 0:8], gmax[:, tt, :], LG[:, tt, 0:8]), tm, t)
        t = dve(lambda e, tt=tt: e.tensor_copy(gidx[:, tt, :], IDX[:, 0:8]), t)
    t1 = dve(lambda e: e.tensor_tensor(eg, LG[:, :, 0:8], bc(gmax[:, :, 0:1], 8), ALU.subtract), tm)
    t1 = act(lambda e: e.activation(eg, eg, ACT.Exp), t1)
    t1 = dve(lambda e: e.tensor_reduce(s1, eg, AX, ALU.add), t1)
    t_gp = dve(lambda e: e.reciprocal(gp, s1), t1)
    t2 = dve(lambda e: e.tensor_tensor(el8, C("iota8").rearrange("p (a b) -> p a b", a=1).broadcast_to([128, 4, 8]), bc(gidx[:, :, 0:1], 8), ALU.is_equal), t)
    t2 = [dve(lambda e, tt=tt: e.tensor_tensor(msel[:, tt, :].rearrange("p (a b) -> p a b", b=8), LG[:, tt, 8:72].rearrange("p (a b) -> p a b", b=8),
                                        el8[:, tt, :].rearrange("p (a b) -> p a b", b=1).broadcast_to([128, 8, 8]), ALU.mult), t2) for tt in range(4)][-1]
    t2 = [dve(lambda e, tt=tt: e.tensor_reduce(el8[:, tt, :], msel[:, tt, :].rearrange("p (a b) -> p b a", b=8), AX, ALU.add), t2) for tt in range(4)][-1]
    for tt in range(4):
        tm = dve(lambda e, tt=tt: e.max(emax[:, tt, :], el8[:, tt, :]), t2)
    for tt in range(4):
        t = dve(lambda e, tt=tt: e.max_index(IDX[:, 8:16], emax[:, tt, :], el8[:, tt, :]), tm, t)
        t = dve(lambda e, tt=tt: e.tensor_copy(eidx[:, tt, :], IDX[:, 8:16]), t)
    t3 = dve(lambda e: e.tensor_tensor(eg, emax, bc(emax[:, :, 0:1], 8), ALU.subtract), t_gp, tm)
    t3 = act(lambda e: e.activation(eg, eg, ACT.Exp), t3)
    t3 = dve(lambda e: e.tensor_reduce(s1, eg, AX, ALU.add), t3)
    t3 = dve(lambda e: e.reciprocal(s1, s1), t3)
    t3 = dve(lambda e: e.tensor_tensor(eg, eg, bc(s1, 8), ALU.mult), t3)
    t3 = dve(lambda e: e.tensor_tensor(s2, eg[:, :, 0:1], eg[:, :, 1:2], ALU.add), t3)
    t3 = dve(lambda e: e.reciprocal(s2, s2), t3)
    t3 = dve(lambda e: e.tensor_tensor(s2, s2, gp, ALU.mult), t3)
    WK = [KEEP[:, 4 * i:4 * i + 4].rearrange("p (a b) -> p a b", b=1) for i in range(2)]
    for i in range(2):
        t_wk = dve(lambda e, i=i: e.tensor_tensor(WK[i], eg[:, :, i:i + 1], s2, ALU.mult), t3)
    t4 = dve(lambda e: e.tensor_scalar(gidx[:, :, 0:1], gidx[:, :, 0:1], 8.0, None, ALU.mult), t, t2)
    t4 = dve(lambda e: e.tensor_tensor(eidx[:, :, 0:2], eidx[:, :, 0:2], bc(gidx[:, :, 0:1], 2), ALU.add), t4)
    i64 = C("iota64").rearrange("p (a b) -> p a b", a=1).broadcast_to([128, 4, 64])
    for i in range(2):
        t5 = dve(lambda e, i=i: e.tensor_tensor(OH[i], i64, bc(eidx[:, :, i:i + 1], 64), ALU.is_equal), t4)
    t5 = dve(lambda e: e.tensor_tensor(OHS, OH[0], OH[1], ALU.add), t5)
    b = bank()
    for tt in range(4):
        for s in range(tt + 1):
            tok = pe(lambda e, tt=tt, s=s, b=b: e.matmul(PS[:, b, tt * 64:tt * 64 + 64], C("ustrict") if s == tt else ones, OHS[:, s, :], start=(s == 0), stop=(s == tt)),
                     t5, bank_free[b])
    for s in range(4):
        tok = pe(lambda e, s=s, b=b: e.matmul(PS[:, b, 256:320], ones, OHS[:, s, :], start=(s == 0), stop=(s == 3)))
    tok_pos = tok
    t6 = dve(lambda e, b=b: e.tensor_copy(POS, PS[:, b, 0:256].rearrange("p (a b) -> p a b", a=4)), tok)
    CNTF = CBM[:, 188:254]
    t_cnt = dve(lambda e, b=b: e.tensor_copy(CNTF[:, 0:64], PS[:, b, 256:320]), tok)
    bank_free[b] = [t6, t_cnt]
    NB, INC, VV = (A[:, 10608 + 64 * i:10672 + 64 * i] for i in range(3))
    CNT = CNTF[:, 0:64]
    t9 = dve(lambda e: e.tensor_scalar(NB, CNT, float(BLK), None, ALU.is_gt), t_cnt, mix_done)
    for k in range(2, T // BLK):
        t9 = dve(lambda e, k=k: e.scalar_tensor_tensor(NB, CNT, float(BLK * k), NB, ALU.is_gt, ALU.add), t9)
    t9 = dve(lambda e: e.tensor_tensor_scan(INC, ones[:, 0:64], NB, 0.0, ALU.mult, ALU.add), t9)
    t10 = dve(lambda e: e.tensor_tensor(VV, INC, NB, ALU.subtract), t9)
    t10 = dve(lambda e: e.tensor_tensor(VV, VV, C("iota64"), ALU.subtract), t10)
    t_v = dve(lambda e: e.tensor_scalar(VV, VV, float(BLK), float(MAIN - BLK), ALU.mult, ALU.add), t10)
    t11 = dve(lambda e: e.tensor_scalar(NB, INC, C("tok")[:, 0:1], None, ALU.is_le), t10)
    t11 = dve(lambda e: e.tensor_reduce(KEEP[:, 24:25], NB, AX, ALU.add), t11, t_wk)
    b = bank()
    tok = pe(lambda e, b=b: e.matmul(PS[0:1, b, 0:OVER], KEEP[:, 24:25], ident[:, 0:OVER], start=True, stop=True), t11, bank_free[b])
    OVI = CBM[0:1, 124:141].bitcast(I32)
    t11 = dve(lambda e, b=b: e.tensor_copy(OVI[:, 0:OVER], PS[0:1, b, 0:OVER]), tok)
    bank_free[b] = [t11]
    t_ovi = dve(lambda e: e.tensor_copy(OVI[:, OVER:OVER + 1], INC[0:1, 63:64]), t11)
    vb = VV.rearrange("p (a b) -> p a b", a=1).broadcast_to([128, 4, 64])
    for i in range(2):
        t6 = dve(lambda e, i=i: e.tensor_tensor(OHS, OH[i], POS, ALU.mult), t6, tok_pos)
        t6 = dve(lambda e: e.tensor_reduce(tmp1, OHS, AX, ALU.add), t6)
        t6 = dve(lambda e, i=i: e.tensor_tensor(msel, OH[i], vb, ALU.mult), t6, t_v)
        t6 = dve(lambda e: e.tensor_reduce(tmp2, msel, AX, ALU.add), t6)
        t6 = dve(lambda e: e.scalar_tensor_tensor(tmp2, tmp1, float(BLK), tmp2, ALU.is_ge, ALU.mult), t6)
        t6 = dve(lambda e: e.tensor_tensor(tmp2, tmp2, tmp1, ALU.add), t6)
        t6 = dve(lambda e, i=i: e.scalar_tensor_tensor(tmp2, eidx[:, :, i:i + 1], float(BLK), tmp2, ALU.mult, ALU.add), t6)
        t_slot = dve(lambda e, i=i: e.tensor_copy(SLOTU[:, 4 * i:4 * i + 4].rearrange("p (a b) -> p a b", b=1), tmp2), t6)
        t6 = t_slot
    t7 = dve(lambda e: e.tensor_copy(TOKU[:, :], C("tok")), t_const)
    for i in range(2):
        for tt in range(4):
            t_sc = pool.dma(dsem("scat"), lambda e, i=i, tt=tt: e.indirect_dma_start(a["list_d"], bass.IndirectOffsetOnAxis(ap=SLOTU[:, 4 * i + tt:4 * i + tt + 1], axis=0),
                                                                           TOKU[:, tt:tt + 1], None), t_zl, t_slot, t7)
    ld = a["list_d"][0:MAIN, :].rearrange("(q s j) o -> s j (q o)", s=2, j=BLK)
    for s in range(2):
        t_list = pool.dma(dsem("list"), lambda e, s=s: e.dma_start(LIST[64 * s:64 * s + 64, :], ld[s], allow_slow_non_contiguous=True), t_sc)
    if stop == "route":
        return done(pe, act, dve, pool, sp, counters)

    route_done = [t_list, t_slot, t_ovi, t_wk] + dense_done + t_n2ds
    for i in range(4):
        extra_slots[i].free = dense_done + ([t_h2t] if i == 0 else [])
    extra_slots[4].free = t_n2ds + dense_done
    for i in (2, 3):
        s = Slot(RG[:, i * WC:(i + 1) * WC], f"w{i}")
        s.free = dense_done
        ring.appendleft(s)
    for s in extra_slots[::-1]:
        ring.appendleft(s)
    XG = [A[:, 1024 * i:1024 * (i + 1)] for i in range(2)]
    XT = [view(2048 + 1024 * i, 8, 128) for i in range(2)]
    H13 = [A[:, 8192 + 512 * i:8192 + 512 * (i + 1)] for i in range(2)]
    YO = [A[:, 9216 + 512 * i:9216 + 512 * (i + 1)] for i in range(2)]
    HT = [view(10240 + 256 * i, 4, 64) for i in range(2)]
    SL = [view(10752 + 256 * i, 4, 64) for i in range(2)]
    xg_free, xt_free, h13_free, yo_free, ht_free = ([route_done, route_done] for _ in range(5))
    t_xt = {}

    def m_gather(q):
        i = q % 2
        t = pool.dma(dsem(f"xg{i}"), lambda e: e.indirect_dma_start(XG[i], None, a["n2_d"], bass.IndirectOffsetOnAxis(ap=LIST[:, q:q + 1], axis=0)),
                     xg_free[i], t_n2ds)
        for half in range(2):
            b = bank()
            for j in range(4):
                k = 4 * half + j
                tok = pe(lambda e, b=b, j=j, k=k: e.transpose(PS[:, b, j * 128:(j + 1) * 128], XG[i][:, k * 128:(k + 1) * 128], ident), t, bank_free[b], inc=(j == 3))
            fn = lambda e, b=b, half=half: e.tensor_copy(XT[i][:, 4 * half:4 * half + 4, :], PS[:, b, :].rearrange("p (a b) -> p a b", a=4))
            t_ = dve(fn, tok, xt_free[i])
            bank_free[b] = [t_]
        xg_free[i] = [tok]
        t_xt[q] = t_

    hst, tst = {}, {}
    w2s = {}

    def m_h(ex):
        q, s = divmod(ex, 2)
        i = q % 2
        sl1, tw1, w1_ = fetch_w(a["w1"][ex], 0)
        sl3, tw3, w3_ = fetch_w(a["w3"][ex], 0)
        sl2, tw2 = fetch((0, (4, D), a["w2"][ex].rearrange("(k p) n -> p k n", p=128)))
        w2s[ex] = (sl2, tw2, sl2.ap.rearrange("p (k n) -> p k n", k=4))
        b = bank()
        for k in range(8):
            for hh, w, tw in ((0, w1_, tw1), (1, w3_, tw3)):
                tok = pe(lambda e, k=k, hh=hh, w=w, b=b: e.matmul(PS[64 * hh:64 * hh + 64, b, :], XT[i][:, k, 64 * s:64 * s + 64], w[:, k, :], start=(k == 0), stop=(k == 7)),
                         tw, t_xt[q], bank_free[b] if k == 0 and hh == 0 else None, inc=(k == 7 and hh == 1))
        sl1.free, sl3.free = [tok], [tok]
        if s == 1:
            xt_free[i] = [tok]
        p = ex % 2
        t = act(lambda e: e.activation(H13[p], PS[:, b, :], ACT.Copy), tok, h13_free[p])
        bank_free[b] = [t]
        hst[ex] = t

    def m_t(ex):
        p = ex % 2
        b = bank()
        for j in range(4):
            tok = pe(lambda e, j=j: e.transpose(PS[:, b, j * 128:(j + 1) * 128], H13[p][:, j * 128:(j + 1) * 128], ident), hst[ex], bank_free[b], inc=(j == 3))
        h13_free[p] = [tok]
        pv = PS[:, b, :].rearrange("p (a b) -> p a b", a=4)
        t = act(lambda e: e.activation(SL[p], pv[:, :, 0:64], ACT.Silu), tok, ht_free[p])
        t = dve(lambda e: e.tensor_tensor(HT[p], SL[p], pv[:, :, 64:128], ALU.mult), t, tok)
        bank_free[b] = [t]
        tst[ex] = t

    def m_y(ex):
        p = ex % 2
        sl2, tw2, w2_ = w2s[ex]
        b = bank()
        for k in range(4):
            for hh in range(2):
                tok = pe(lambda e, k=k, hh=hh: e.matmul(PS[64 * hh:64 * hh + 64, b, :], HT[p][:, k, :], w2_[:, k, 512 * hh:512 * hh + 512], start=(k == 0), stop=(k == 3)),
                         tw2, tst[ex], bank_free[b] if k == 0 and hh == 0 else None, inc=(k == 3 and hh == 1))
        sl2.free = [tok]
        ht_free[p] = [tok]
        t = dve(lambda e: e.tensor_copy(YO[p], PS[:, b, :]), tok, yo_free[p])
        bank_free[b] = [t]
        for hh in range(2):
            t_ = act.dma(dsem(f"yo{p}"), lambda e, hh=hh: e.dma_start(a["y_d"][BLK * ex:BLK * ex + BLK, 512 * hh:512 * hh + 512], YO[p][64 * hh:64 * hh + 64, :]), t)
        yo_free[p] = [t_]

    nx = 4 if stop == "moe4" else NE
    for n in range(nx + 2):
        if n < nx:
            if n == 0:
                m_gather(0)
            if n % 2 == 0 and n + 2 < nx:
                m_gather(n // 2 + 1)
            m_h(n)
        if 1 <= n <= nx:
            m_t(n - 1)
        if n >= 2:
            m_y(n - 2)
    if stop == "moe4":
        return done(pe, act, dve, pool, sp, counters)

    o_ = {n: sem_of("o_" + n) for n in ("load", "gather", "xt", "xtc", "h", "hc", "ht", "silu", "mul", "y", "yc", "store", "end", "pad")}
    moe_done = [(pe.sem, pe.count), (dve.sem, dve.count), (act.sem, act.count)] + [tuple(dsem(f"yo{p}")) for p in range(2)]
    OW = [A[:, 11264 + WC * i:11264 + WC * (i + 1)] for i in range(3)]
    o1, o3 = (w.rearrange("p (k n) -> p k n", k=8) for w in OW[0:2])
    o2 = OW[2].rearrange("p (k n) -> p k n", k=4)
    LX = CBM[0:BLK, 142:143].bitcast(U32)
    OXG, OXT, OH13, OSL, OHT, OYO = XG[0][0:BLK, :], view(2048, 8, BLK), H13[0], SL[0], HT[0], YO[0]

    def blocks(e, body):
        e.wait_ge(t_ovi[0], t_ovi[1])
        n = e.value_load(OVI[0:1, OVER:OVER + 1], min_val=0, max_val=OVER - 1)
        i = e.alloc_register()
        e.reg_mov(i, 0)
        with e.While(lambda: e.snap(i, min_val=0, max_val=OVER - 1) < n):
            at = e.snap(i, min_val=0, max_val=OVER - 2)
            body(at, at + 1)
            e.reg_add(i, i, 1)
        e.drain().then_inc(o_["end"], 1)

    def await_block(e, sem, value):
        e.wait_ge(sem, value)
        e.sem_inc(o_["pad"], 1)

    def o_sp(e):
        def body(at, done):
            await_block(e, o_["store"], done * 32)
            ex = e.value_load(OVI[0:1, bass.ds(at, 1)], min_val=0, max_val=NE - 1)
            for dst, w, k in ((o1, a["w1"], 8), (o3, a["w3"], 8), (o2, a["w2"], 4)):
                src = w.rearrange("x (k p) n -> x p k n", p=128)[bass.ds(ex, 1)].rearrange("x p k n -> (x p) k n")
                e.dma_start(dst, src).then_inc(o_["load"], 16)
            e.dma_start(LX, a["list_d"][MAIN:ROWS, :].rearrange("(x j) o -> x j o", j=BLK)[bass.ds(at, 1)].rearrange("x j o -> (x j) o")).then_inc(o_["load"], 16)
        for sem, v in moe_done:
            e.wait_ge(sem, v)
        e.sem_inc(o_["store"], 32)
        blocks(e, body)

    def o_pool(e):
        def body(at, done):
            await_block(e, o_["load"], done * 64)
            e.indirect_dma_start(OXG, None, a["n2_d"], bass.IndirectOffsetOnAxis(ap=LX, axis=0)).then_inc(o_["gather"], 16)
        blocks(e, body)

    def o_pe(e):
        def body(at, done):
            await_block(e, o_["gather"], done * 16)
            for k in range(8):
                m = e.transpose(PS[:, 0, k * BLK:(k + 1) * BLK], OXG[:, k * 128:(k + 1) * 128], C("ident", 0, BLK)[:, 0:BLK])
            m.then_inc(o_["xt"], 1)
            await_block(e, o_["xtc"], done)
            await_block(e, o_["load"], done * 64)
            for k in range(8):
                for hh, w in ((0, o1), (1, o3)):
                    m = e.matmul(PS[64 * hh:64 * hh + 64, 1, :], OXT[:, k, :], w[:, k, :], start=(k == 0), stop=(k == 7))
            m.then_inc(o_["h"], 1)
            await_block(e, o_["hc"], done)
            for j in range(4):
                m = e.transpose(PS[:, 2, j * 128:(j + 1) * 128], OH13[:, j * 128:(j + 1) * 128], ident)
            m.then_inc(o_["ht"], 1)
            await_block(e, o_["mul"], done)
            for k in range(4):
                for hh in range(2):
                    m = e.matmul(PS[64 * hh:64 * hh + 64, 3, :], OHT[:, k, :], o2[:, k, 512 * hh:512 * hh + 512], start=(k == 0), stop=(k == 3))
            m.then_inc(o_["y"], 1)
        blocks(e, body)

    def o_act(e):
        def body(at, done):
            await_block(e, o_["h"], done)
            e.activation(OH13, PS[:, 1, :], ACT.Copy).then_inc(o_["hc"], 1)
            await_block(e, o_["ht"], done)
            e.activation(OSL, PS[:, 2, :].rearrange("p (a b) -> p a b", a=4)[:, :, 0:64], ACT.Silu).then_inc(o_["silu"], 1)
            await_block(e, o_["yc"], done)
            rows = a["y_d"][MAIN:ROWS, :].rearrange("(x j) n -> x j n", j=BLK)[bass.ds(at, 1)].rearrange("x j n -> (x j) n")
            for hh in range(2):
                e.dma_start(rows[:, 512 * hh:512 * hh + 512], OYO[64 * hh:64 * hh + 64, :]).then_inc(o_["store"], 16)
        blocks(e, body)

    def o_dve(e):
        def body(at, done):
            await_block(e, o_["xt"], done)
            e.tensor_copy(OXT, PS[:, 0, :].rearrange("p (a b) -> p a b", a=8)).then_inc(o_["xtc"], 1)
            await_block(e, o_["silu"], done)
            e.tensor_tensor(OHT, OSL, PS[:, 2, :].rearrange("p (a b) -> p a b", a=4)[:, :, 64:128], ALU.mult).then_inc(o_["mul"], 1)
            await_block(e, o_["y"], done)
            e.tensor_copy(OYO, PS[:, 3, :]).then_inc(o_["yc"], 1)
        blocks(e, body)

    for q, fn in ((sp, o_sp), (pool, o_pool), (pe, o_pe), (act, o_act), (dve, o_dve)):
        q.raw(fn)
    over_done = [(o_["end"], 5)]
    def last_store(e):
        n = e.value_load(OVI[0:1, OVER:OVER + 1], min_val=0, max_val=OVER - 1)
        e.wait_ge(o_["store"], (n + 1) * 32)
        e.sem_inc(o_["end"], 1)
    sp.raw(last_store)
    over_done = [(o_["end"], 6)]

    G2 = A[:, 0:1024]
    FG = A[:, 1024:2048]
    GC = KEEP[:, 8:16]
    t = dve(lambda e: e.tensor_copy(GC, MOD[:, 40:48]), ada["tok"])
    t = act.dma(dsem("g2"), lambda e: e.dma_start(a["g2_d"].rearrange("o (k p) -> p (o k)", p=128), GC, allow_slow_non_contiguous=True), t)
    t_g2 = act.dma(dsem("g2b"), lambda e: e.dma_start(G2, a["g2_d"].broadcast_to([128, D])), t, over_done)
    t_fg = act.dma(dsem("fg"), lambda e: e.dma_start(FG, a["final_g"].broadcast_to([128, D])), over_done)
    Y = [[A[:, 11264 + 2048 * tt + 1024 * i:11264 + 2048 * tt + 1024 * (i + 1)] for i in range(2)] for tt in range(4)]
    OUT = [A[:, 20480 + 1024 * tt:20480 + 1024 * (tt + 1)] for tt in range(4)]
    SS = KEEP[:, 16:20]
    for tt in range(4):
        for i in range(2):
            ty = pool.dma(dsem(f"fy{tt}"), lambda e, tt=tt, i=i: e.indirect_dma_start(Y[tt][i], None, a["y_d"], bass.IndirectOffsetOnAxis(ap=SLOTU[:, 4 * i + tt:4 * i + tt + 1], axis=0)),
                          over_done)
        y0, y1, o = Y[tt][0], Y[tt][1], OUT[tt]
        hrow = h2t[:, tt, :]
        t = act(lambda e, y0=y0, tt=tt: e.activation(y0, y0, ACT.Copy, scale=KEEP[:, tt:tt + 1]), ty, t_wk)
        t = dve(lambda e, y0=y0, y1=y1, tt=tt: e.scalar_tensor_tensor(y0, y1, KEEP[:, 4 + tt:5 + tt], y0, ALU.mult, ALU.add), t, ty)
        t = dve(lambda e, y0=y0: e.tensor_tensor(y0, y0, G2, ALU.mult), t, t_g2)
        t = dve(lambda e, y0=y0, hrow=hrow: e.tensor_tensor(y0, y0, hrow, ALU.add), t, t_h2t)
        ts = act(lambda e, y0=y0, y1=y1, tt=tt: e.activation(y1, y0, ACT.Square, accum_out=SS[:, tt:tt + 1]), t)
        ts = act(lambda e, tt=tt: e.activation(SS[:, tt:tt + 1], SS[:, tt:tt + 1], ACT.Sqrt, scale=1.0 / D, bias=C("eps")), ts)
        ts = dve(lambda e, tt=tt: e.reciprocal(SS[:, tt:tt + 1], SS[:, tt:tt + 1]), ts)
        t = dve(lambda e, y0=y0, o=o, tt=tt: e.scalar_tensor_tensor(o, y0, SS[:, tt:tt + 1], FG, ALU.mult, ALU.mult), ts, t, t_fg)
        sp.dma(dsem("out"), lambda e, tt=tt, o=o: e.dma_start(a["out"][tt * 128:(tt + 1) * 128, :], o), t)
    return done(pe, act, dve, pool, sp, counters)


def done(pe, act, dve, pool, sp, counters):
    sp.wait(*[(c[0], c[1]) for c in counters.values()])
    sp.wait((pe.sem, pe.count), (act.sem, act.count), (dve.sem, dve.count), (pool.sem, pool.count))


def shape_constants():
    i = np.arange(128)
    c = np.zeros((128, CN), np.float32)

    def put(name, x):
        at, n = CO[name]
        c[:, at:at + n] = x

    put("ident", np.eye(128))
    put("ones", 1.0)
    put("bones", (i[:, None] // 64 == i[None] // 64))
    put("ustrict", i[:, None] < i[None])
    put("cmask", np.where(i[None] <= i[:, None], 0.0, -1e30))
    put("smask", i[None] >= i[:, None])
    put("iota8", np.arange(8)[None])
    put("iota64", np.arange(64)[None])
    put("tok", i[:, None] + 128 * np.arange(4)[None])
    put("eps", EPS)
    put("sel4", (i[:, None] % 32 == 0))
    put("sel16", (i[:, None] % 32 == np.arange(16)[None]))
    return c


def lay_params(x):
    p = np.zeros((128, PN), np.float32)

    def put(name, v, rows=128):
        at, n = PO[name]
        p[:rows, at:at + n] = v

    col = lambda v: np.asarray(v).reshape(-1, 128).T
    put("attn_norm", col(x["attn_norm"]))
    put("ffn_norm", col(x["ffn_norm"]))
    put("final_norm", col(x["final_norm"]))
    put("qg", np.tile(x["fox_q_norm"][0], 2)[:, None])
    put("kg", np.tile(x["fox_k_norm"][0], 2)[:, None])
    put("bf", x["fox_b_f"][0][:, None], 16)
    put("norm1", col(x["norm1_g_2"]))
    put("cvw", x["cv_dw_w_2"][0].T.reshape(8, 128, 31).transpose(1, 0, 2).reshape(128, 248))
    put("cvb", col(x["cv_dw_b_2"]))
    put("lng", col(x["cv_ln_g_2"]))
    put("lnb", col(x["cv_ln_b_2"]))
    put("scw", x["ssm_conv_w_2"][0].T.reshape(24, 128, 4).transpose(1, 0, 2).reshape(128, 96))
    put("scb", col(x["ssm_conv_b_2"]))
    put("dtb", x["dt_bias_2"][0][:, None], 32)
    put("alog", x["a_log_2"][0][:, None], 32)
    put("dsk", np.repeat(x["d_skip_2"][0].reshape(16, 2).T, 64, axis=0))
    put("sng", col(x["ssm_norm_g_2"]))
    put("norm2", col(x["norm2_g_2"]))
    put("c", col(x["c_2"]))
    put("bada", col(x["b_ada_2"]))
    put("rb", np.broadcast_to(np.concatenate([x["b_grp_2"][0], x["b_er_2"][0]])[None], (128, 72)))
    put("wf", x["fox_w_in"][0][:, 4096:4112].reshape(8, 128, 16).transpose(1, 0, 2).reshape(128, 128))
    put("wdt", x["w_in_2"][0][:, 7168:7200].reshape(8, 128, 32).transpose(1, 0, 2).reshape(128, 256))
    return p


def arrays(x):
    xt = np.concatenate([x["meta_tokens"], x["x"][0]], axis=0)
    return {
        "consts": shape_constants(),
        "params": lay_params(x),
        "xT": np.ascontiguousarray(xt.T.reshape(8, 128, L).transpose(1, 0, 2)),
        "rw": np.ascontiguousarray(np.concatenate([x["w_grp_2"][0], x["w_er_2"][0]], axis=1).reshape(8, 128, 72).transpose(1, 0, 2)),
        "fox_w_in": x["fox_w_in"][0], "fox_w_out": x["fox_w_out"][0], "ffn_w_in": x["ffn_w_in"][0], "ffn_w_out": x["ffn_w_out"][0],
        "w_ada": x["w_ada_2"][0], "w_in": x["w_in_2"][0], "w_cv_out": x["w_cv_out_2"][0], "w_ssm_out": x["w_ssm_out_2"][0],
        "w_mix_out": x["w_mix_out_2"][0], "w1": x["w1_2"][0], "w3": x["w3_2"][0], "w2": x["w2_2"][0],
        "final_g": x["final_g_2"].reshape(1, D),
    }


def declare(nc, arr):
    a = {k: nc.dram_tensor("in_" + k, v.shape, mybir.dt.from_np(v.dtype), kind="ExternalInput").ap() for k, v in arr.items()}
    a["out"] = nc.dram_tensor("out_0", (T, D), F32, kind="ExternalOutput").ap()
    for name, shape, dt in (("x2_d", (128, 8, T), F32), ("ymix_d", (128, 8, T), F32), ("y01_d", (128, 8, T), F32), ("n2_d", (T, D), F32), ("g2_d", (1, D), F32),
                            ("list_d", (ROWS, 1), U32), ("y_d", (ROWS, D), F32)):
        a[name] = nc.dram_tensor(name, shape, dt).ap()
    return a


def kernel(**inputs):
    from concourse import bacc
    from concourse.bass_utils import run_bass_kernel_spmd

    arr = {k: np.ascontiguousarray(v) for k, v in arrays({k: np.asarray(v) for k, v in inputs.items()}).items()}
    nc = bacc.Bacc("TRN2", target_bir_lowering=False, num_devices=1)
    a = declare(nc, arr)
    build_program(nc, a)
    r = run_bass_kernel_spmd(nc, [{"in_" + k: v for k, v in arr.items()}], core_ids=[0])
    return r.results[0]["out_0"].reshape(1, T, D)
```

```python
from collections import deque
from contextlib import ExitStack

import numpy as np
import concourse.bass as bass
from concourse import mybir

F32 = mybir.dt.float32
U32 = mybir.dt.uint32
I32 = mybir.dt.int32
F32R = mybir.dt.float32r
ALU = mybir.AluOpType
ACT = mybir.ActivationFunctionType
AX = mybir.AxisListType.X

T = 512
NM = 16
L = T + NM
D = 1024
FH = 2816
EPS = 1e-6
NE = 64
BLK = 64
MAIN = NE * BLK
OVER = 16
ROWS = MAIN + OVER * BLK
WC = 4096

CONST_COLS = [("ident", 128), ("ones", 128), ("bones", 128), ("ustrict", 128), ("cmask", 128), ("smask", 128),
              ("iota8", 8), ("iota64", 64), ("tok", 4), ("eps", 1), ("sel4", 1), ("sel16", 16)]
PARAM_COLS = [("attn_norm", 8), ("ffn_norm", 8), ("final_norm", 8), ("qg", 1), ("kg", 1), ("bf", 1), ("norm1", 8),
              ("cvw", 248), ("cvb", 8), ("lng", 8), ("lnb", 8), ("scw", 96), ("scb", 24), ("dtb", 1), ("alog", 1),
              ("dsk", 16), ("sng", 16), ("norm2", 8), ("c", 8), ("bada", 48), ("rb", 72), ("wf", 128), ("wdt", 256)]


PARTS_AT = [(4224, 4096), (25984, 4096), (8448, 4224), (17792, 4096), (8320, 4096), (12416, 6144), (18560, 6144), (0, 4096), (4096, 4096), (8192, 4096), (12528, 4096), (12288, 4096), (28672, 4096), (16384, 4096), (24576, 4096)]


def offsets(cols):
    out, at = {}, 0
    for name, n in cols:
        out[name] = (at, n)
        at += n
    return out, at


CO, CN = offsets(CONST_COLS)
PO, PN = offsets(PARAM_COLS)


class Queue:

    def __init__(self, engine, sem):
        self.engine, self.sem, self.count, self.seen = engine, sem, 0, {}

    def wait(self, *toks):
        for tok in toks:
            if tok is None:
                continue
            if isinstance(tok, list):
                self.wait(*tok)
                continue
            sem, value = tok
            if self.seen.get(id(sem), 0) < value:
                self.seen[id(sem)] = value
                if self.engine is not None:
                    self.engine.wait_ge(sem, value)

    def __call__(self, fn, *toks, inc=True):
        self.wait(*toks)
        self.count += inc
        if self.engine is not None:
            ins = fn(self.engine)
            if inc:
                ins.then_inc(self.sem, 1)
        return (self.sem, self.count)

    def raw(self, fn):
        if self.engine is not None:
            fn(self.engine)

    def dma(self, counter, fn, *toks):
        self.wait(*toks)
        counter[1] += 16
        if self.engine is not None:
            fn(self.engine).then_inc(counter[0], 16)
        return (counter[0], counter[1])


def build_program(nc, a, stop=None):
    with ExitStack() as ctx:
        made = {}

        def tensor(name, shape, dt=F32):
            if name not in made:
                made[name] = ctx.enter_context(nc.sbuf_tensor(name, shape, dt))
            return made[name]

        def semaphore(name):
            if name not in made:
                made[name] = ctx.enter_context(nc.semaphore(name))
            return made[name]

        for name, off, n in [(f"r{off}", off, n) for off, n in PARTS_AT] + [("ring_r", 32768 + 2 * WC, 2 * WC)]:
            with ExitStack() as under:
                if off:
                    under.enter_context(nc.sbuf_tensor("before_" + name, [128, off], F32))
                made[name] = under.enter_context(nc.sbuf_tensor(name, [128, n], F32R))
        PS = ctx.enter_context(nc.psum_tensor("ps", [128, 8, 512], F32))
        program(a, tensor, semaphore, PS, {}, stop)
        block = ctx.enter_context(nc.Block())

        @block.sync
        def _(e):
            program(a, tensor, semaphore, PS, {"sp": e}, stop)

        @block.tensor
        def _(e):
            program(a, tensor, semaphore, PS, {"pe": e}, stop)

        @block.scalar
        def _(e):
            program(a, tensor, semaphore, PS, {"act": e}, stop)

        @block.vector
        def _(e):
            program(a, tensor, semaphore, PS, {"dve": e}, stop)

        @block.gpsimd
        def _(e):
            program(a, tensor, semaphore, PS, {"pool": e}, stop)


def program(a, sb, sem_of, PS, engines, stop):
    pe, act, dve, pool, sp = (Queue(engines.get(n), sem_of(f"s_{n}")) for n in ("pe", "act", "dve", "pool", "sp"))
    counters = {}

    def dsem(name):
        if name not in counters:
            counters[name] = [sem_of("d_" + name), 0]
        return counters[name]

    A = sb("arena", [128, 32768])
    RG = sb("ring", [128, 4 * WC])
    CS = sb("consts_sb", [128, CN])
    PR = sb("params_sb", [128, PN])
    SCR = sb("scr", [128, 1640])
    CBM = sb("cbm", [128, 512])
    RR = sb("ring_r", None)
    PSF = PS[:, :, :].rearrange("p a b -> p (a b)")

    def C(name, r0=0, r1=128):
        at, n = CO[name]
        return CS[r0:r1, at:at + n]

    def P(name, r0=0, r1=128):
        at, n = PO[name]
        return PR[r0:r1, at:at + n]

    def pc(name, k, r0=0, r1=128):
        at, n = PO[name]
        return PR[r0:r1, at + k:at + k + 1]

    def parts_at(off, n):
        return sb(f"r{off}", None)[:, :].rearrange("p (a b) -> p a b", a=n)

    def view(off, *dims):
        n = int(np.prod(dims))
        v = A[:, off:off + n]
        if len(dims) == 2:
            v = v.rearrange("p (a b) -> p a b", a=dims[0])
        if len(dims) == 3:
            v = v.rearrange("p (a b c) -> p a b c", a=dims[0], b=dims[1])
        return v

    ident, ones, bones = C("ident"), C("ones"), C("bones")

    class Slot:
        def __init__(self, ap, name):
            self.ap, self.free, self.counter, self.busy = ap, [], dsem(name), False

    ring = deque(Slot(RG[:, i * WC:(i + 1) * WC], f"w{i}") for i in range(2))

    def fetch(*parts):
        slot = ring.popleft()
        assert not slot.busy
        ring.append(slot)
        tok = None
        for off, shape, src in parts:
            n = int(np.prod(shape))
            dst = slot.ap[:, off:off + n].rearrange("p (a b) -> p a b", a=shape[0])
            tok = sp.dma(slot.counter, lambda e, dst=dst, src=src: e.dma_start(dst, src), slot.free)
        slot.free = []
        return slot, tok

    def wrows(w, r0, nk, c0, nc_):
        return w[r0:r0 + nk * 128, c0:c0 + nc_].rearrange("(k p) n -> p k n", p=128)

    def fetch_w(w, c0, ncol=512, r0=0, nk=8):
        slot, tok = fetch((0, (nk, ncol), wrows(w, r0, nk, c0, ncol)))
        return slot, tok, slot.ap[:, :nk * ncol].rearrange("p (k n) -> p k n", k=nk)

    class Gran:
        def __init__(self, i):
            o = 2048 * i
            self.H, self.L, self.free = RR[:, o:o + 1024], RR[:, o + 1024:o + 2048], []

    grans, plan, ready = deque(Gran(i) for i in range(4)), deque(), deque()
    chunk = {"slot": None, "tok": None, "todo": deque()}

    def split(hi, lo, x, *toks, by=pool):
        t = act(lambda e: e.activation(hi, x, ACT.Copy), *toks)
        return by(lambda e: e.tensor_tensor(lo, x, hi.bitcast(F32), ALU.subtract), t, *toks)

    def feed(ahead=4):
        while len(ready) < ahead and (plan or chunk["todo"]):
            if not chunk["todo"]:
                parts, views = plan.popleft()
                chunk["slot"], chunk["tok"] = fetch(*parts) if parts else (None, t_param)
                if parts:
                    chunk["slot"].busy = True
                chunk["todo"] = deque(views)
            raw = chunk["todo"].popleft()
            slot = chunk["slot"]
            if slot is not None:
                raw = raw(slot.ap)
            g = grans.popleft()
            grans.append(g)
            _, nk, n = raw.shape
            H, L = (x[:, :nk * n].rearrange("p (k n) -> p k n", k=nk) for x in (g.H, g.L))
            t = split(H, L, raw, chunk["tok"], g.free)
            if slot is not None and not chunk["todo"]:
                slot.free.append(t)
                slot.busy = False
            ready.append((g, H, L, t, slot, chunk["tok"]))

    def gran():
        feed()
        return ready.popleft()

    def plan_w(w, c0, r0=0, nk=8):
        plan.append(([(0, (nk, 512), wrows(w, r0, nk, c0, 512))],
                     [lambda ap, j=j: ap[:, :nk * 512].rearrange("p (k n) -> p k n", k=nk)[:, :, j * 128:(j + 1) * 128] for j in range(4)]))

    def plan_two(w, c0, c1):
        plan.append(([(2048 * i, (8, 256), wrows(w, 0, 8, c, 256)) for i, c in enumerate((c0, c1))],
                     [lambda ap, j=j, i=i: ap.rearrange("p (g k n) -> p g k n", g=2, k=8)[:, i, :, j * 128:(j + 1) * 128] for j in range(2) for i in range(2)]))

    def plan_tiles(*tiles):
        plan.append(([(1024 * i, (8, 128), wrows(w, 0, 8, c, 128)) for i, (w, c) in enumerate(tiles)],
                     [lambda ap, i=i: ap[:, 1024 * i:1024 * (i + 1)].rearrange("p (k n) -> p k n", k=8) for i in range(len(tiles))]))

    fw, wi = a["fox_w_in"], a["w_in"]
    for c in range(2):
        plan_w(fw, 1024 + 512 * c)
    plan.append((None, [P("wf").rearrange("p (k n) -> p k n", k=8)]))
    for c in range(2):
        plan.append(([(0, (8, 512), wrows(fw, 0, 8, 2048 + 512 * c, 512))],
                     [lambda ap, j=j: ap.rearrange("p (k n) -> p k n", k=8)[:, 2 * j:2 * j + 2, :] for j in range(4)]))
    for c in range(2):
        plan_w(fw, 512 * c)
    for c in range(2):
        plan_w(fw, 3072 + 512 * c)
    for c in range(2):
        plan_w(a["fox_w_out"], 512 * c)
    NG = 6
    HALVES = [(0, 12), (12, 10)]
    for k0, n in HALVES:
        for nt in range(k0, k0 + n, 2):
            plan_two(a["ffn_w_in"], 128 * nt, FH + 128 * nt)
        for c in range(2):
            plan_w(a["ffn_w_out"], 512 * c, r0=128 * k0)
            plan_w(a["ffn_w_out"], 512 * c, r0=128 * (k0 + 8), nk=n - 8)
    for nt in range(8):
        plan_tiles((wi, 1024 + 128 * nt), (wi, 128 * nt), (wi, 6144 + 128 * nt), (wi, 7200 + 128 * nt))
        if nt == 0:
            plan.append((None, [P("wdt").rearrange("p (k n) -> p k n", k=8)]))
    plan_tiles(*[(wi, 8224 + 128 * i) for i in range(4)])
    plan_tiles(*[(wi, 8224 + 128 * i) for i in range(4, NG)])
    for c in range(2):
        plan_w(a["w_cv_out"], 512 * c)
    for g_ in range(4):
        plan_w(wi, 4096 + 512 * g_)
        plan_w(wi, 2048 + 512 * g_)
    plan_tiles(*[(wi, 8224 + 128 * i) for i in range(NG, 8)])
    for c in range(2):
        plan_w(a["w_ssm_out"], 512 * c, r0=1024)
        plan_w(a["w_ssm_out"], 512 * c)
    for c in range(2):
        plan_w(a["w_mix_out"], 512 * c)

    def mm3(out, g, X, toks, start=True, stop=True, k0=0):
        _, WH, WL, tw = g[:4]
        nk = WH.shape[1]
        tok = None
        for k in range(nk):
            XH, XL, tx = X(k0 + k)
            for i, (w, x) in enumerate(((WH, XH), (WH, XL), (WL, XH))):
                s, e_ = start and k == 0 and i == 0, stop and k == nk - 1 and i == 2
                tok = pe(lambda e, w=w, x=x, k=k, s=s, e_=e_: e.matmul(out, w[:, k, :], x, start=s, stop=e_), tw, tx, toks, inc=(k == nk - 1 and i == 2))
        g[0].free = [tok]
        return tok

    def tile(X, m=128, n=512):
        b = bank()
        return b, mm3(PS[0:m, b, :n], gran(), X, bank_free[b])

    bank_free = [[] for _ in range(8)]
    turn, held = [0], set()

    def bank(n=1, among=None):
        if among is None:
            while turn[0] % 8 in held:
                turn[0] += 1
            b = turn[0] % 8
            turn[0] += 1
        else:
            b = among[turn[0] % len(among)]
            turn[0] += 1
        return b

    def mms(out, pairs, *toks, start=True, stop=True, inc=True):
        tok = None
        for i, (lt, r) in enumerate(pairs):
            last = i == len(pairs) - 1
            tok = pe(lambda e, lt=lt, r=r, s=(start and i == 0), t=(stop and last): e.matmul(out, lt, r, start=s, stop=t),
                     *(toks if i == 0 else ()), inc=inc and last)
        return tok

    t_const = act.dma(dsem("const"), lambda e: e.dma_start(CS[:, :], a["consts"]))
    t_xk = [act.dma(dsem(f"x{i}"), lambda e, i=i: e.dma_start(view(0, 8, L)[:, 2 * i:2 * i + 2, :], a["xT"][:, 2 * i:2 * i + 2, :])) for i in range(4)]
    t_param = act.dma(dsem("param"), lambda e: e.dma_start(PR[:, :], a["params"]))
    sp.wait(*t_xk[0:3])

    hT = view(0, 8, L)
    hnH, hnL = parts_at(4224, 8), parts_at(25984, 8)
    hnm = CBM[:, 0:256].rearrange("p (a b) -> p a b", a=8)
    kT = view(8448, 8, L)
    v = view(13696, 4, D)
    vm = view(31184, 1, D)[0:NM, 0, :]
    qT = view(17792, 8, T)
    gT = view(21888, 8, T)
    oH, oL = sb("r8448", None)[:, :].rearrange("p (a b) -> p a b", a=8)[:, :, 0:T], parts_at(17792, 8)

    ZERO = view(21888, 1, D)[:, 0, :]
    t_zero = pool(lambda e: e.memset(ZERO, 0.0))

    def zero_rows():
        for i in range(OVER * BLK // 128):
            tz = act.dma(dsem("zy"), lambda e, i=i: e.dma_start(a["y_d"][MAIN + 128 * i:MAIN + 128 * i + 128, :], ZERO), t_zero)
        return tz

    t_zl = pool.dma(dsem("zl"), lambda e: e.dma_start(a["list_d"].rearrange("(p n) o -> p (n o)", p=128), ZERO[:, 0:ROWS // 128].bitcast(U32)), t_zero)

    TMP = [SCR[:, 0:528], SCR[:, 528:1056]]
    RST = SCR[:, 1056:1584]
    tmp_free = [[], []]
    tmp_turn = [0]

    def take_tmp():
        i = tmp_turn[0] % 2
        tmp_turn[0] += 1
        return i, TMP[i], tmp_free[i]

    rst_free = []

    def colsum(src, nk, segs, mat, tok_of, square=True):
        banks = [bank() for _ in segs]
        tok = None
        for k in range(nk):
            if square:
                i, tmp, free = take_tmp()
                n = segs[-1][0] + segs[-1][1]
                s = src(k)
                t_sq = act(lambda e, tmp=tmp, s=s, n=n: e.activation(tmp[:, :n], s, ACT.Square), tok_of(k), free)
                m, ready = tmp, t_sq
            else:
                m, ready = src(k), tok_of(k)
            for b, (s0, n) in zip(banks, segs):
                tok = pe(lambda e, b=b, m=m, s0=s0, n=n, k=k: e.matmul(PS[:, b, :n], mat, m[:, s0:s0 + n], start=(k == 0), stop=(k == nk - 1)),
                         ready, bank_free[b] if k == 0 else None, t_const, inc=True)
            if square:
                tmp_free[i] = [tok]
        return banks, tok

    def rstd(banks, segs, scale, tok, out=None):
        out = RST if out is None else out
        t = None
        for b, (s0, n) in zip(banks, segs):
            t = act(lambda e, b=b, s0=s0, n=n: e.activation(out[:, s0:s0 + n], PS[:, b, :n], ACT.Sqrt, scale=scale, bias=C("eps")),
                    tok, rst_free)
            bank_free[b] = [t]
        n = segs[-1][0] + segs[-1][1]
        return dve(lambda e: e.reciprocal(out[:, :n], out[:, :n]), t)

    def rms_to(dst, src, nk, segs, scale, gain, tok_of, extra=None):
        banks, tok = colsum(src, nk, segs, ones, tok_of)
        t = rstd(banks, segs, scale, tok)
        n = segs[-1][0] + segs[-1][1]
        out = []
        for k in range(nk):
            out.append(dve(lambda e, k=k: e.scalar_tensor_tensor(dst(k), src(k), gain(k), RST[:, :n], ALU.mult, ALU.mult),
                           t, t_param, extra, tok_of(k)))
        rst_free[:] = [out[-1]]
        return out

    SC = SCR[:, 1584:1592]
    MOD = SCR[:, 1592:1640]
    ada = {"n": 0, "tok": None}
    ADAP = view(30080, 1, 512)[:, 0, :]
    ada_free = []

    def ada_step():
        n = ada["n"]
        if n == 12:
            return
        ada["n"] += 1
        slot, tw, w = fetch_w(a["w_ada"], n * 512)
        b = bank()
        tok = None
        for k in range(8):
            g = k % 4
            tok = pe(lambda e, k=k, g=g, w=w, b=b: e.matmul(PS[32 * g:32 * g + 32, b, :], SC[:, k:k + 1].broadcast_to([128, 32]), w[:, k, :],
                                                       start=(k < 4), stop=(k >= 4)),
                     tw, t_sc, bank_free[b] if k == 0 else None, inc=(k == 7))
        slot.free = [tok]
        t = act(lambda e, b=b: e.activation(ADAP, PS[:, b, :], ACT.Copy), tok, ada_free)
        bank_free[b] = [t]
        b2 = bank()
        for j in range(4):
            tok = pe(lambda e, j=j, b2=b2: e.matmul(PS[:, b2, j:j + 1], ADAP[:, j * 128:(j + 1) * 128], C("sel4"), start=True, stop=True),
                     t, bank_free[b2] if j == 0 else None, t_const, inc=(j == 3))
        ada_free[:] = [tok]
        o = PO["bada"][0] + 4 * n
        t = dve(lambda e, b2=b2, n=n, o=o: e.tensor_tensor(MOD[:, 4 * n:4 * n + 4], PS[:, b2, 0:4], PR[:, o:o + 4], ALU.add), tok, t_param)
        bank_free[b2] = [t]
        ada["tok"] = t

    SEGL = [(0, 512), (512, 16)]
    SEGT = [(0, 512)]
    banks, tok = colsum(lambda k: hT[:, k, :], 8, SEGL, ones, lambda k: t_xk[k // 2])
    t = rstd(banks, SEGL, 1.0 / D, tok)
    feed(2)
    t_hn = []
    for k in range(8):
        i, tmp, free = take_tmp()
        t1 = dve(lambda e, k=k, tmp=tmp: e.scalar_tensor_tensor(tmp, hT[:, k, :], pc("attn_norm", k), RST, ALU.mult, ALU.mult), t, t_param, free)
        t_hm = dve(lambda e, k=k, tmp=tmp: e.tensor_copy(hnm[:, k, :], tmp[:, 0:32]), t1)
        t_hn.append(split(hnH[:, k, :], hnL[:, k, :], tmp[:, NM:L], t1, by=(pool, dve)[k % 2]))
        tmp_free[i] = [t_hn[-1], t_hm]
    rst_free[:] = [t1]
    XN = lambda k: (hnH[:, k, :], hnL[:, k, :], t_hn[k])

    def meta_rows(g):
        slot, tw = g[4:6]
        w = slot.ap.rearrange("p (k n) -> p k n", k=8)
        b = bank()
        for k in range(8):
            r = 32 * (k % 4)
            tok = pe(lambda e, k=k, r=r: e.matmul(PS[r:r + 32, b, :], hnm[:, k, :], w[:, k, :], start=(k < 4), stop=(k >= 4)),
                     tw, t_hm, bank_free[b] if k == 0 else None, inc=(k == 7))
        slot.free.append(tok)
        t = act(lambda e: e.activation(ADAP, PS[:, b, :], ACT.Copy), tok, ada_free)
        bank_free[b] = [t]
        return t

    norms, norm_now = deque(), []
    t_k, t_q = [None] * 8, [None] * 8

    def norm_step():
        if norm_now:
            x, nt, n, segs, gain, i, tmp, t_sq, t_raw, res = norm_now.pop()
            bs = [bank() for _ in segs]
            for b, (s0, m) in zip(bs, segs):
                tok = pe(lambda e, b=b, s0=s0, m=m: e.matmul(PS[:, b, :m], bones, tmp[:, s0:s0 + m], start=True, stop=True), t_sq, bank_free[b], t_const)
            tmp_free[i] = [tok]
            t = rstd(bs, segs, 1.0 / 64, tok)
            t = dve(lambda e: e.scalar_tensor_tensor(x[:, nt, :], x[:, nt, :], gain, RST[:, :n], ALU.mult, ALU.mult), t, t_param, t_qg, t_raw)
            rst_free[:] = [t]
            res[nt] = t
        if norms:
            x, nt, n, segs, gain, t_raw, res = norms.popleft()
            i, tmp, free = take_tmp()
            t_sq = act(lambda e: e.activation(tmp[:, :n], x[:, nt, :], ACT.Square), t_raw, free)
            norm_now.append((x, nt, n, segs, gain, i, tmp, t_sq, t_raw, res))

    t_zy = zero_rows()
    t_sc = act(lambda e: e.activation(SC, P("c"), ACT.Silu), t_param)
    t_qg = dve(lambda e: e.tensor_scalar(pc("qg", 0), pc("qg", 0), 0.125, None, ALU.mult), t_param)
    SEL16 = C("sel16")
    t_kraw = [None] * 8
    for c in range(2):
        feed()
        t_m = meta_rows(ready[0])
        for j in range(4):
            nt = 4 * c + j
            b, tok = tile(XN)
            t = act(lambda e, b=b, nt=nt: e.activation(kT[:, nt, NM:L], PS[:, b, :], ACT.Copy), tok)
            bank_free[b] = [t]
            t_kraw[nt] = t
            norm_step()
        b = bank()
        for j in range(4):
            tok = pe(lambda e, b=b, j=j: e.matmul(PS[:, b, 16 * j:16 * j + 16], ADAP[:, j * 128:(j + 1) * 128], SEL16, start=True, stop=True),
                     t_m, bank_free[b], t_const, inc=(j == 3))
        ada_free[:] = [tok]
        t = dve(lambda e, b=b, c=c: e.tensor_copy(kT[:, 4 * c:4 * c + 4, 0:NM], PS[:, b, 0:64].rearrange("p (a b) -> p a b", a=4)), tok)
        bank_free[b] = [t]
        for j in range(4):
            norms.append((kT, 4 * c + j, L, SEGL, pc("kg", 0), [t_kraw[4 * c + j], t], t_k))
        ada_step()
    wf = P("wf").rearrange("p (k n) -> p k n", k=8)
    FL = view(30656, 4, L)[0:16]
    t = None
    b = bank()
    g = gran()
    tok = mm3(PS[0:16, b, :], g, XN, bank_free[b])
    t = act(lambda e, b=b: e.activation(FL[:, 0, NM:L], PS[0:16, b, :], ACT.Identity, bias=P("bf", 0, 16)), tok)
    bank_free[b] = [t]
    b = bank()
    tok = mms(PS[0:16, b, :NM], [(wf[:, k, :], hnm[:, k, 0:NM]) for k in range(8)], t_param, t_hm, bank_free[b])
    t = act(lambda e, b=b: e.activation(FL[:, 0, 0:NM], PS[0:16, b, :NM], ACT.Identity, bias=P("bf", 0, 16)), tok)
    bank_free[b] = [t]

    def log1p_exp(z, u, s, q, tok, rows):
        t = dve(lambda e: e.tensor_scalar(u, z, -1.0, None, ALU.mult), tok)
        t = dve(lambda e: e.tensor_tensor(u, u, z, ALU.min), t)
        t = act(lambda e: e.activation(u, u, ACT.Exp), t)
        t = dve(lambda e: e.tensor_scalar(s, u, 2.0, None, ALU.add), t)
        t = dve(lambda e: e.reciprocal(s, s), t)
        t = dve(lambda e: e.tensor_tensor(u, u, s, ALU.mult), t)
        t = dve(lambda e: e.tensor_tensor(s, u, u, ALU.mult), t)
        t = dve(lambda e: e.tensor_scalar(q, s, 1.0 / 17, None, ALU.mult), t)
        for c in (15, 13, 11, 9, 7, 5, 3):
            t = dve(lambda e, c=c: e.scalar_tensor_tensor(q, q, 1.0 / c, s, ALU.add, ALU.mult), t)
        t = dve(lambda e: e.scalar_tensor_tensor(q, q, 1.0, u, ALU.add, ALU.mult), t)
        return dve(lambda e: e.tensor_scalar(q, q, 2.0, None, ALU.mult), t)

    t = log1p_exp(FL[:, 0, :], FL[:, 1, :], FL[:, 2, :], FL[:, 3, :], t, 16)
    t = dve(lambda e: e.scalar_tensor_tensor(FL[:, 1, :], FL[:, 0, :], 0.0, FL[:, 3, :], ALU.min, ALU.subtract), t)
    cT = FL[:, 0, :]
    t_c = dve(lambda e: e.tensor_tensor_scan(cT, C("ones", 0, 16)[:, 0:1].broadcast_to([16, L]), FL[:, 1, :], 0.0, ALU.mult, ALU.add), t)
    CQ = CBM[:, 384:448].rearrange("p (a b) -> p a b", a=4)
    t_cq = [None]

    def queries_c():
        b = bank()
        for tt in range(4):
            tok = pe(lambda e, tt=tt, b=b: e.transpose(PS[:, b, tt * 16:tt * 16 + 16], cT[:, NM + tt * 128:NM + tt * 128 + 128], C("ident", 0, 16)[:, 0:16]),
                     t_c, bank_free[b], t_const, inc=(tt == 3))
        t_cq[0] = dve(lambda e, b=b: e.tensor_copy(CQ, PS[:, b, 0:64].rearrange("p (a b) -> p a b", a=4)), tok)
        bank_free[b] = [t_cq[0]]

    for c in range(2):
        feed()
        t_m = meta_rows(ready[0])
        bs = [bank() for _ in range(4)]
        held.update(bs)
        for kk in range(4):
            g = gran()
            for tt in range(4):
                for k in range(2):
                    kx = 2 * kk + k
                    sl = slice(tt * 128, (tt + 1) * 128)
                    for i, (x, w) in enumerate(((hnH, g[1]), (hnL, g[1]), (hnH, g[2]))):
                        last = kx == 7 and i == 2
                        tok = pe(lambda e, x=x, w=w, k=k, kx=kx, sl=sl, i=i, last=last, b=bs[tt]: e.matmul(PS[:, b, :], x[:, kx, sl], w[:, k, :], start=(kx == 0 and i == 0), stop=last),
                                 g[3], t_hn[kx], bank_free[bs[tt]] if kx == 0 else None, inc=last or (tt == 3 and k == 1 and i == 2))
                if kk == 3:
                    t_v = act(lambda e, b=bs[tt], tt=tt, c=c: e.activation(v[:, tt, c * 512:(c + 1) * 512], PS[:, b, :], ACT.Copy), tok)
                    bank_free[bs[tt]] = [t_v]
            g[0].free = [tok]
            norm_step()
        held.clear()
        b = bank()
        tok = pe(lambda e, b=b: e.matmul(PS[0:16, b, :], SEL16, ADAP, start=True, stop=True), t_m, bank_free[b], t_const)
        ada_free[:] = [tok]
        t_vm = dve(lambda e, b=b, c=c: e.tensor_copy(vm[:, c * 512:(c + 1) * 512], PS[0:16, b, :]), tok, t_c)
        bank_free[b] = [t_vm]
        ada_step()
    t_v = [t_v, t_vm]
    queries_c()
    t_qraw = [None] * 8
    for c in range(2):
        for j in range(4):
            nt = 4 * c + j
            b, tok = tile(XN)
            t = act(lambda e, b=b, nt=nt: e.activation(qT[:, nt, :], PS[:, b, :], ACT.Copy), tok)
            bank_free[b] = [t]
            norm_step()
            norms.append((qT, nt, T, SEGT, pc("qg", 0), t, t_q))
        ada_step()

    if stop == "qkv":
        return done(pe, act, dve, pool, sp, counters)

    t_g = [None] * 8

    def gate_out(nt, b, tok):
        t_g[nt] = act(lambda e: e.activation(gT[:, nt, :], PS[:, b, :], ACT.Sigmoid), tok, t_zy, t_zl)
        bank_free[b] = [t_g[nt]]

    for nt in range(2):
        b, tok = tile(XN)
        gate_out(nt, b, tok)
        norm_step()
    ada_step()
    while norms or norm_now:
        norm_step()

    NCK = [A[:, 32240:32768], A[:, 30080:30608]]
    PB = [TMP[0], TMP[1], RST]
    PT = [A[:, 12672 + 512 * i:13184 + 512 * i] for i in range(2)]
    PTM = [CBM[0:NM, 128 * i:128 * i + 128] for i in range(2)]
    NMX, SUM = CBM[:, 256:320], CBM[:, 320:384]
    proj_done = [(pe.sem, pe.count), t_c, t_v]
    nck_free = [[proj_done], [proj_done]]
    pb_free = [tmp_free[0] + [proj_done], tmp_free[1] + [proj_done], rst_free + [proj_done]]
    pt_free = [[proj_done], [proj_done]]
    st = {}
    NCKTOK = [None, None]
    aux = [0]

    def aux_bank():
        b = 4 + aux[0] % 2
        aux[0] += 1
        return b

    def at_s(n):
        h, qt = divmod(n, 4)
        i, off = h // 2, 64 * (h % 2)
        if qt == 0:
            ba = aux_bank()
            sl = C("ident", 0, 16)[:, h:h + 1].broadcast_to([16, 128])
            tok = pe(lambda e: e.matmul(PS[:, ba, :], sl, cT[:, 0:512], start=True, stop=True), bank_free[ba], t_c, t_const)
            u = h % 2
            t1 = act(lambda e: e.activation(NCK[u][:, 0:512], PS[:, ba, :], ACT.Copy, scale=-1.0), tok, nck_free[u])
            bank_free[ba] = [t1]
            ba = aux_bank()
            tok = pe(lambda e, ba=ba: e.matmul(PS[:, ba, 0:16], sl, cT[:, 512:528], start=True, stop=True), bank_free[ba])
            t1 = act(lambda e, ba=ba: e.activation(NCK[u][:, 512:528], PS[:, ba, 0:16], ACT.Copy, scale=-1.0), tok)
            bank_free[ba] = [t1]
            NCKTOK[u] = t1
        pr = (n % 2) * 2
        ln = NM + 128 * (qt + 1)
        q = qT[off:off + 64, i, qt * 128:(qt + 1) * 128]
        m = min(ln, 512)
        tok = pe(lambda e: e.matmul(PS[:, pr, 0:m], q, kT[off:off + 64, i, 0:m], start=True, stop=True),
                 bank_free[pr], t_q[i], t_k[i])
        if ln > 512:
            tok = pe(lambda e: e.matmul(PS[:, pr + 1, 0:ln - 512], q, kT[off:off + 64, i, 512:ln], start=True, stop=True), bank_free[pr + 1])
        pb = PB[n % 3]
        S = PSF[:, pr * 512:pr * 512 + ln]
        u = h % 2
        t = dve(lambda e: e.scalar_tensor_tensor(pb[:, :ln], S, CQ[:, qt, h:h + 1], NCK[u][:, :ln], ALU.add, ALU.add),
                tok, NCKTOK[u], t_cq, pb_free[n % 3])
        bank_free[pr] = [t]
        if ln > 512:
            bank_free[pr + 1] = [t]
        if qt == 3:
            nck_free[u] = [t]
        t = dve(lambda e: e.tensor_tensor(pb[:, ln - 128:ln], pb[:, ln - 128:ln], C("cmask"), ALU.add), t)
        t = dve(lambda e: e.tensor_reduce(NMX[:, n:n + 1], pb[:, :ln], AX, ALU.max, negate=True), t)
        t = act(lambda e: e.activation(pb[:, :ln], pb[:, :ln], ACT.Exp, bias=NMX[:, n:n + 1], accum_out=SUM[:, n:n + 1]), t)
        t = dve(lambda e: e.reciprocal(SUM[:, n:n + 1], SUM[:, n:n + 1]), t)
        st[n] = pool(lambda e: e.tensor_scalar(pb[:, :ln], pb[:, :ln], SUM[:, n:n + 1], 1.0, ALU.mult, ALU.mult), t)

    def at_t(n):
        h, qt = divmod(n, 4)
        ln = NM + 128 * (qt + 1)
        pb, pt = PB[n % 3], PT[n % 2]
        ba = aux_bank()
        mb, mo = (ba, 128 * (qt + 1)) if qt < 3 else (3, 128)
        for j in range(qt + 1):
            tok = pe(lambda e, j=j: e.transpose(PS[:, ba, j * 128:(j + 1) * 128], pb[:, NM + 128 * j:NM + 128 * (j + 1)], ident),
                     st[n], bank_free[ba], inc=False)
        tok = pe(lambda e: e.transpose(PS[0:NM, mb, mo:mo + 128], pb[:, 0:NM], ident), bank_free[mb] if qt == 3 else None)
        pb_free[n % 3] = [tok]
        t1 = act(lambda e: e.activation(pt[:, 0:128 * (qt + 1)], PS[:, ba, 0:128 * (qt + 1)], ACT.Copy), tok, pt_free[n % 2])
        t2 = act(lambda e: e.activation(PTM[n % 2], PS[0:NM, mb, mo:mo + 128], ACT.Copy), tok, pt_free[n % 2])
        bank_free[ba] = [t1, t2]
        if qt == 3:
            bank_free[3] = [t2]
        st[n] = [t1, t2]

    def at_pv(n):
        h, qt = divmod(n, 4)
        i, off = h // 2, 64 * (h % 2)
        pt = PT[n % 2]
        bo = 6 + i % 2
        out = PS[off:off + 64, bo, qt * 128:(qt + 1) * 128]
        pairs = [(vm[:, 64 * h:64 * h + 64], PTM[n % 2])]
        pairs += [(v[:, j, 64 * h:64 * h + 64], pt[:, j * 128:(j + 1) * 128]) for j in range(qt + 1)]
        tok = mms(out, pairs, st[n], t_v, bank_free[bo] if h % 2 == 0 and qt == 0 else None)
        pt_free[n % 2] = [tok]
        if h % 2 == 1 and qt == 3:
            t = dve(lambda e: e.tensor_tensor(gT[:, i, :], PS[:, bo, :], gT[:, i, :], ALU.mult), tok, t_g[i])
            bank_free[bo] = [t]
            t_o[i] = split(oH[:, i, :], oL[:, i, :], gT[:, i, :], t)

    t_o = [None] * 8
    gate = {"nt": 2, "k": 0}

    def at_gate():
        nt, k = gate["nt"], gate["k"]
        if nt == 8:
            return
        if k == 8:
            gate["nt"], gate["k"] = nt + 1, 0
            return
        if k == 0:
            gate["g"] = gran()
        g = gate["g"]
        XH, XL, tx = XN(k)
        for i, (w, x) in enumerate(((g[1], XH), (g[1], XL), (g[2], XH))):
            last = k == 7 and i == 2
            tok = pe(lambda e, w=w, x=x, i=i, last=last: e.matmul(PS[:, 1, :], w[:, k, :], x, start=(k == 0 and i == 0), stop=last),
                     g[3], bank_free[1], inc=last)
        if k == 7:
            g[0].free = [tok]
            gate_out(nt, 1, tok)
        gate["k"] += 1

    for n in range(64 + 3):
        if n < 64:
            at_s(n)
        at_gate()
        if 2 <= n < 66:
            at_t(n - 2)
        if n >= 3:
            at_pv(n - 3)
    tmp_free[0], tmp_free[1], rst_free[:] = pb_free[0], pb_free[1], pb_free[2]
    turn[0] = 0
    if stop == "attn":
        return done(pe, act, dve, pool, sp, counters)

    t_h = [None] * 8
    XO = lambda k: (oH[:, k, :], oL[:, k, :], t_o[k])
    for c in range(2):
        for j in range(4):
            nt = 4 * c + j
            b, tok = tile(XO)
            t_h[nt] = dve(lambda e, b=b, nt=nt: e.tensor_tensor(hT[:, nt, NM:L], hT[:, nt, NM:L], PS[:, b, :], ALU.add), tok)
            bank_free[b] = [t_h[nt]]
        ada_step()
    h1 = lambda k: hT[:, k, NM:L]
    attn_done = (pe.sem, pe.count)

    def norm_parts(H, Lo, src, gain, tok_of, extra, shift=None, t_gain=None):
        banks, tok = colsum(src, 8, SEGT, ones, tok_of)
        t = rstd(banks, SEGT, 1.0 / D, tok)
        out = []
        for k in range(8):
            i, tmp, free = take_tmp()
            x = tmp[:, :T]
            t1 = dve(lambda e, k=k, x=x: e.scalar_tensor_tensor(x, src(k), gain(k), RST[:, :T], ALU.mult, ALU.mult), t, t_param, t_gain, tok_of(k), free)
            rst_free[:] = [t1]
            if shift is not None:
                t1 = dve(lambda e, k=k, x=x: e.tensor_scalar(x, x, shift(k), None, ALU.add), t1)
            out.append(split(H[:, k, :], Lo[:, k, :], x, t1, extra))
            tmp_free[i] = [out[-1]]
        return out

    fH, fL = parts_at(4224, 8), parts_at(8320, 8)
    t_n = norm_parts(fH, fL, h1, lambda k: pc("ffn_norm", k), lambda k: t_h[k], attn_done)
    XF = lambda k: (fH[:, k, :], fL[:, k, :], t_n[k])
    hidH, hidL = parts_at(12416, 12), parts_at(18560, 12)
    HTM = [A[:, 24704 + 512 * i:25216 + 512 * i] for i in range(4)]
    htm_free = [[attn_done] for _ in range(4)]
    hid_free = attn_done
    for k0, nk in HALVES:
        t_hid = [None] * 22
        for nt in range(k0, k0 + nk):
            b0, tok0 = tile(XF)
            x = HTM[nt % 4]
            t = act(lambda e, b=b0, x=x: e.activation(x, PS[:, b, :], ACT.Silu), tok0, htm_free[nt % 4])
            bank_free[b0] = [t]
            b1, tok1 = tile(XF)
            t = dve(lambda e, b=b1, x=x: e.tensor_tensor(x, x, PS[:, b, :], ALU.mult), t, tok1)
            bank_free[b1] = [t]
            t_hid[nt] = split(hidH[:, nt - k0, :], hidL[:, nt - k0, :], x, t, hid_free)
            htm_free[nt % 4] = [t_hid[nt]]
            if nt % 2 == 1 and nt < 8:
                ada_step()
        XH_ = lambda k: (hidH[:, k - k0, :], hidL[:, k - k0, :], t_hid[k])
        for c in range(2):
            bs = [bank() for _ in range(4)]
            for r, n in ((0, 8), (8, nk - 8)):
                for j in range(4):
                    tok = mm3(PS[:, bs[j], :], gran(), XH_, bank_free[bs[j]] if r == 0 else None, start=(r == 0), stop=(r == 8), k0=k0 + r)
                    if r == 8:
                        nt = 4 * c + j
                        t_h[nt] = dve(lambda e, b=bs[j], nt=nt: e.tensor_tensor(hT[:, nt, NM:L], hT[:, nt, NM:L], PS[:, b, :], ALU.add), tok)
                        bank_free[bs[j]] = [t_h[nt]]
        hid_free = (pe.sem, pe.count)
    x2 = view(28672, 8, T)
    t_x2 = rms_to(lambda k: x2[:, k, :], h1, 8, SEGT, 1.0 / D, lambda k: pc("final_norm", k), lambda k: t_h[k])
    if stop == "fb":
        return done(pe, act, dve, pool, sp, counters)
    assert ada["n"] == 12
    t_spill = act.dma(dsem("spill"), lambda e: e.dma_start(a["x2_d"], x2), t_x2[7])

    def modcol(j, k):
        return MOD[:, 8 * j + k:8 * j + k + 1]

    def ada_norm(dst, src, tok_of, gname, jsh, jsc, gm, extra):
        t = dve(lambda e: e.tensor_scalar(gm, MOD[:, 8 * jsc:8 * jsc + 8], 1.0, None, ALU.add), ada["tok"], extra)
        t_gm = dve(lambda e: e.tensor_tensor(gm, gm, P(gname), ALU.mult), t, t_param)
        banks, tok = colsum(src, 8, SEGT, ones, tok_of)
        t = rstd(banks, SEGT, 1.0 / D, tok)
        out = []
        ts = [dve(lambda e, k=k: e.scalar_tensor_tensor(dst(k), src(k), gm[:, k:k + 1], RST[:, :T], ALU.mult, ALU.mult), t, t_gm, extra)
              for k in range(8)]
        rst_free[:] = [ts[-1]]
        for k in range(8):
            out.append(act(lambda e, k=k: e.activation(dst(k), dst(k), ACT.Identity, bias=modcol(jsh, k)), ts[k]))
        return out

    n1H, n1L = parts_at(0, 8), parts_at(4096, 8)
    hT_done = [t_x2[7], (pe.sem, pe.count)]
    t = dve(lambda e: e.tensor_scalar(SC, MOD[:, 8:16], 1.0, None, ALU.add), ada["tok"])
    t_gm = dve(lambda e: e.tensor_tensor(SC, SC, P("norm1"), ALU.mult), t, t_param)
    t_n1 = norm_parts(n1H, n1L, lambda k: x2[:, k, :], lambda k: SC[:, k:k + 1], lambda k: t_x2[k], hT_done, shift=lambda k: modcol(0, k), t_gain=t_gm)
    X1 = lambda k: (n1H[:, k, :], n1L[:, k, :], t_n1[k])
    if stop == "n1":
        return done(pe, act, dve, pool, sp, counters)

    UW = T + 30
    u = view(8192, 8, UW)
    cv = view(12528, 8, T)
    cvH, cvL = parts_at(8192, 8), parts_at(12528, 8)
    ymix = view(28672, 8, T)
    ffn_done = hT_done
    t_z = dve(lambda e: e.memset(u[:, :, 0:30], 0.0), ffn_done)
    t_cv = [None] * 8
    def xbc_tile(nt, dst, raw, raw_free, extra=None):
        b, tok = tile(X1)
        t = act(lambda e: e.activation(raw[:, 3:3 + T], PS[:, b, :], ACT.Copy), tok, raw_free)
        bank_free[b] = [t]
        s0 = PO["scw"][0] + 4 * nt
        t = dve(lambda e: e.tensor_scalar(dst, raw[:, 0:T], PR[:, s0:s0 + 1], pc("scb", nt), ALU.mult, ALU.add), t, t_rz, extra)
        for i in range(1, 4):
            t = dve(lambda e, i=i: e.scalar_tensor_tensor(dst, raw[:, i:i + T], PR[:, s0 + i:s0 + i + 1], dst, ALU.mult, ALU.add), t)
        return tok, lambda: act(lambda e: e.activation(dst, dst, ACT.Silu), t), t

    Bf = view(18432, 4, T)
    Cf = view(20480, 4, T)
    Bt = view(22528, 4, 512)
    RAW = [A[:, 24576 + 516 * i:24576 + 516 * i + 515] for i in range(2)]
    t_rz = [dve(lambda e, i=i: e.memset(RAW[i][:, 0:3], 0.0), ffn_done) for i in range(2)]
    raw_free = [[], []]
    t_B, t_C = [None] * 4, [None] * 4
    RED = bank()
    held.add(RED)

    def conv_tile(nt):
        bs = [tile(X1) for _ in range(2)]
        dst = u[:, nt, 30:UW]
        t = act(lambda e: e.activation(dst, PS[:, bs[0][0], :], ACT.Sigmoid), bs[0][1], ffn_done)
        bank_free[bs[0][0]] = [t]
        t = dve(lambda e: e.tensor_tensor(dst, dst, PS[:, bs[1][0], :], ALU.mult), t, bs[1][1], t_z)
        bank_free[bs[1][0]] = [t]
        w0 = PO["cvw"][0] + 31 * nt
        t = dve(lambda e: e.tensor_scalar(cv[:, nt, :], u[:, nt, 0:T], PR[:, w0:w0 + 1], pc("cvb", nt), ALU.mult, ALU.add), t)
        for i in range(1, 31):
            t = dve(lambda e, i=i: e.scalar_tensor_tensor(cv[:, nt, :], u[:, nt, i:i + T], PR[:, w0 + i:w0 + i + 1], cv[:, nt, :], ALU.mult, ALU.add), t)
        t_cv[nt] = t

    def conv_sum(k):
        return pe(lambda e: e.matmul(PS[:, RED, :], ones, cv[:, k, :], start=(k == 0), stop=(k == 7)), t_cv[k], bank_free[RED] if k == 0 else None, t_const)

    DT = view(25632, 4, T)[0:32]
    dtT, acsT = DT[:, 0, :], DT[:, 2, :]
    TK = view(27680, 5, 128)
    ts_ = {}

    def steps_a():
        b, tok = tile(X1, m=32)
        t = act(lambda e, b=b: e.activation(DT[:, 0, :], PS[0:32, b, :], ACT.Identity, bias=P("dtb", 0, 32)), tok, ffn_done)
        bank_free[b] = [t]
        t = log1p_exp(DT[:, 0, :], DT[:, 1, :], DT[:, 2, :], DT[:, 3, :], t, 32)
        t_dt = dve(lambda e: e.scalar_tensor_tensor(DT[:, 0, :], DT[:, 0, :], 0.0, DT[:, 3, :], ALU.max, ALU.add), t)
        alg = P("alog", 0, 32)
        t = act(lambda e: e.activation(alg, alg, ACT.Exp), t_param)
        t = dve(lambda e: e.tensor_scalar(DT[:, 1, :], DT[:, 0, :], alg, -1.0, ALU.mult, ALU.mult), t, t_dt)
        for c in range(4):
            ts_["acs"] = dve(lambda e, c=c: e.tensor_tensor_scan(DT[:, 2, c * 128:(c + 1) * 128], C("ones", 0, 32),
                                                          DT[:, 1, c * 128:(c + 1) * 128], 0.0, ALU.mult, ALU.add), t)

    def steps_b():
        b = bank()
        for w_, srcT in enumerate((dtT, acsT)):
            for c in range(4):
                tok = pe(lambda e, w_=w_, c=c, srcT=srcT, b=b: e.transpose(PS[:, b, w_ * 128 + c * 32:w_ * 128 + c * 32 + 32], srcT[:, c * 128:(c + 1) * 128],
                                                                 C("ident", 0, 32)[:, 0:32]), bank_free[b], ts_["acs"], inc=(w_ == 1 and c == 3))
        ts_["tk"] = dve(lambda e: e.tensor_copy(TK[:, 0:2, :], PS[:, b, 0:256].rearrange("p (a b) -> p a b", a=2)), tok, ffn_done)
        bank_free[b] = [ts_["tk"]]

    def steps_c():
        b = bank()
        tok = pe(lambda e: e.matmul(PS[:, b, 0:128], ident[:, 127:128].broadcast_to([128, 128]), TK[:, 1, :], start=True, stop=True), bank_free[b], ts_["tk"])
        t = dve(lambda e: e.tensor_copy(TK[:, 2, :], PS[:, b, 0:128]), tok)
        bank_free[b] = [t]
        t = dve(lambda e: e.tensor_tensor(TK[:, 3, :], TK[:, 2, :], TK[:, 1, :], ALU.subtract), t)
        t = act(lambda e: e.activation(TK[:, 3, :], TK[:, 3, :], ACT.Exp), t)
        ts_["tk2"] = act(lambda e: e.activation(TK[:, 4, :], TK[:, 2, :], ACT.Exp), t)

    t_cg = [None] * 8
    for nt in range(8):
        conv_tile(nt)
        i = nt % 2
        dst, tt_ = ((Bf, t_B), (Cf, t_C))[nt // 4]
        if nt > 0:
            late_silu()
        _, silu, t = xbc_tile(16 + nt, dst[:, nt % 4, :], RAW[i], raw_free[i], ffn_done)

        def late_silu(silu=silu, tt_=tt_, nt=nt):
            tt_[nt % 4] = silu()

        raw_free[i] = [t]
        b1, tok1 = tile(X1)
        t_cg[nt] = act(lambda e, b1=b1, nt=nt: e.activation(ymix[:, nt, :], PS[:, b1, :], ACT.Sigmoid), tok1, t_spill)
        bank_free[b1] = [t_cg[nt]]
        if nt >= 2:
            conv_sum(nt - 2)
        if nt == 0:
            steps_a()
        if nt == 3:
            steps_b()
        if nt == 5:
            steps_c()
            for tt in range(4):
                b = bank()
                for g in range(4):
                    tok = pe(lambda e, tt=tt, g=g, b=b: e.transpose(PS[:, b, g * 128:(g + 1) * 128], Bf[:, g, tt * 128:(tt + 1) * 128], ident),
                             bank_free[b], t_B[g], inc=(g == 3))
                t_Bt = act(lambda e, tt=tt, b=b: e.activation(Bt[:, tt, :], PS[:, b, :], ACT.Copy), tok)
                bank_free[b] = [t_Bt]
    t_acs, t_tk, t_tk2 = ts_["acs"], ts_["tk"], ts_["tk2"]

    SGS = [A[:, 17408 + 512 * i:17408 + 512 * (i + 1)] for i in range(2)]
    sgs_free = [ffn_done, ffn_done]

    def early_gate(nt):
        i = nt % 2
        b1, tok1 = tile(X1)
        t = act(lambda e: e.activation(SGS[i], PS[:, b1, :], ACT.Sigmoid), tok1, sgs_free[i])
        bank_free[b1] = [t]
        sgs_free[i] = [act.dma(dsem(f"sgs{i}"), lambda e: e.dma_start(a["sg_d"][:, nt, :], SGS[i]), t)]

    late_silu()
    early_gate(0)
    conv_sum(6)
    early_gate(1)
    early_gate(2)
    tok = conv_sum(7)
    t = act(lambda e: e.activation(RST[:, :T], PS[:, RED, :], ACT.Copy, scale=1.0 / D), tok, rst_free)
    bank_free[RED] = [t]
    held.clear()
    tc = [dve(lambda e, k=k: e.tensor_tensor(cv[:, k, :], cv[:, k, :], RST[:, :T], ALU.subtract), t) for k in range(8)]
    rst_free[:] = [tc[-1]]
    early_gate(3)
    banks, tok = colsum(lambda k: cv[:, k, :], 8, SEGT, ones, lambda k: tc[k])
    early_gate(4)
    early_gate(5)
    t = rstd(banks, SEGT, 1.0 / D, tok)
    tl = []
    for k in range(8):
        t1 = dve(lambda e, k=k: e.tensor_tensor(cv[:, k, :], cv[:, k, :], RST[:, :T], ALU.mult), t, tc[k])
        rst_free[:] = [t1]
        t1 = act(lambda e, k=k: e.activation(cv[:, k, :], cv[:, k, :], ACT.Silu, scale=pc("lng", k), bias=pc("lnb", k)), t1)
        tl.append(split(cvH[:, k, :], cvL[:, k, :], cv[:, k, :], t1, t_cv[7], by=(pool, dve)[k % 2]))
    XC = lambda k: (cvH[:, k, :], cvL[:, k, :], tl[k])
    t_y = [None] * 8
    for nt in range(8):
        b2, tok2 = tile(XC)
        t_y[nt] = dve(lambda e, b2=b2, nt=nt: e.tensor_tensor(ymix[:, nt, :], ymix[:, nt, :], PS[:, b2, :], ALU.mult), t_cg[nt], tok2)
        bank_free[b2] = [t_y[nt]]
    if stop == "ycv":
        return done(pe, act, dve, pool, sp, counters)

    cv_done = [(pe.sem, pe.count), (dve.sem, dve.count), t_spill] + sgs_free[0] + sgs_free[1]
    t_yspill = act.dma(dsem("yspill"), lambda e: e.dma_start(a["ymix_d"], ymix), t_y[7])
    free2 = cv_done + [t_yspill]
    xsf = view(8192, 4, T)
    xdt = view(10240, 4, 512)
    yT = view(28672, 8, T)
    yt = lambda k: yT[:, k % 8, :]
    STS = [A[:, 13312 + 512 * i:13312 + 512 * (i + 1)] for i in range(3)]
    XD = [A[:, 14848 + 512 * i:14848 + 512 * (i + 1)] for i in range(2)]
    EB = [A[:, 15872 + 512 * i:15872 + 512 * (i + 1)] for i in range(2)]
    ZB = [A[:, 16896:17408], A[:, 26144:26656]]
    MB = [view(12288, 2, 512), view(17408, 2, 512)]
    mb_free, eb_free, xd_free = [free2, free2], [free2, free2], [free2, free2]
    zb_free, st_free, cbm_free, xs_free, xdt_free = [free2, t_acs], free2, [], free2, free2
    t_ysp = [None, None]
    h64 = lambda x: x.rearrange("p (h d) -> p h d", d=64)
    cb = CBM[:, :].rearrange("p (a b) -> p a b", a=1).broadcast_to([128, 2, 512])
    pa, pending_norm = {}, None

    def pair_a(g, i):
        m, eb, zb = MB[i % 2], EB[i % 2], ZB[i % 2]
        h0 = 8 * g + 2 * i
        for hh in range(2):
            b = bank()
            tok = pe(lambda e, b=b, hh=hh: e.matmul(PS[:, b, :], C("ident", 0, 32)[:, h0 + hh:h0 + hh + 1].broadcast_to([32, 128]), acsT, start=True, stop=True),
                     t_acs, bank_free[b])
            for c in range(4):
                t = dve(lambda e, b=b, hh=hh, c=c: e.tensor_scalar(m[:, hh, c * 128:(c + 1) * 128], PS[:, b, c * 128:(c + 1) * 128],
                                                            TK[:, 1, c * 32 + h0 + hh:c * 32 + h0 + hh + 1], 0.0, ALU.subtract, ALU.min), tok, mb_free[i % 2], t_tk)
            bank_free[b] = [t]
        t = act(lambda e: e.activation(m, m, ACT.Exp), t)
        t_m = dve(lambda e: e.tensor_tensor(m, m, cb, ALU.mult), t, t_cb)
        b = bank()
        for hh in range(2):
            tok = pe(lambda e, hh=hh: e.matmul(PS[64 * hh:64 * hh + 64, b, :], C("ident", 0, 32)[:, h0 + hh:h0 + hh + 1].broadcast_to([32, 64]), acsT,
                                               start=True, stop=True), t_acs, bank_free[b])
        t_eb = act(lambda e: e.activation(eb, PS[:, b, :], ACT.Exp), tok, eb_free[i % 2])
        bank_free[b] = [t_eb]
        bz, tokz = tile(X1)
        t_zz = act(lambda e: e.activation(zb, PS[:, bz, :], ACT.Silu), tokz, zb_free[i % 2])
        bank_free[bz] = [t_zz]
        pa[i] = (t_eb, t_m, t_zz)

    def pair_b(g, i):
        nt = 4 * g + i
        m, eb, zb = MB[i % 2], EB[i % 2], ZB[i % 2]
        t_eb, t_m, t_zz = pa[i]
        bo = bank()
        for c in range(1, 4):
            tok = pe(lambda e, c=c: e.matmul(PS[:, bo, c * 128:(c + 1) * 128], STS[c - 1][:, i * 128:(i + 1) * 128], Cf[:, g, c * 128:(c + 1) * 128],
                                             start=True, stop=True), t_st[c - 1], bank_free[bo], inc=(c == 3))
        t = dve(lambda e: e.tensor_tensor(eb[:, 128:512], eb[:, 128:512], PS[:, bo, 128:512], ALU.mult), t_eb, tok)
        bank_free[bo] = [t]
        bd = bank()
        for c in range(4):
            for hh in range(2):
                tok = pe(lambda e, c=c, hh=hh: e.matmul(PS[64 * hh:64 * hh + 64, bd, c * 128:(c + 1) * 128], xdt[:, c, (2 * i + hh) * 64:(2 * i + hh) * 64 + 64],
                                                 m[:, hh, c * 128:(c + 1) * 128], start=True, stop=True),
                         t_m, t_xdt[c], bank_free[bd] if c == 0 and hh == 0 else None, inc=(c == 3 and hh == 1))
        mb_free[i % 2] = [tok]
        t2 = dve(lambda e: e.scalar_tensor_tensor(yt(nt), xsf[:, i, :], pc("dsk", nt), PS[:, bd, :], ALU.mult, ALU.add), tok, free2, t_ysp[g % 2])
        bank_free[bd] = [t2]
        t2 = dve(lambda e: e.tensor_tensor(yt(nt)[:, 128:512], yt(nt)[:, 128:512], eb[:, 128:512], ALU.add), t, t2)
        eb_free[i % 2] = [t2]
        t2 = dve(lambda e: e.tensor_tensor(yt(nt), yt(nt), zb, ALU.mult), t2, t_zz)
        zb_free[i % 2] = [t2]
        t_yg.append(t2)
        return tok

    def group_norm(g, t_yg):
        banks, tok = colsum(lambda k: yt(4 * g + k), 4, SEGT, ones, lambda k: t_yg[k])
        t = rstd(banks, SEGT, 1.0 / 512, tok)
        for k in range(4):
            nt = 4 * g + k
            t_yl = dve(lambda e, nt=nt: e.scalar_tensor_tensor(yt(nt), yt(nt), pc("sng", nt), RST[:, :T], ALU.mult, ALU.mult), t, t_param)
        rst_free[:] = [t_yl]
        if g < 2:
            t_ysp[g] = act.dma(dsem(f"ysp{g}"), lambda e, g=g: e.dma_start(a["y01_d"][:, 4 * g:4 * g + 4, :], yT[:, 4 * g:4 * g + 4, :]), t_yl)
        return t_yl

    for g in range(4):
        t_xs = []
        for j in range(4):
            i = j % 2
            tok, silu, t = xbc_tile(4 * g + j, xsf[:, j, :], RAW[i], raw_free[i], xs_free)
            raw_free[i] = [t]
            t_xs.append(silu())
        b = bank()
        for c in range(4):
            tok = pe(lambda e, c=c, b=b, g=g: e.matmul(PS[:, b, c * 128:(c + 1) * 128], Bf[:, g, c * 128:(c + 1) * 128], Cf[:, g, c * 128:(c + 1) * 128],
                                                  start=True, stop=True), bank_free[b], t_B[g], t_C[g], inc=(c == 3))
        sm = C("smask").rearrange("p (a b) -> p a b", a=1).broadcast_to([128, 4, 128])
        t_cb = dve(lambda e, b=b, sm=sm: e.tensor_tensor(CBM[:, :].rearrange("p (a b) -> p a b", a=4), PS[:, b, :].rearrange("p (a b) -> p a b", a=4), sm, ALU.mult),
                   tok, cbm_free)
        bank_free[b] = [t_cb]
        pair_a(g, 0)
        t_xdt, t_yg = [], []
        for c in range(4):
            b = bank()
            for j in range(4):
                tok = pe(lambda e, c=c, j=j, b=b: e.transpose(PS[:, b, j * 128:(j + 1) * 128], xsf[:, j, c * 128:(c + 1) * 128], ident),
                         bank_free[b], t_xs[j], inc=(j == 3))
            sc = TK[:, 0, c * 32 + 8 * g:c * 32 + 8 * g + 8].rearrange("p (h d) -> p h d", d=1).broadcast_to([128, 8, 64])
            t = dve(lambda e, c=c, b=b, sc=sc: e.tensor_tensor(h64(xdt[:, c, :]), h64(PS[:, b, :]), sc, ALU.mult), tok, xdt_free, t_tk)
            bank_free[b] = [t]
            t_xdt.append(t)
        t_st = [None] * 3
        for c in range(3):
            i = c % 2
            dc = TK[:, 3, c * 32 + 8 * g:c * 32 + 8 * g + 8].rearrange("p (h d) -> p h d", d=1).broadcast_to([128, 8, 64])
            t = dve(lambda e, c=c, i=i, dc=dc: e.tensor_tensor(h64(XD[i]), h64(xdt[:, c, :]), dc, ALU.mult), t_xdt[c], xd_free[i], t_tk2)
            b = bank()
            tok = pe(lambda e, c=c, b=b, g=g, i=i: e.matmul(PS[:, b, :], Bt[:, c, g * 128:(g + 1) * 128], XD[i], start=True, stop=True), t, t_Bt, bank_free[b])
            xd_free[i] = [tok]
            if c == 0:
                t = dve(lambda e, b=b: e.tensor_copy(STS[0], PS[:, b, :]), tok, st_free)
            else:
                cd = TK[:, 4, c * 32 + 8 * g:c * 32 + 8 * g + 8].rearrange("p (h d) -> p h d", d=1).broadcast_to([128, 8, 64])
                t = dve(lambda e, c=c, cd=cd: e.tensor_tensor(h64(STS[c]), h64(STS[c - 1]), cd, ALU.mult), t_st[c - 1], st_free)
                t = dve(lambda e, c=c, b=b: e.tensor_tensor(STS[c], STS[c], PS[:, b, :], ALU.add), t, tok)
            bank_free[b] = [t]
            t_st[c] = t
        for i in range(4):
            if i < 3:
                pair_a(g, i + 1)
            if i == 1 and pending_norm is not None:
                pending_norm()
            xdt_done = pair_b(g, i)
        cbm_free, xs_free, xdt_free, st_free = [pa[3][1]], [t_yg[-1]], [xdt_done], [xdt_done]
        pending_norm = lambda g=g, t_yg=t_yg: group_norm(g, t_yg)
    t_yl = pending_norm()
    ssd_done = [t_yl, (pe.sem, pe.count)]
    if stop == "ssd":
        return done(pe, act, dve, pool, sp, counters)

    ymix2 = view(24576, 8, T)
    x2b = view(0, 8, T)
    y01 = view(8192, 8, T)
    t_y01 = act.dma(dsem("back3"), lambda e: e.dma_start(y01, a["y01_d"]), ssd_done, t_ysp)
    t_ym = act.dma(dsem("back"), lambda e: e.dma_start(ymix2, a["ymix_d"]), ssd_done)
    SG = view(20480, 8, T)
    t_sg = [act.dma(dsem("sgb"), lambda e: e.dma_start(SG[:, 0:NG, :], a["sg_d"][:, 0:NG, :]), ssd_done)] * NG
    for nt in range(NG, 8):
        b1, tok1 = tile(X1)
        t = act(lambda e, b1=b1, nt=nt: e.activation(SG[:, nt, :], PS[:, b1, :], ACT.Sigmoid), tok1, ssd_done)
        bank_free[b1] = [t]
        t_sg.append(t)
    gate_done = (pe.sem, pe.count)
    t_x2b = act.dma(dsem("back2"), lambda e: e.dma_start(x2b, a["x2_d"]), gate_done)
    yH = [parts_at(12288, 8), parts_at(4096, 8)]
    yL = [parts_at(8192, 8), parts_at(28672, 8)]
    t_yp = [split(yH[1][:, k, :], yL[1][:, k, :], yT[:, k, :], gate_done, t_yl, by=(pool, dve)[k % 2]) for k in range(8)]
    t_yp = [split(yH[0][:, k, :], yL[0][:, k, :], y01[:, k, :], t_y01, ssd_done, by=(pool, dve)[k % 2]) for k in range(8)] + t_yp
    XY = lambda k: (yH[k // 8][:, k % 8, :], yL[k // 8][:, k % 8, :], t_yp[k])
    mH, mL = parts_at(16384, 8), parts_at(24576, 8)
    t_m_ = [None] * 8
    for c in range(2):
        bs = [bank() for _ in range(4)]
        for r in (8, 0):
            for j in range(4):
                nt = 4 * c + j
                tok = mm3(PS[:, bs[j], :], gran(), XY, bank_free[bs[j]] if r == 8 else None, start=(r == 8), stop=(r == 0), k0=r)
                if r == 0:
                    t = dve(lambda e, b=bs[j], nt=nt: e.tensor_tensor(SG[:, nt, :], SG[:, nt, :], PS[:, b, :], ALU.mult), t_sg[nt], tok)
                    bank_free[bs[j]] = [t]
                    t = dve(lambda e, nt=nt: e.tensor_tensor(ymix2[:, nt, :], ymix2[:, nt, :], SG[:, nt, :], ALU.add), t, t_ym)
                    t_m_[nt] = split(mH[:, nt, :], mL[:, nt, :], ymix2[:, nt, :], t)
    RW = view(8192, 8, 72)
    t_rw = pool.dma(dsem("rw"), lambda e: e.dma_start(RW, a["rw"]), (pe.sem, pe.count))
    XM = lambda k: (mH[:, k, :], mL[:, k, :], t_m_[k])
    t_h2 = [None] * 8
    for c in range(2):
        for j in range(4):
            nt = 4 * c + j
            b, tok = tile(XM)
            t_h2[nt] = dve(lambda e, b=b, nt=nt: e.scalar_tensor_tensor(x2b[:, nt, :], PS[:, b, :], modcol(2, nt), x2b[:, nt, :], ALU.mult, ALU.add), tok, t_x2b)
            bank_free[b] = [t_h2[nt]]
    n2 = view(27648, 8, T)
    mix_done = [(pe.sem, pe.count)]
    t_n2 = ada_norm(lambda k: n2[:, k, :], lambda k: x2b[:, k, :], lambda k: t_h2[k], "norm2", 3, 4, SC, mix_done)
    if stop == "n2":
        return done(pe, act, dve, pool, sp, counters)

    LG = view(8768, 4, 72)
    R = 9088
    r3 = lambda o, n: view(R + o, 4, n)
    gmax, gidx, emax, eidx = r3(0, 8), r3(32, 8), r3(64, 8), r3(96, 8)
    eg = r3(128, 8)
    s1, s2, gp, wa, wb, tmp1, tmp2 = (r3(160 + 4 * i, 1) for i in range(7))
    el8 = r3(200, 8)
    msel = view(R + 240, 4, 64)
    OH = [view(R + 496 + 256 * i, 4, 64) for i in range(2)]
    OHS = view(R + 1008, 4, 64)
    POS = view(R + 1264, 4, 64)
    PRE = SCR[:, 1056:1376].rearrange("p (a b) -> p a b", a=5)
    t_pre = dve(lambda e: e.memset(PRE[:, 0, :], 0.0), rst_free)
    IDX = CBM[:, 64:80].bitcast(U32)
    KEEP = CBM[:, 0:64]
    SLOTU = CBM[:, 80:88].bitcast(U32)
    LIST = CBM[:, 88:120].bitcast(U32)
    TOKU = CBM[:, 120:124].bitcast(U32)
    LGT = A[0:72, 10752:11264]
    b = bank()
    for k in range(8):
        tok = pe(lambda e, k=k, b=b: e.matmul(PS[0:72, b, :], RW[:, k, :], n2[:, k, :], start=(k == 0), stop=(k == 7)), t_rw, t_n2[k], bank_free[b], inc=(k == 7))
    t = act(lambda e, b=b: e.activation(LGT, PS[0:72, b, :], ACT.Copy), tok, mix_done)
    bank_free[b] = [t]
    b = bank()
    for tt in range(4):
        tok = pe(lambda e, b=b, tt=tt: e.transpose(PS[:, b, 128 * tt:128 * tt + 72], LGT[:, tt * 128:(tt + 1) * 128], C("ident", 0, 72)[:, 0:72]), t, bank_free[b], inc=(tt == 3))
    t_lg = dve(lambda e, b=b: e.tensor_tensor(LG, PS[:, b, :].rearrange("p (a b) -> p a b", a=4)[:, :, 0:72],
                                       P("rb").rearrange("p (a b) -> p a b", a=1).broadcast_to([128, 4, 72]), ALU.add), tok, t_param)
    bank_free[b] = [t_lg]
    h2t = view(4096, 4, D)
    n2t = [A[:, 31744:32768], SCR[:, 0:1024]]
    n2t_free = [[mix_done], [mix_done] + tmp_free[0] + tmp_free[1]]
    last_n2t = {}
    def by_token(tt):
        for half in range(2):
            for src, dst_of in ((n2, None), (x2b, h2t)):
                b = bank()
                for j in range(4):
                    tok = pe(lambda e, half=half, j=j, src=src, b=b: e.transpose(PS[:, b, j * 128:(j + 1) * 128], src[:, 4 * half + j, tt * 128:(tt + 1) * 128], ident),
                             bank_free[b], t_n2, t_h2, inc=(j == 3))
                dst = (n2t[tt % 2] if dst_of is None else h2t[:, tt, :])[:, 512 * half:512 * half + 512]
                t = act(lambda e, dst=dst, b=b: e.activation(dst, PS[:, b, :], ACT.Copy), tok, n2t_free[tt % 2] if dst_of is None else mix_done)
                bank_free[b] = [t]
                last_n2t["n2" if dst_of is None else "h2"] = t
        n2t_free[tt % 2] = [act.dma(dsem(f"n2d{tt % 2}"), lambda e: e.dma_start(a["n2_d"][tt * 128:(tt + 1) * 128, :], n2t[tt % 2]), last_n2t["n2"])]

    bc = lambda x, n: x.broadcast_to([128, 4, n])
    t = t_lg
    for tt in range(4):
        tm = dve(lambda e, tt=tt: e.max(gmax[:, tt, :], LG[:, tt, 0:8]), t)
    for tt in range(4):
        t = dve(lambda e, tt=tt: e.max_index(IDX[:, 0:8], gmax[:, tt, :], LG[:, tt, 0:8]), tm, t)
        t = dve(lambda e, tt=tt: e.tensor_copy(gidx[:, tt, :], IDX[:, 0:8]), t)
    t1 = dve(lambda e: e.tensor_tensor(eg, LG[:, :, 0:8], bc(gmax[:, :, 0:1], 8), ALU.subtract), tm)
    t1 = act(lambda e: e.activation(eg, eg, ACT.Exp), t1)
    by_token(0)
    by_token(1)
    t1 = dve(lambda e: e.tensor_reduce(s1, eg, AX, ALU.add), t1)
    t_gp = dve(lambda e: e.reciprocal(gp, s1), t1)
    t2 = dve(lambda e: e.tensor_tensor(el8, C("iota8").rearrange("p (a b) -> p a b", a=1).broadcast_to([128, 4, 8]), bc(gidx[:, :, 0:1], 8), ALU.is_equal), t)
    t2 = [dve(lambda e, tt=tt: e.tensor_tensor(msel[:, tt, :].rearrange("p (a b) -> p a b", b=8), LG[:, tt, 8:72].rearrange("p (a b) -> p a b", b=8),
                                        el8[:, tt, :].rearrange("p (a b) -> p a b", b=1).broadcast_to([128, 8, 8]), ALU.mult), t2) for tt in range(4)][-1]
    t2 = [dve(lambda e, tt=tt: e.tensor_reduce(el8[:, tt, :], msel[:, tt, :].rearrange("p (a b) -> p b a", b=8), AX, ALU.add), t2) for tt in range(4)][-1]
    for tt in range(4):
        tm = dve(lambda e, tt=tt: e.max(emax[:, tt, :], el8[:, tt, :]), t2)
    for tt in range(4):
        t = dve(lambda e, tt=tt: e.max_index(IDX[:, 8:16], emax[:, tt, :], el8[:, tt, :]), tm, t)
        t = dve(lambda e, tt=tt: e.tensor_copy(eidx[:, tt, :], IDX[:, 8:16]), t)
    t3 = dve(lambda e: e.tensor_tensor(eg, emax, bc(emax[:, :, 0:1], 8), ALU.subtract), t_gp, tm)
    t3 = act(lambda e: e.activation(eg, eg, ACT.Exp), t3)
    t3 = dve(lambda e: e.tensor_reduce(s1, eg, AX, ALU.add), t3)
    t3 = dve(lambda e: e.reciprocal(s1, s1), t3)
    t3 = dve(lambda e: e.tensor_tensor(eg, eg, bc(s1, 8), ALU.mult), t3)
    t3 = dve(lambda e: e.tensor_tensor(s2, eg[:, :, 0:1], eg[:, :, 1:2], ALU.add), t3)
    t3 = dve(lambda e: e.reciprocal(s2, s2), t3)
    t3 = dve(lambda e: e.tensor_tensor(s2, s2, gp, ALU.mult), t3)
    WK = [KEEP[:, 4 * i:4 * i + 4].rearrange("p (a b) -> p a b", b=1) for i in range(2)]
    for i in range(2):
        t_wk = dve(lambda e, i=i: e.tensor_tensor(WK[i], eg[:, :, i:i + 1], s2, ALU.mult), t3)
    t4 = dve(lambda e: e.tensor_scalar(gidx[:, :, 0:1], gidx[:, :, 0:1], 8.0, None, ALU.mult), t, t2)
    t4 = dve(lambda e: e.tensor_tensor(eidx[:, :, 0:2], eidx[:, :, 0:2], bc(gidx[:, :, 0:1], 2), ALU.add), t4)
    i64 = C("iota64").rearrange("p (a b) -> p a b", a=1).broadcast_to([128, 4, 64])
    for i in range(2):
        t5 = dve(lambda e, i=i: e.tensor_tensor(OH[i], i64, bc(eidx[:, :, i:i + 1], 64), ALU.is_equal), t4)
    t5 = dve(lambda e: e.tensor_tensor(OHS, OH[0], OH[1], ALU.add), t5)
    t5 = dve(lambda e: e.tensor_copy(PRE[:, 1, :], OHS[:, 0, :]), t5, t_pre)
    for k in range(1, 4):
        t5 = dve(lambda e, k=k: e.tensor_tensor(PRE[:, k + 1, :], PRE[:, k, :], OHS[:, k, :], ALU.add), t5)
    b = bank()
    pe(lambda e, b=b: e.matmul(PS[:, b, 0:256], C("ustrict"), OHS.rearrange("p a b -> p (a b)"), start=True, stop=False), t5, bank_free[b], inc=False)
    pe(lambda e, b=b: e.matmul(PS[:, b, 0:256], ones, PRE[:, 0:4, :].rearrange("p a b -> p (a b)"), start=False, stop=True), inc=False)
    tok = pe(lambda e, b=b: e.matmul(PS[:, b, 256:320], ones, PRE[:, 4, :], start=True, stop=True))
    held.add(b)
    by_token(2)
    by_token(3)
    held.clear()
    t_h2t = last_n2t["h2"]
    t_n2ds = n2t_free[0] + n2t_free[1]
    dense_done = [(pe.sem, pe.count)]
    tok_pos = tok
    t6 = dve(lambda e, b=b: e.tensor_copy(POS, PS[:, b, 0:256].rearrange("p (a b) -> p a b", a=4)), tok)
    CNTF = CBM[:, 188:254]
    t_cnt = dve(lambda e, b=b: e.tensor_copy(CNTF[:, 0:64], PS[:, b, 256:320]), tok)
    bank_free[b] = [t6, t_cnt]
    NB, INC, VV = (A[:, 10608 + 64 * i:10672 + 64 * i] for i in range(3))
    CNT = CNTF[:, 0:64]
    t9 = dve(lambda e: e.tensor_scalar(NB, CNT, float(BLK), None, ALU.is_gt), t_cnt, mix_done)
    for k in range(2, T // BLK):
        t9 = dve(lambda e, k=k: e.scalar_tensor_tensor(NB, CNT, float(BLK * k), NB, ALU.is_gt, ALU.add), t9)
    t9 = dve(lambda e: e.tensor_tensor_scan(INC, ones[:, 0:64], NB, 0.0, ALU.mult, ALU.add), t9)
    t10 = dve(lambda e: e.tensor_tensor(VV, INC, NB, ALU.subtract), t9)
    t10 = dve(lambda e: e.tensor_tensor(VV, VV, C("iota64"), ALU.subtract), t10)
    t_v = dve(lambda e: e.tensor_scalar(VV, VV, float(BLK), float(MAIN - BLK), ALU.mult, ALU.add), t10)
    t11 = dve(lambda e: e.tensor_scalar(NB, INC, C("tok")[:, 0:1], None, ALU.is_le), t10)
    t11 = dve(lambda e: e.tensor_reduce(KEEP[:, 24:25], NB, AX, ALU.add), t11, t_wk)
    b = bank()
    tok = pe(lambda e, b=b: e.matmul(PS[0:1, b, 0:OVER], KEEP[:, 24:25], ident[:, 0:OVER], start=True, stop=True), t11, bank_free[b])
    OVI = CBM[0:1, 124:141].bitcast(I32)
    t11 = dve(lambda e, b=b: e.tensor_copy(OVI[:, 0:OVER], PS[0:1, b, 0:OVER]), tok)
    bank_free[b] = [t11]
    t_ovi = dve(lambda e: e.tensor_copy(OVI[:, OVER:OVER + 1], INC[0:1, 63:64]), t11)
    vb = VV.rearrange("p (a b) -> p a b", a=1).broadcast_to([128, 4, 64])
    for i in range(2):
        t6 = dve(lambda e, i=i: e.tensor_tensor(OHS, OH[i], POS, ALU.mult), t6, tok_pos)
        t6 = dve(lambda e: e.tensor_reduce(tmp1, OHS, AX, ALU.add), t6)
        t6 = dve(lambda e, i=i: e.tensor_tensor(msel, OH[i], vb, ALU.mult), t6, t_v)
        t6 = dve(lambda e: e.tensor_reduce(tmp2, msel, AX, ALU.add), t6)
        t6 = dve(lambda e: e.scalar_tensor_tensor(tmp2, tmp1, float(BLK), tmp2, ALU.is_ge, ALU.mult), t6)
        t6 = dve(lambda e: e.tensor_tensor(tmp2, tmp2, tmp1, ALU.add), t6)
        t6 = dve(lambda e, i=i: e.scalar_tensor_tensor(tmp2, eidx[:, :, i:i + 1], float(BLK), tmp2, ALU.mult, ALU.add), t6)
        t_slot = dve(lambda e, i=i: e.tensor_copy(SLOTU[:, 4 * i:4 * i + 4].rearrange("p (a b) -> p a b", b=1), tmp2), t6)
        t6 = t_slot
    t7 = dve(lambda e: e.tensor_copy(TOKU[:, :], C("tok")), t_const)
    for i in range(2):
        for tt in range(4):
            t_sc = pool.dma(dsem("scat"), lambda e, i=i, tt=tt: e.indirect_dma_start(a["list_d"], bass.IndirectOffsetOnAxis(ap=SLOTU[:, 4 * i + tt:4 * i + tt + 1], axis=0),
                                                                           TOKU[:, tt:tt + 1], None), t_zl, t_slot, t7)
    ld = a["list_d"][0:MAIN, :].rearrange("(q s j) o -> s j (q o)", s=2, j=BLK)
    for s in range(2):
        t_list = pool.dma(dsem("list"), lambda e, s=s: e.dma_start(LIST[64 * s:64 * s + 64, :], ld[s], allow_slow_non_contiguous=True), t_sc)
    if stop == "route":
        return done(pe, act, dve, pool, sp, counters)

    route_done = [t_list, t_slot, t_ovi, t_wk] + dense_done + t_n2ds
    for i in (2, 3):
        s = Slot(RG[:, i * WC:(i + 1) * WC], f"w{i}")
        s.free = mix_done
        ring.append(s)
    for i in range(5):
        s = Slot(A[:, 11264 + WC * i:11264 + WC * (i + 1)], f"x{i}")
        s.free = list(mix_done if i < 4 else dense_done)
        ring.append(s)
    XG = [A[:, 1024 * i:1024 * (i + 1)] for i in range(2)]
    XT = [view(2048 + 1024 * i, 8, 128) for i in range(2)]
    H13 = [A[:, 8192 + 512 * i:8192 + 512 * (i + 1)] for i in range(2)]
    YO = [A[:, 9216 + 512 * i:9216 + 512 * (i + 1)] for i in range(2)]
    HT = [view(10240 + 256 * i, 4, 64) for i in range(2)]
    SL = [view(10752 + 256 * i, 4, 64) for i in range(2)]
    xg_free, xt_free, h13_free, yo_free, ht_free = ([route_done, route_done] for _ in range(5))
    t_xt = {}

    def m_gather(q):
        i = q % 2
        t = pool.dma(dsem(f"xg{i}"), lambda e: e.indirect_dma_start(XG[i], None, a["n2_d"], bass.IndirectOffsetOnAxis(ap=LIST[:, q:q + 1], axis=0)),
                     xg_free[i], t_n2ds)
        for half in range(2):
            b = bank()
            for j in range(4):
                k = 4 * half + j
                tok = pe(lambda e, b=b, j=j, k=k: e.transpose(PS[:, b, j * 128:(j + 1) * 128], XG[i][:, k * 128:(k + 1) * 128], ident), t, bank_free[b], inc=(j == 3))
            fn = lambda e, b=b, half=half: e.tensor_copy(XT[i][:, 4 * half:4 * half + 4, :], PS[:, b, :].rearrange("p (a b) -> p a b", a=4))
            t_ = dve(fn, tok, xt_free[i])
            bank_free[b] = [t_]
        xg_free[i] = [tok]
        t_xt[q] = t_
        return t

    hst, tst = {}, {}
    w2s = {}

    def m_h(ex):
        q, s = divmod(ex, 2)
        i = q % 2
        sl1, tw1, w1_ = fetch_w(a["w1"][ex], 0)
        sl3, tw3, w3_ = fetch_w(a["w3"][ex], 0)
        sl2, tw2 = fetch((0, (4, D), a["w2"][ex].rearrange("(k p) n -> p k n", p=128)))
        w2s[ex] = (sl2, tw2, sl2.ap.rearrange("p (k n) -> p k n", k=4))
        b = bank()
        for k in range(8):
            for hh, w, tw in ((0, w1_, tw1), (1, w3_, tw3)):
                tok = pe(lambda e, k=k, hh=hh, w=w, b=b: e.matmul(PS[64 * hh:64 * hh + 64, b, :], XT[i][:, k, 64 * s:64 * s + 64], w[:, k, :], start=(k == 0), stop=(k == 7)),
                         tw, t_xt[q], bank_free[b] if k == 0 and hh == 0 else None, inc=(k == 7 and hh == 1))
        sl1.free, sl3.free = [tok], [tok]
        if s == 1:
            xt_free[i] = [tok]
        p = ex % 2
        t = act(lambda e: e.activation(H13[p], PS[:, b, :], ACT.Copy), tok, h13_free[p])
        bank_free[b] = [t]
        hst[ex] = t

    def m_t(ex):
        p = ex % 2
        b = bank()
        for j in range(4):
            tok = pe(lambda e, j=j: e.transpose(PS[:, b, j * 128:(j + 1) * 128], H13[p][:, j * 128:(j + 1) * 128], ident), hst[ex], bank_free[b], inc=(j == 3))
        h13_free[p] = [tok]
        pv = PS[:, b, :].rearrange("p (a b) -> p a b", a=4)
        t = act(lambda e: e.activation(SL[p], pv[:, :, 0:64], ACT.Silu), tok, ht_free[p])
        t = dve(lambda e: e.tensor_tensor(HT[p], SL[p], pv[:, :, 64:128], ALU.mult), t, tok)
        bank_free[b] = [t]
        tst[ex] = t

    def m_y(ex):
        p = ex % 2
        sl2, tw2, w2_ = w2s[ex]
        b = bank()
        for k in range(4):
            for hh in range(2):
                tok = pe(lambda e, k=k, hh=hh: e.matmul(PS[64 * hh:64 * hh + 64, b, :], HT[p][:, k, :], w2_[:, k, 512 * hh:512 * hh + 512], start=(k == 0), stop=(k == 3)),
                         tw2, tst[ex], bank_free[b] if k == 0 and hh == 0 else None, inc=(k == 3 and hh == 1))
        sl2.free = [tok]
        ht_free[p] = [tok]
        t = dve(lambda e: e.tensor_copy(YO[p], PS[:, b, :]), tok, yo_free[p])
        bank_free[b] = [t]
        for hh in range(2):
            t_ = act.dma(dsem(f"yo{p}"), lambda e, hh=hh: e.dma_start(a["y_d"][BLK * ex:BLK * ex + BLK, 512 * hh:512 * hh + 512], YO[p][64 * hh:64 * hh + 64, :]), t)
        yo_free[p] = [t_]

    nx = 4 if stop == "moe4" else NE
    for n in range(nx + 2):
        if n < nx:
            if n == 0:
                m_gather(0)
            if n % 2 == 0 and n + 2 < nx:
                t = m_gather(n // 2 + 1)
                if n == 0:
                    s.free.append(t)
            m_h(n)
        if 1 <= n <= nx:
            m_t(n - 1)
        if n >= 2:
            m_y(n - 2)
    if stop == "moe4":
        return done(pe, act, dve, pool, sp, counters)

    o_ = {n: sem_of("o_" + n) for n in ("load", "gather", "xt", "xtc", "h", "hc", "ht", "silu", "mul", "y", "yc", "store", "end", "pad")}
    moe_done = [(pe.sem, pe.count), (dve.sem, dve.count), (act.sem, act.count)] + [tuple(dsem(f"yo{p}")) for p in range(2)]
    OW = [A[:, 11264 + WC * i:11264 + WC * (i + 1)] for i in range(3)]
    o1, o3 = (w.rearrange("p (k n) -> p k n", k=8) for w in OW[0:2])
    o2 = OW[2].rearrange("p (k n) -> p k n", k=4)
    LX = CBM[0:BLK, 142:143].bitcast(U32)
    OXG, OXT, OH13, OSL, OHT, OYO = XG[0][0:BLK, :], view(2048, 8, BLK), H13[0], SL[0], HT[0], YO[0]

    def blocks(e, body):
        e.wait_ge(t_ovi[0], t_ovi[1])
        n = e.value_load(OVI[0:1, OVER:OVER + 1], min_val=0, max_val=OVER - 1)
        i = e.alloc_register()
        e.reg_mov(i, 0)
        with e.While(lambda: e.snap(i, min_val=0, max_val=OVER - 1) < n):
            at = e.snap(i, min_val=0, max_val=OVER - 2)
            body(at, at + 1)
            e.reg_add(i, i, 1)
        e.drain().then_inc(o_["end"], 1)

    def await_block(e, sem, value):
        e.wait_ge(sem, value)
        e.sem_inc(o_["pad"], 1)

    def o_sp(e):
        def body(at, done):
            await_block(e, o_["store"], done * 32)
            ex = e.value_load(OVI[0:1, bass.ds(at, 1)], min_val=0, max_val=NE - 1)
            for dst, w, k in ((o1, a["w1"], 8), (o3, a["w3"], 8), (o2, a["w2"], 4)):
                src = w.rearrange("x (k p) n -> x p k n", p=128)[bass.ds(ex, 1)].rearrange("x p k n -> (x p) k n")
                e.dma_start(dst, src).then_inc(o_["load"], 16)
            e.dma_start(LX, a["list_d"][MAIN:ROWS, :].rearrange("(x j) o -> x j o", j=BLK)[bass.ds(at, 1)].rearrange("x j o -> (x j) o")).then_inc(o_["load"], 16)
        for sem, v in moe_done:
            e.wait_ge(sem, v)
        e.sem_inc(o_["store"], 32)
        blocks(e, body)

    def o_pool(e):
        def body(at, done):
            await_block(e, o_["load"], done * 64)
            e.indirect_dma_start(OXG, None, a["n2_d"], bass.IndirectOffsetOnAxis(ap=LX, axis=0)).then_inc(o_["gather"], 16)
        blocks(e, body)

    def o_pe(e):
        def body(at, done):
            await_block(e, o_["gather"], done * 16)
            for k in range(8):
                m = e.transpose(PS[:, 0, k * BLK:(k + 1) * BLK], OXG[:, k * 128:(k + 1) * 128], C("ident", 0, BLK)[:, 0:BLK])
            m.then_inc(o_["xt"], 1)
            await_block(e, o_["xtc"], done)
            await_block(e, o_["load"], done * 64)
            for k in range(8):
                for hh, w in ((0, o1), (1, o3)):
                    m = e.matmul(PS[64 * hh:64 * hh + 64, 1, :], OXT[:, k, :], w[:, k, :], start=(k == 0), stop=(k == 7))
            m.then_inc(o_["h"], 1)
            await_block(e, o_["hc"], done)
            for j in range(4):
                m = e.transpose(PS[:, 2, j * 128:(j + 1) * 128], OH13[:, j * 128:(j + 1) * 128], ident)
            m.then_inc(o_["ht"], 1)
            await_block(e, o_["mul"], done)
            for k in range(4):
                for hh in range(2):
                    m = e.matmul(PS[64 * hh:64 * hh + 64, 3, :], OHT[:, k, :], o2[:, k, 512 * hh:512 * hh + 512], start=(k == 0), stop=(k == 3))
            m.then_inc(o_["y"], 1)
        blocks(e, body)

    def o_act(e):
        def body(at, done):
            await_block(e, o_["h"], done)
            e.activation(OH13, PS[:, 1, :], ACT.Copy).then_inc(o_["hc"], 1)
            await_block(e, o_["ht"], done)
            e.activation(OSL, PS[:, 2, :].rearrange("p (a b) -> p a b", a=4)[:, :, 0:64], ACT.Silu).then_inc(o_["silu"], 1)
            await_block(e, o_["yc"], done)
            rows = a["y_d"][MAIN:ROWS, :].rearrange("(x j) n -> x j n", j=BLK)[bass.ds(at, 1)].rearrange("x j n -> (x j) n")
            for hh in range(2):
                e.dma_start(rows[:, 512 * hh:512 * hh + 512], OYO[64 * hh:64 * hh + 64, :]).then_inc(o_["store"], 16)
        blocks(e, body)

    def o_dve(e):
        def body(at, done):
            await_block(e, o_["xt"], done)
            e.tensor_copy(OXT, PS[:, 0, :].rearrange("p (a b) -> p a b", a=8)).then_inc(o_["xtc"], 1)
            await_block(e, o_["silu"], done)
            e.tensor_tensor(OHT, OSL, PS[:, 2, :].rearrange("p (a b) -> p a b", a=4)[:, :, 64:128], ALU.mult).then_inc(o_["mul"], 1)
            await_block(e, o_["y"], done)
            e.tensor_copy(OYO, PS[:, 3, :]).then_inc(o_["yc"], 1)
        blocks(e, body)

    for q, fn in ((sp, o_sp), (pool, o_pool), (pe, o_pe), (act, o_act), (dve, o_dve)):
        q.raw(fn)
    over_done = [(o_["end"], 5)]
    def last_store(e):
        n = e.value_load(OVI[0:1, OVER:OVER + 1], min_val=0, max_val=OVER - 1)
        e.wait_ge(o_["store"], (n + 1) * 32)
        e.sem_inc(o_["end"], 1)
    sp.raw(last_store)
    over_done = [(o_["end"], 6)]

    G2 = A[:, 0:1024]
    FG = A[:, 1024:2048]
    GC = KEEP[:, 8:16]
    t = dve(lambda e: e.tensor_copy(GC, MOD[:, 40:48]), ada["tok"])
    t = act.dma(dsem("g2"), lambda e: e.dma_start(a["g2_d"].rearrange("o (k p) -> p (o k)", p=128), GC, allow_slow_non_contiguous=True), t)
    t_g2 = act.dma(dsem("g2b"), lambda e: e.dma_start(G2, a["g2_d"].broadcast_to([128, D])), t, over_done)
    t_fg = act.dma(dsem("fg"), lambda e: e.dma_start(FG, a["final_g"].broadcast_to([128, D])), over_done)
    Y = [[A[:, 11264 + 2048 * tt + 1024 * i:11264 + 2048 * tt + 1024 * (i + 1)] for i in range(2)] for tt in range(4)]
    OUT = [A[:, 20480 + 1024 * tt:20480 + 1024 * (tt + 1)] for tt in range(4)]
    SS = KEEP[:, 16:20]
    t_fy = []
    for tt in range(4):
        for i in range(2):
            ty = pool.dma(dsem(f"fy{tt}"), lambda e, tt=tt, i=i: e.indirect_dma_start(Y[tt][i], None, a["y_d"], bass.IndirectOffsetOnAxis(ap=SLOTU[:, 4 * i + tt:4 * i + tt + 1], axis=0)),
                          over_done)
        t_fy.append(ty)
    for tt in range(4):
        ty = t_fy[tt]
        y0, y1, o = Y[tt][0], Y[tt][1], OUT[tt]
        hrow = h2t[:, tt, :]
        t = act(lambda e, y0=y0, tt=tt: e.activation(y0, y0, ACT.Copy, scale=KEEP[:, tt:tt + 1]), ty, t_wk)
        t = dve(lambda e, y0=y0, y1=y1, tt=tt: e.scalar_tensor_tensor(y0, y1, KEEP[:, 4 + tt:5 + tt], y0, ALU.mult, ALU.add), t, ty)
        t = dve(lambda e, y0=y0: e.tensor_tensor(y0, y0, G2, ALU.mult), t, t_g2)
        t = dve(lambda e, y0=y0, hrow=hrow: e.tensor_tensor(y0, y0, hrow, ALU.add), t, t_h2t)
        ts = act(lambda e, y0=y0, y1=y1, tt=tt: e.activation(y1, y0, ACT.Square, accum_out=SS[:, tt:tt + 1]), t)
        ts = act(lambda e, tt=tt: e.activation(SS[:, tt:tt + 1], SS[:, tt:tt + 1], ACT.Sqrt, scale=1.0 / D, bias=C("eps")), ts)
        ts = dve(lambda e, tt=tt: e.reciprocal(SS[:, tt:tt + 1], SS[:, tt:tt + 1]), ts)
        t = dve(lambda e, y0=y0, o=o, tt=tt: e.scalar_tensor_tensor(o, y0, SS[:, tt:tt + 1], FG, ALU.mult, ALU.mult), ts, t, t_fg)
        sp.dma(dsem("out"), lambda e, tt=tt, o=o: e.dma_start(a["out"][tt * 128:(tt + 1) * 128, :], o), t)
    return done(pe, act, dve, pool, sp, counters)


def done(pe, act, dve, pool, sp, counters):
    sp.wait(*[(c[0], c[1]) for c in counters.values()])
    sp.wait((pe.sem, pe.count), (act.sem, act.count), (dve.sem, dve.count), (pool.sem, pool.count))


def shape_constants():
    i = np.arange(128)
    c = np.zeros((128, CN), np.float32)

    def put(name, x):
        at, n = CO[name]
        c[:, at:at + n] = x

    put("ident", np.eye(128))
    put("ones", 1.0)
    put("bones", (i[:, None] // 64 == i[None] // 64))
    put("ustrict", i[:, None] < i[None])
    put("cmask", np.where(i[None] <= i[:, None], 0.0, -1e30))
    put("smask", i[None] >= i[:, None])
    put("iota8", np.arange(8)[None])
    put("iota64", np.arange(64)[None])
    put("tok", i[:, None] + 128 * np.arange(4)[None])
    put("eps", EPS)
    put("sel4", (i[:, None] % 32 == 0))
    put("sel16", (i[:, None] % 32 == np.arange(16)[None]))
    return c


def lay_params(x):
    p = np.zeros((128, PN), np.float32)

    def put(name, v, rows=128):
        at, n = PO[name]
        p[:rows, at:at + n] = v

    col = lambda v: np.asarray(v).reshape(-1, 128).T
    put("attn_norm", col(x["attn_norm"]))
    put("ffn_norm", col(x["ffn_norm"]))
    put("final_norm", col(x["final_norm"]))
    put("qg", np.tile(x["fox_q_norm"][0], 2)[:, None])
    put("kg", np.tile(x["fox_k_norm"][0], 2)[:, None])
    put("bf", x["fox_b_f"][0][:, None], 16)
    put("norm1", col(x["norm1_g_2"]))
    put("cvw", x["cv_dw_w_2"][0].T.reshape(8, 128, 31).transpose(1, 0, 2).reshape(128, 248))
    put("cvb", col(x["cv_dw_b_2"]))
    put("lng", col(x["cv_ln_g_2"]))
    put("lnb", col(x["cv_ln_b_2"]))
    put("scw", x["ssm_conv_w_2"][0].T.reshape(24, 128, 4).transpose(1, 0, 2).reshape(128, 96))
    put("scb", col(x["ssm_conv_b_2"]))
    put("dtb", x["dt_bias_2"][0][:, None], 32)
    put("alog", x["a_log_2"][0][:, None], 32)
    put("dsk", np.repeat(x["d_skip_2"][0].reshape(16, 2).T, 64, axis=0))
    put("sng", col(x["ssm_norm_g_2"]))
    put("norm2", col(x["norm2_g_2"]))
    put("c", col(x["c_2"]))
    put("bada", col(x["b_ada_2"]))
    put("rb", np.broadcast_to(np.concatenate([x["b_grp_2"][0], x["b_er_2"][0]])[None], (128, 72)))
    put("wf", x["fox_w_in"][0][:, 4096:4112].reshape(8, 128, 16).transpose(1, 0, 2).reshape(128, 128))
    put("wdt", x["w_in_2"][0][:, 7168:7200].reshape(8, 128, 32).transpose(1, 0, 2).reshape(128, 256))
    return p


def arrays(x):
    xt = np.concatenate([x["meta_tokens"], x["x"][0]], axis=0)
    return {
        "consts": shape_constants(),
        "params": lay_params(x),
        "xT": np.ascontiguousarray(xt.T.reshape(8, 128, L).transpose(1, 0, 2)),
        "rw": np.ascontiguousarray(np.concatenate([x["w_grp_2"][0], x["w_er_2"][0]], axis=1).reshape(8, 128, 72).transpose(1, 0, 2)),
        "fox_w_in": x["fox_w_in"][0], "fox_w_out": x["fox_w_out"][0], "ffn_w_in": x["ffn_w_in"][0], "ffn_w_out": x["ffn_w_out"][0],
        "w_ada": x["w_ada_2"][0], "w_in": x["w_in_2"][0], "w_cv_out": x["w_cv_out_2"][0], "w_ssm_out": x["w_ssm_out_2"][0],
        "w_mix_out": x["w_mix_out_2"][0], "w1": x["w1_2"][0], "w3": x["w3_2"][0], "w2": x["w2_2"][0],
        "final_g": x["final_g_2"].reshape(1, D),
    }


def declare(nc, arr):
    a = {k: nc.dram_tensor("in_" + k, v.shape, mybir.dt.from_np(v.dtype), kind="ExternalInput").ap() for k, v in arr.items()}
    a["out"] = nc.dram_tensor("out_0", (T, D), F32, kind="ExternalOutput").ap()
    for name, shape, dt in (("x2_d", (128, 8, T), F32), ("ymix_d", (128, 8, T), F32), ("y01_d", (128, 8, T), F32), ("sg_d", (128, 8, T), F32), ("n2_d", (T, D), F32), ("g2_d", (1, D), F32),
                            ("list_d", (ROWS, 1), U32), ("y_d", (ROWS, D), F32)):
        a[name] = nc.dram_tensor(name, shape, dt).ap()
    return a


def kernel(**inputs):
    from concourse import bacc
    from concourse.bass_utils import run_bass_kernel_spmd

    arr = {k: np.ascontiguousarray(v) for k, v in arrays({k: np.asarray(v) for k, v in inputs.items()}).items()}
    nc = bacc.Bacc("TRN2", target_bir_lowering=False, num_devices=1)
    a = declare(nc, arr)
    build_program(nc, a)
    r = run_bass_kernel_spmd(nc, [{"in_" + k: v for k, v in arr.items()}], core_ids=[0])
    return r.results[0]["out_0"].reshape(1, T, D)
```
